# Optimizing a Trainium2 kernel written in Bass

```python
import math
import jax, jax.numpy as jnp
from jax import lax
import numpy as np

D_MODEL = 1024
BATCH = 1
SEQ = 512
DEPTH = 2

N_EVEN = (DEPTH + 1) // 2
N_ODD = DEPTH // 2

RWKV_WIDTH = D_MODEL // 2
RWKV_HEAD_DIM = 64
RWKV_HEADS = RWKV_WIDTH // RWKV_HEAD_DIM
DECAY_LORA = 64
ICLR_LORA = 64
GATE_LORA = 128
GN_EPS = 64e-5
POOL_WINDOWS = (2, 4, 8, 16)
POOL_GROUPS = len(POOL_WINDOWS)
POOL_WIDTH = D_MODEL // 2
POOL_GROUP_DIM = POOL_WIDTH // POOL_GROUPS
SHIFT_WIDTH = 3 * RWKV_WIDTH + DECAY_LORA + ICLR_LORA + GATE_LORA
IN_WIDTH = SHIFT_WIDTH + POOL_WIDTH
SPLITS = (0, RWKV_WIDTH, 2 * RWKV_WIDTH, 3 * RWKV_WIDTH, 3 * RWKV_WIDTH + DECAY_LORA,
          3 * RWKV_WIDTH + DECAY_LORA + ICLR_LORA, SHIFT_WIDTH)
ATT_HEADS = 8
ATT_HEAD_DIM = D_MODEL // (2 * ATT_HEADS)
ATT_V_DIM = 2 * ATT_HEAD_DIM
ROPE_DIMS = ATT_HEAD_DIM // 4
ROPE_THETA = 500000.0
Q_BLOCK = 128
SUBLN_EPS = 1e-5
MOE_GROUPS = 4
MOE_EXPERTS_PER_GROUP = 8
MOE_EXPERTS = MOE_GROUPS * MOE_EXPERTS_PER_GROUP
MOE_TOP_K = 2
MOE_HIDDEN = D_MODEL // 2
MOE_BLOCK = 128
RMS_EPS = 1e-6

kernel_name = "hybrid_rwkv7_pool_diffattn_hmoe"

def _rmsnorm(x, g, eps):
    xf = x.astype(jnp.float32)
    y = xf * lax.rsqrt(jnp.mean(xf * xf, axis=-1, keepdims=True) + eps)
    return (y * g.astype(jnp.float32)).astype(x.dtype)

def _rwkv7_step(S, inp):
    r_t, w_t, k_t, v_t, kk_t, b_t = inp
    sa = jnp.einsum('bhij,bhj->bhi', S, kk_t)
    S = S * w_t[:, :, None, :] - sa[..., None] * b_t[:, :, None, :] + v_t[..., None] * k_t[:, :, None, :]
    return S, jnp.einsum('bhij,bhj->bhi', S, r_t)

def _rwkv_pool_mixer(h, w_in, mu, w0, w2, a0, a2, g2, k_k, k_a, r_k, ln_w, ln_b, w_pool, pool_scale, w_out):
    B, T, _ = h.shape
    f32 = jnp.float32
    H, N = RWKV_HEADS, RWKV_HEAD_DIM
    p = h @ w_in
    ps = p[..., :SHIFT_WIDTH].astype(f32)
    prev = jnp.pad(ps, ((0, 0), (1, 0), (0, 0)))[:, :-1]
    z = ps + (prev - ps) * mu.astype(f32)
    r, k, v, wd, ad, gd = (z[..., SPLITS[j]:SPLITS[j + 1]] for j in range(6))
    w_log = -jax.nn.softplus(-(w0.astype(f32) + jnp.tanh(wd) @ w2.astype(f32))) - 0.5
    decay = jnp.exp(-jnp.exp(w_log))
    a = jax.nn.sigmoid(a0.astype(f32) + ad @ a2.astype(f32))
    g = jax.nn.sigmoid(gd) @ g2.astype(f32)
    heads = lambda t: t.reshape(B, T, H, N)
    r, k, v, a, decay = heads(r), heads(k), heads(v), heads(a), heads(decay)
    kk = k * k_k.astype(f32).reshape(H, N)
    kk = kk / jnp.maximum(jnp.sqrt(jnp.sum(kk * kk, axis=-1, keepdims=True)), 1e-12)
    k = k * (1.0 + (a - 1.0) * k_a.astype(f32).reshape(H, N))
    sf = lambda t: jnp.moveaxis(t, 1, 0)
    S0 = jnp.zeros((B, H, N, N), f32)
    _, y = lax.scan(_rwkv7_step, S0, (sf(r), sf(decay), sf(k), sf(v), sf(kk), sf(kk * a)))
    y = jnp.moveaxis(y, 0, 1)
    mean = jnp.mean(y, axis=-1, keepdims=True)
    var = jnp.mean(jnp.square(y - mean), axis=-1, keepdims=True)
    y = (y - mean) * lax.rsqrt(var + GN_EPS)
    y = y * ln_w.astype(f32).reshape(H, N) + ln_b.astype(f32).reshape(H, N)
    y = y + jnp.sum(r * k * r_k.astype(f32), axis=-1, keepdims=True) * v
    y_a = y.reshape(B, T, RWKV_WIDTH) * g
    u = p[..., SHIFT_WIDTH:].astype(f32).reshape(B, T, POOL_GROUPS, POOL_GROUP_DIM)
    c = jnp.pad(jnp.cumsum(u, axis=1), ((0, 0), (1, 0), (0, 0), (0, 0)))
    t_idx = jnp.arange(T)
    means = []
    for gi, win in enumerate(POOL_WINDOWS):
        lo = jnp.maximum(t_idx + 1 - win, 0)
        cnt = (t_idx + 1 - lo).astype(f32)
        cg = c[:, :, gi]
        means.append((cg[:, 1:] - cg[:, lo]) / cnt[None, :, None])
    pooled = jnp.stack(means, axis=2)
    y_b = jnp.einsum('btgc,gcd->btgd', pooled - u, w_pool.astype(f32)).reshape(B, T, POOL_WIDTH)
    y_b = y_b * pool_scale.astype(f32)
    return jnp.concatenate([y_a, y_b], axis=-1).astype(h.dtype) @ w_out

def _partial_rope(x, cos, sin):
    half = ROPE_DIMS // 2
    x1 = x[..., :half]
    x2 = x[..., half:ROPE_DIMS]
    c = cos[:, None, None, :]
    s = sin[:, None, None, :]
    return jnp.concatenate([x1 * c - x2 * s, x2 * c + x1 * s, x[..., ROPE_DIMS:]], axis=-1)

def _diff_attention(h, w_qkv, lq1, lk1, lq2, lk2, subln_w, w_out, lambda_init, cos, sin):
    B, T, _ = h.shape
    f32 = jnp.float32
    H, dh, dv = ATT_HEADS, ATT_HEAD_DIM, ATT_V_DIM
    qkv = (h @ w_qkv).astype(f32)
    q = qkv[..., :2 * H * dh].reshape(B, T, H, 2, dh)
    k = qkv[..., 2 * H * dh:4 * H * dh].reshape(B, T, H, 2, dh)
    v = qkv[..., 4 * H * dh:].reshape(B, T, H, dv)
    q = _partial_rope(q, cos, sin)
    k = _partial_rope(k, cos, sin)
    lam = (jnp.exp(jnp.sum(lq1.astype(f32) * lk1.astype(f32)))
           - jnp.exp(jnp.sum(lq2.astype(f32) * lk2.astype(f32))) + lambda_init)
    nb = T // Q_BLOCK
    qb = q.reshape(B, nb, Q_BLOCK, H, 2, dh).transpose(1, 0, 3, 4, 2, 5)
    kt = k.transpose(0, 2, 3, 1, 4)
    vt = v.transpose(0, 2, 1, 3)
    key_pos = jnp.arange(T)
    scale = ATT_HEAD_DIM ** -0.5

    def attend(args):
        q_blk, bi = args
        s = jnp.einsum('bhcqd,bhckd->bhcqk', q_blk, kt) * scale
        q_pos = bi * Q_BLOCK + jnp.arange(Q_BLOCK)
        s = jnp.where(key_pos[None, :] <= q_pos[:, None], s, -jnp.inf)
        pr = jax.nn.softmax(s, axis=-1)
        return jnp.einsum('bhqk,bhkd->bhqd', pr[:, :, 0] - lam * pr[:, :, 1], vt)

    o = lax.map(attend, (qb, jnp.arange(nb)))
    o = o.transpose(1, 0, 3, 2, 4).reshape(B, T, H, dv)
    o = o * lax.rsqrt(jnp.mean(o * o, axis=-1, keepdims=True) + SUBLN_EPS)
    o = o * subln_w.astype(f32) * (1.0 - lambda_init)
    return o.reshape(B, T, H * dv).astype(h.dtype) @ w_out

def _expert_dispatch(x, eid, wts, w_gate, w_up, w_down):
    n_tok, D = x.shape
    M = n_tok * MOE_TOP_K
    eid = eid.reshape(M)
    wts = wts.reshape(M)
    tok = jnp.repeat(jnp.arange(n_tok), MOE_TOP_K)
    order = jnp.argsort(eid)
    eid_s, tok_s, wt_s = eid[order], tok[order], wts[order]
    counts = jnp.bincount(eid, length=MOE_EXPERTS)
    padded = (counts + MOE_BLOCK - 1) // MOE_BLOCK * MOE_BLOCK
    pad_end = jnp.cumsum(padded)
    pad_start = pad_end - padded
    start = jnp.cumsum(counts) - counts
    dest = pad_start[eid_s] + jnp.arange(M) - start[eid_s]
    n_blocks = (M + MOE_EXPERTS * (MOE_BLOCK - 1) + MOE_BLOCK - 1) // MOE_BLOCK
    P = n_blocks * MOE_BLOCK
    xp = jnp.zeros((P, D), x.dtype).at[dest].set(x[tok_s])
    blk_e = jnp.minimum(jnp.searchsorted(pad_end, jnp.arange(n_blocks) * MOE_BLOCK, side='right'),
                        MOE_EXPERTS - 1)

    def expert_block(args):
        xb, e = args
        return (jax.nn.silu(xb @ w_gate[e]) * (xb @ w_up[e])) @ w_down[e]

    yp = lax.map(expert_block, (xp.reshape(n_blocks, MOE_BLOCK, D), blk_e)).reshape(P, D)
    y = yp[dest] * wt_s[:, None].astype(x.dtype)
    return jnp.zeros((n_tok, D), x.dtype).at[tok_s].add(y)

def _hier_moe(h, w_group, b_group, w_expert, b_expert, w_gate, w_up, w_down):
    B, T, D = h.shape
    f32 = jnp.float32
    x = h.reshape(B * T, D)
    xf = x.astype(f32)
    p_grp = jax.nn.softmax(xf @ w_group.astype(f32) + b_group.astype(f32), axis=-1)
    g_idx = jnp.argmax(p_grp, axis=-1)
    g_w = jnp.take_along_axis(p_grp, g_idx[:, None], axis=-1)
    e_logits = (xf @ w_expert.astype(f32) + b_expert.astype(f32)).reshape(-1, MOE_GROUPS, MOE_EXPERTS_PER_GROUP)
    e_in = jnp.take_along_axis(e_logits, g_idx[:, None, None], axis=1)[:, 0]
    top_v, top_i = lax.top_k(e_in, MOE_TOP_K)
    wts = jax.nn.softmax(top_v, axis=-1) * g_w
    eid = (g_idx[:, None] * MOE_EXPERTS_PER_GROUP + top_i).astype(jnp.int32)
    return _expert_dispatch(x, eid, wts, w_gate, w_up, w_down).reshape(B, T, D)

def setup_inputs(seed: int = 0) -> dict:
    key = jax.random.key(seed)
    ks = iter(jax.random.split(key, 48))
    f32 = jnp.float32
    nrm = lambda shape, scale: jax.random.normal(next(ks), shape, f32) * scale
    uni = lambda shape, lo, hi: jax.random.uniform(next(ks), shape, f32, lo, hi)
    D = D_MODEL
    return {
        'x': nrm((BATCH, SEQ, D), 1.0),
        'norm_mix': 1.0 + nrm((DEPTH, D), 0.05),
        'norm_ffn': 1.0 + nrm((DEPTH, D), 0.05),
        'final_norm': 1.0 + nrm((D,), 0.05),
        'a_w_in': nrm((N_EVEN, D, IN_WIDTH), D ** -0.5),
        'a_mu': uni((N_EVEN, SHIFT_WIDTH), 0.0, 1.0),
        'a_w0': uni((N_EVEN, RWKV_WIDTH), -6.0, 1.0),
        'a_w2': nrm((N_EVEN, DECAY_LORA, RWKV_WIDTH), 0.5 * DECAY_LORA ** -0.5),
        'a_a0': nrm((N_EVEN, RWKV_WIDTH), 0.1),
        'a_a2': nrm((N_EVEN, ICLR_LORA, RWKV_WIDTH), ICLR_LORA ** -0.5),
        'a_g2': nrm((N_EVEN, GATE_LORA, RWKV_WIDTH), GATE_LORA ** -0.5),
        'a_k_k': 0.85 + nrm((N_EVEN, RWKV_WIDTH), 0.05),
        'a_k_a': 1.0 + nrm((N_EVEN, RWKV_WIDTH), 0.05),
        'a_r_k': nrm((N_EVEN, RWKV_HEADS, RWKV_HEAD_DIM), 0.1),
        'a_ln_w': 1.0 + nrm((N_EVEN, RWKV_WIDTH), 0.05),
        'a_ln_b': nrm((N_EVEN, RWKV_WIDTH), 0.01),
        'b_w_pool': nrm((N_EVEN, POOL_GROUPS, POOL_GROUP_DIM, POOL_GROUP_DIM), POOL_GROUP_DIM ** -0.5),
        'b_pool_scale': 1.0 + nrm((N_EVEN, POOL_WIDTH), 0.05),
        'ab_w_out': nrm((N_EVEN, RWKV_WIDTH + POOL_WIDTH, D), (RWKV_WIDTH + POOL_WIDTH) ** -0.5),
        'c_w_qkv': nrm((N_ODD, D, 4 * ATT_HEADS * ATT_HEAD_DIM + ATT_HEADS * ATT_V_DIM), D ** -0.5),
        'c_lambda_q1': nrm((N_ODD, ATT_HEAD_DIM), 0.1),
        'c_lambda_k1': nrm((N_ODD, ATT_HEAD_DIM), 0.1),
        'c_lambda_q2': nrm((N_ODD, ATT_HEAD_DIM), 0.1),
        'c_lambda_k2': nrm((N_ODD, ATT_HEAD_DIM), 0.1),
        'c_subln': 1.0 + nrm((N_ODD, ATT_V_DIM), 0.05),
        'c_w_out': nrm((N_ODD, ATT_HEADS * ATT_V_DIM, D), (ATT_HEADS * ATT_V_DIM) ** -0.5),
        'moe_w_group': nrm((DEPTH, D, MOE_GROUPS), D ** -0.5),
        'moe_b_group': nrm((DEPTH, MOE_GROUPS), 0.01),
        'moe_w_expert': nrm((DEPTH, D, MOE_EXPERTS), D ** -0.5),
        'moe_b_expert': nrm((DEPTH, MOE_EXPERTS), 0.01),
        'moe_w_gate': nrm((DEPTH, MOE_EXPERTS, D, MOE_HIDDEN), D ** -0.5),
        'moe_w_up': nrm((DEPTH, MOE_EXPERTS, D, MOE_HIDDEN), D ** -0.5),
        'moe_w_down': nrm((DEPTH, MOE_EXPERTS, MOE_HIDDEN, D), MOE_HIDDEN ** -0.5),
    }

def reference(x, norm_mix, norm_ffn, final_norm, a_w_in, a_mu, a_w0, a_w2, a_a0, a_a2, a_g2,
              a_k_k, a_k_a, a_r_k, a_ln_w, a_ln_b, b_w_pool, b_pool_scale, ab_w_out,
              c_w_qkv, c_lambda_q1, c_lambda_k1, c_lambda_q2, c_lambda_k2, c_subln, c_w_out,
              moe_w_group, moe_b_group, moe_w_expert, moe_b_expert, moe_w_gate, moe_w_up, moe_w_down):
    T = x.shape[1]
    pos = jnp.arange(T, dtype=jnp.float32)
    inv_freq = jnp.power(ROPE_THETA, -jnp.arange(0, ROPE_DIMS, 2, dtype=jnp.float32) / ROPE_DIMS)
    ang = pos[:, None] * inv_freq[None, :]
    cos, sin = jnp.cos(ang), jnp.sin(ang)
    for layer in range(DEPTH):
        i = layer // 2
        hn = _rmsnorm(x, norm_mix[layer], RMS_EPS)
        if layer % 2 == 0:
            x = x + _rwkv_pool_mixer(hn, a_w_in[i], a_mu[i], a_w0[i], a_w2[i], a_a0[i], a_a2[i], a_g2[i],
                                     a_k_k[i], a_k_a[i], a_r_k[i], a_ln_w[i], a_ln_b[i],
                                     b_w_pool[i], b_pool_scale[i], ab_w_out[i])
        else:
            lambda_init = 0.8 - 0.6 * math.exp(-0.3 * layer)
            x = x + _diff_attention(hn, c_w_qkv[i], c_lambda_q1[i], c_lambda_k1[i], c_lambda_q2[i],
                                    c_lambda_k2[i], c_subln[i], c_w_out[i], lambda_init, cos, sin)
        hn = _rmsnorm(x, norm_ffn[layer], RMS_EPS)
        x = x + _hier_moe(hn, moe_w_group[layer], moe_b_group[layer], moe_w_expert[layer],
                          moe_b_expert[layer], moe_w_gate[layer], moe_w_up[layer], moe_w_down[layer])
    return _rmsnorm(x, final_norm, RMS_EPS)


_drawn_inputs = setup_inputs


def setup_inputs(seed=0):
    import zlib

    import numpy as np

    out = dict(_drawn_inputs(seed))
    spreads = {}
    factors = {}
    for name, (base, spread) in spreads.items():
        noise = np.random.default_rng([zlib.crc32(name.encode()), seed]).standard_normal(out[name].shape)
        drawn = base * np.exp(spread * noise) if base else spread * noise
        out[name] = __import__('jax').numpy.asarray(drawn.astype(out[name].dtype))
    for name, factor in factors.items():
        out[name] = (out[name] * factor).astype(out[name].dtype)
    return out
```

```python
from contextlib import ExitStack
import math

import numpy as np

import concourse.bass as bass
from concourse import mybir

F32 = mybir.dt.float32
BF16 = mybir.dt.bfloat16
I32 = mybir.dt.int32
ALU = mybir.AluOpType
ACT = mybir.ActivationFunctionType
AX = mybir.AxisListType.X

P = 128
T = 512
D = 1024
NT = T // P
NC = D // P
H = 8
N = 64
C = 64
NCH = T // C
NPAIR = H // 2
GN_EPS = 64e-5
RMS_EPS = 1e-6
SUBLN_EPS = 1e-5
WINDOWS = (2, 4, 8, 16)
EXPERTS = 32
GROUPS = 4
PER_GROUP = 8
FF = 512
TB = 80
EXTRA = (2 * T - 1) // TB
MAIN_SLOTS = EXPERTS * TB
SLOTS = MAIN_SLOTS + EXTRA * TB
LAMBDA_INIT = 0.8 - 0.6 * math.exp(-0.3)
ROPE_DIMS = 16
ROPE_THETA = 500000.0
SCALE = 64 ** -0.5
BIG = 1e30
ROUTER_E2 = 732
UNIT = 4096
SLAB = 2048


def constant_table():
    p = np.arange(P)
    f = np.arange(P)
    blocks = {}
    blocks["ident"] = np.eye(P)
    blocks["earlier"] = (p[:, None] < f[None, :])
    blocks["ones"] = np.ones((P, P))
    blocks["head_mean"] = (p[:, None] // N == f[None, :] // N) / N
    sel = np.zeros((P, NPAIR, H))
    for j in range(NPAIR):
        sel[p, j, 2 * j + p // N] = 1
    blocks["head_sel"] = sel.reshape(P, -1)
    spread = np.zeros((P, NPAIR, P))
    for j in range(NPAIR):
        spread[2 * j + p // N, j, p] = 1
    blocks["head_spread"] = spread.reshape(P, -1)
    r, c = (p % C)[:, None], np.arange(C)[None, :]
    blocks["eye64"] = (r == c)
    blocks["low1"] = -((r // 2 == c // 2) & (r > c)).astype(float)
    blocks["up1"] = -((r // 2 == c // 2) & (r < c)).astype(float)
    for m in (2, 4, 8, 16, 32):
        blocks[f"join{m}"] = (r // (2 * m) == c // (2 * m)) & (r % (2 * m) < m) & (c % (2 * m) >= m)
    blocks["strict"] = (r < c)
    blocks["upto"] = (r <= c)
    win = np.ones((P, 4, 16))
    for g, w in enumerate(WINDOWS):
        t = np.arange(16)
        win[:, g] = w / np.minimum(t + 1, w)
    blocks["short_window"] = win.reshape(P, -1)
    blocks["iota4"] = np.tile(np.arange(4), (P, 1))
    blocks["iota32"] = np.tile(np.arange(32), (P, 1))
    blocks["iota_extra"] = np.tile(np.arange(EXTRA), (P, 1))
    blocks["first_slot"] = np.tile(TB * np.arange(EXPERTS), (P, 1))
    blocks["minus_half"] = np.full((P, 4), -0.5)
    at, n = {}, 0
    for k, v in blocks.items():
        at[k] = (n, n + v.shape[1])
        n += v.shape[1]
    return at, np.concatenate([np.asarray(v, np.float32) for v in blocks.values()], axis=1)


def rope_table():
    inv = ROPE_THETA ** (-np.arange(0, ROPE_DIMS, 2, dtype=np.float32) / ROPE_DIMS)
    ang = np.arange(T, dtype=np.float32)[:, None] * inv.astype(np.float32)[None, :]
    cos, sin = np.ones((P, T)), np.zeros((P, T))
    swap = np.zeros((P, P))
    half = ROPE_DIMS // 2
    for base in (0, 64):
        for i in range(half):
            a, b = base + i, base + half + i
            cos[a] = cos[b] = np.cos(ang[:, i])
            sin[a] = sin[b] = np.sin(ang[:, i])
            swap[b, a] = -1
            swap[a, b] = 1
    q, k = np.arange(P)[:, None], np.arange(P)[None, :]
    mask = np.where(k <= q, 0.0, -BIG)
    return np.concatenate([cos, sin, swap, mask], axis=1).astype(np.float32)


class Steps:

    def __init__(self, eng, sem):
        self.eng, self.sem, self.n = eng, sem, 0

    def mark(self, ins):
        self.n += 1
        ins.then_inc(self.sem, 1)

    def hold(self):
        self.eng.wait_ge(self.sem, self.n)

    def next(self, ins):
        self.mark(ins)
        self.hold()


def build(nc, a, consts, ropes, out, stop=99, dbg=None):
    at, _ = constant_table()
    xp = nc.dram_tensor("expert_rows", [SLOTS, D], F32, kind="Internal").ap()
    yp = nc.dram_tensor("expert_out", [SLOTS, D], F32, kind="Internal").ap()
    ctx = ExitStack()
    with ctx:
        def sb(name, shape, dt=F32):
            return ctx.enter_context(nc.sbuf_tensor(name, shape, dt))

        def sem(name):
            return ctx.enter_context(nc.semaphore(name))

        x_sb = sb("x_sb", [P, NT, D])
        ring = sb("ring", [P, 3, UNIT])
        S1 = sb("shared_scratch", [P, 3 * UNIT])
        S2 = sb("scratch", [P, 9 * SLAB])
        cst = sb("cst", [P, consts.shape[1]])
        lora_w = sb("lora_w", [P, 512])
        gate_w2 = sb("gate_w2", [P, 512])
        wpool = sb("wpool", [P, 4, P])
        vec = sb("vec", [P, 160])
        rowv = sb("rowv", [1, 2 * 36])
        small = sb("small", [P, 64])
        gateT_in = sb("gateT_in", [P, T])

        bank_pair = [ctx.enter_context(nc.psum_tensor(f"bank_pair{i}", [P, 2, 512], F32)) for i in range(4)]
        bank67 = bank_pair[3]

        def bank(i):
            return bank_pair[i // 2][:, i % 2, :]

        def K(name, rows=P):
            return cst[0:rows, at[name][0]:at[name][1]]

        ident = K("ident")

        def slab(n, cols=SLAB):
            if n < 9:
                return S2[:, n * SLAB:n * SLAB + cols]
            if n < 16:
                return S1[:, (n - 10) * SLAB:(n - 10) * SLAB + cols]
            return ring[:, 2, (n - 16) * SLAB:(n - 16) * SLAB + cols]

        def slot(s):
            return ring[:, s, :] if s < 3 else S1[:, (s - 3) * UNIT:(s - 2) * UNIT]

        hnT = S2[:, 0:UNIT].rearrange("p (c t) -> p c t", c=NC)
        hn = S2[:, UNIT:2 * UNIT].rearrange("p (i d) -> p i d", i=NT)

        cols = {}
        used = [0]

        def column(name, n):
            cols[name] = vec[:, used[0]:used[0] + n]
            used[0] += n

        for nm, n in (("g_mix0", 8), ("g_ffn0", 8), ("g_mix1", 8), ("g_ffn1", 8), ("mu", 14), ("w0", 4), ("a0", 4),
                      ("k_k", 4), ("k_a", 4), ("r_k", 4), ("ln_w", 4), ("ln_b", 4), ("pool_scale", 4), ("subln", 1),
                      ("lq", 4), ("one_minus_mu", 14), ("half_w0", 4), ("half_a0", 4), ("lam", 6), ("subln_s", 1),
                      ("ss", 4), ("ms", 4), ("rstd", 4), ("half_decay", 1), ("sub_eps", 1)):
            column(nm, n)
        vec_loads = [
            (cols["g_mix0"], a["norm_mix"][0].rearrange("(p c) -> p c", c=8)),
            (cols["g_mix1"], a["norm_mix"][1].rearrange("(p c) -> p c", c=8)),
            (cols["g_ffn0"], a["norm_ffn"][0].rearrange("(p c) -> p c", c=8)),
            (cols["g_ffn1"], a["norm_ffn"][1].rearrange("(p c) -> p c", c=8)),
            (cols["mu"], a["a_mu"][0].rearrange("(c p) -> p c", p=P)),
            (cols["w0"], a["a_w0"][0].rearrange("(c p) -> p c", p=P)),
            (cols["a0"], a["a_a0"][0].rearrange("(c p) -> p c", p=P)),
            (cols["k_k"], a["a_k_k"][0].rearrange("(c p) -> p c", p=P)),
            (cols["k_a"], a["a_k_a"][0].rearrange("(c p) -> p c", p=P)),
            (cols["r_k"], a["a_r_k"][0].rearrange("(c h) n -> (h n) c", h=2)),
            (cols["ln_w"], a["a_ln_w"][0].rearrange("(c p) -> p c", p=P)),
            (cols["ln_b"], a["a_ln_b"][0].rearrange("(c p) -> p c", p=P)),
            (cols["pool_scale"], a["b_pool_scale"][0].rearrange("(c p) -> p c", p=P)),
            (cols["subln"], a["c_subln"].rearrange("o p -> p o")),
            (cols["lq"][0:64, 0:1], a["c_lambda_q1"].rearrange("o p -> p o")),
            (cols["lq"][0:64, 1:2], a["c_lambda_k1"].rearrange("o p -> p o")),
            (cols["lq"][0:64, 2:3], a["c_lambda_q2"].rearrange("o p -> p o")),
            (cols["lq"][0:64, 3:4], a["c_lambda_k2"].rearrange("o p -> p o")),
            (lora_w[0:64, :], a["a_w2"][0]),
            (lora_w[64:128, :], a["a_a2"][0]),
            (gate_w2[:, :], a["a_g2"][0]),
            (rowv[0:1, 0:4], a["moe_b_group"][0:1]),
            (rowv[0:1, 4:36], a["moe_b_expert"][0:1]),
            (rowv[0:1, 36:40], a["moe_b_group"][1:2]),
            (rowv[0:1, 40:72], a["moe_b_expert"][1:2]),
            (wpool[:, :, :], a["b_w_pool"][0].rearrange("g c d -> c g d")),
        ]

        s_x = sem("x_loaded")
        s_cst = sem("constants_loaded")
        s_vec = sem("vectors_loaded")
        s_zero = sem("zeros_made")
        s_zrows = sem("rows_zeroed")
        s_full = [sem(f"slot_full{i}") for i in range(6)]
        s_dve = sem("vector_order")
        s_act = sem("scalar_order")
        s_pool = sem("pool_order")
        s_ss = sem("square_sums")
        s_rstd = sem("rstd_made")
        s_hn = sem("rows_normed")
        s_tr = sem("norm_transposed")
        s_trv = sem("norm_evac_vector")
        s_tra = sem("norm_evac_scalar")
        s_proj = sem("proj_done")
        s_sh = sem("shift_part_made")
        s_z = sem("shifted_made")
        s_tanh = sem("lora_inner_made")
        s_lora = sem("lora_mm")
        s_wdec = sem("decay_made")
        s_am = sem("iclr_tanh_made")
        s_sq = sem("k_squares_made")
        s_hsum = sem("head_sums")
        s_hroot = sem("head_roots")
        s_hinv = sem("head_inverse")
        s_hb = sem("head_spread_mm")
        s_kk = sem("kk_made")
        s_rkp = sem("rk_products")
        s_rs = sem("bonus_sum_copied")
        s_bon = sem("bonus_made")
        s_prep = sem("prep_made")
        s_prepp = sem("prep_pool_made")
        s_u = sem("pool_input_copied")
        s_win = sem("window_sums")
        s_pd = sem("pool_diff")
        s_pmm = sem("pool_mm")
        s_yb = sem("pool_out")
        s_pw = sem("pool_weights_loaded")
        s_tt = sem("token_transposed")
        s_tev = sem("token_evac_vector")
        s_tea = sem("token_evac_scalar")
        s_gm = sem("gram_mm")
        s_gv = sem("gram_masked")
        s_jb = sem("join_blocks")
        s_jx = sem("join_x_mm")
        s_jxa = sem("join_x_copied")
        s_jt = sem("join_t_mm")
        s_jtv = sem("join_t_updated")
        s_lx = sem("ak_v_mm")
        s_lxa = sem("ak_v_copied")
        s_lw = sem("w_mm")
        s_lwa = sem("w_copied")
        s_lu = sem("uv_mm")
        s_luv = sem("uv_copied")
        s_um = sem("u_mm")
        s_ua = sem("u_made")
        s_y0m = sem("y_state_part_mm")
        s_sm = sem("state_mm")
        s_sv = sem("state_made")
        s_ym = sem("y_mm")
        s_ya = sem("y_copied")
        s_gn = sem("gn_mm")
        s_gnv = sem("gn_vector")
        s_gna = sem("gn_scalar")
        s_g = sem("gate_made")
        s_gmm = sem("gate_out_mm")
        s_yav = sem("ya_made")
        s_om = sem("out_mm")
        s_res = sem("residual_added")
        s_rw = sem("router_weights")
        s_lg = sem("logits_mm")
        s_rt = sem("router_vector")
        s_re = sem("router_exp")
        s_oh = sem("choices_made")
        s_rk = sem("ranks_mm")
        s_slot = sem("slots_made")
        s_disp = sem("rows_dispatched")
        s_rows = [sem(f"rows_loaded{i}") for i in range(2)]
        s_xt = sem("block_transposed")
        s_xtv = sem("block_evac")
        s_gate = sem("gate_mm")
        s_th = sem("gate_tanh")
        s_h1 = sem("gate_used")
        s_up = sem("up_mm")
        s_h = sem("hidden_made")
        s_ht = sem("hidden_transposed")
        s_hta = sem("hidden_evac")
        s_down = sem("down_mm")
        s_y0 = sem("expert_out_scalar")
        s_y1 = sem("expert_out_vector")
        s_yw = [sem(f"expert_out_written{i}") for i in range(2)]
        s_ov = [{k: sem(f"extra{l}_{k}") for k in ("w", "rows", "pe", "dve", "act", "written")} for l in range(2)]
        EXTRA_MARKS = {"xt": ("pe", 4, 1), "up": ("pe", 4, 2), "ht": ("pe", 4, 3), "down": ("pe", 4, 4),
                       "xtv": ("dve", 4, 1), "h1": ("dve", 4, 2), "h": ("dve", 4, 3), "y1": ("dve", 4, 4),
                       "th": ("act", 3, 1), "hta": ("act", 3, 2), "y0": ("act", 3, 3)}

        def wait_extra(eng, l, what, b):
            name, per, at_ = EXTRA_MARKS[what]
            eng.wait_ge(s_ov[l][name], b * per + at_)

        s_got = [sem(f"expert_out_gathered{i}") for i in range(NT)]
        s_comb = sem("combined")
        s_rope = sem("rope_loaded")
        s_lam = sem("lambda_steps")
        s_lamm_in = sem("lambda_products")
        s_lamm = sem("lambda_mm")
        s_qm = sem("qk_mm")
        s_qa = sem("qk_copied")
        s_rm = sem("rot_mm")
        s_qv = sem("qk_roped")
        s_vm = sem("v_mm")
        s_va = sem("v_copied")
        s_mk = sem("mask_cast")
        s_sc = sem("scores_mm")
        s_mx = sem("scores_max")
        s_ex = sem("scores_exp")
        s_pr = sem("probs_made")
        s_pt = sem("probs_transposed")
        s_pta = sem("probs_evac")
        s_ov_ = sem("values_mm")
        s_oc = sem("values_copied")
        s_osq = sem("o_squares")
        s_osm = sem("o_mean_mm")
        s_ort = sem("o_root")
        s_on = sem("o_normed")
        s_fnb = sem("final_weight_mm")
        s_fin = sem("final_rows")
        s_out = sem("stored")

        n_vec = 16 * len(vec_loads)
        n_zero = SLOTS // TB // 2 + EXTRA // 2

        A_SLOTS = [0, 1, 0, 1, 0, 1, 0]
        C_SLOTS = [0, 1, 2, 0, 1, 2, 0, 1]
        before = {"A": [0] * 6}
        before["moe0"] = [A_SLOTS.count(s) for s in range(6)]
        before["C"] = [n + EXPERTS // 2 for n in before["moe0"]]
        before["moe1"] = [n + C_SLOTS.count(s) for s, n in enumerate(before["C"])]

        def use(phase, slots, u):
            return before[phase][slots[u]] + slots[:u + 1].count(slots[u])

        wA = a["a_w_in"][0].rearrange("(p c) n -> p c n", c=NC)
        A_COLS = [(1536, 1792), (512, 1024), (0, 512), (1024, 1536), (1792, 2304)]
        A_SRC = [wA[:, :, lo:hi] for lo, hi in A_COLS]
        woA = a["ab_w_out"][0].rearrange("(c p) n -> p c n", p=P)
        A_SRC += [woA[:, :, 0:512], woA[:, :, 512:1024]]
        wC = a["c_w_qkv"][0].rearrange("(p c) n -> p c n", c=NC)
        woC = a["c_w_out"][0].rearrange("(c p) n -> p c n", p=P)
        C_SRC = [wC[:, :, 512 * u:512 * u + 512] for u in range(6)] + [woC[:, :, 0:512], woC[:, :, 512:1024]]

        def slot_w(s, c=NC):
            return slot(s).rearrange("p (c n) -> p c n", c=c)

        def pairs(n):
            return slab(n).rearrange("p (j t) -> p j t", j=NPAIR)

        kT, rT, vT, ybT = pairs(4), pairs(5), pairs(6), pairs(7)
        wT, pT, aT, kkT, alT = pairs(16), pairs(17), pairs(10), pairs(11), pairs(12)
        bonT, piT = pairs(13), pairs(14)
        rk_tmp = pairs(8)
        zeros = slab(13)
        v_tok, al_tok, k_tok, b_tok = pairs(0), pairs(1), pairs(14), pairs(11)
        shift = [slab(2)[:, 520 * i:520 * i + T + 1] for i in range(2)]
        z_l0 = slab(2)[:, 1040:1040 + T]
        PAD = 16
        upad = [slab(3)[:, 528 * i:528 * i + PAD + T] for i in range(3)]
        sq_tmp = [slab(15)[:, T * i:T * i + T] for i in range(2)]
        scan_in = slab(15)[:, 1024:1024 + T]
        hs = slab(15)[0:H, 1536:1536 + T]
        wk = [{}, {}]
        for q in range(2):
            for n, name in enumerate(("Tm", "TT", "X", "LT", "Bm", "AK")):
                k = q * 6 + n
                wk[q][name] = slab((2, 3, 15)[k // 4])[:, (k % 4) * 512:(k % 4) * 512 + 512]
        keep = [{name: slab(n)[:, k * 512:k * 512 + 512] for k, name in enumerate(("RK", "RB", "UV", "WT"))}
                for n in (8, 16, 17, 8)]
        yT = vT
        yc_sq = slab(16)
        ST = [sb(f"state{i}", [P, NPAIR, N]) for i in range(2)]
        STs = sb("state_sum", [P, NPAIR, N])
        pc = sb("chunk_decay", [P, NPAIR, NCH])
        u_neg = sb("u_neg", [P, 512])

        def heads(ap):
            if len(ap.shape) == 3:
                return ap.rearrange("p a (j n) -> p a j n", j=NPAIR)
            return ap.rearrange("p (a j n) -> p a j n", a=2, j=NPAIR)

        def per_head(ap):
            return ap.unsqueeze(1).unsqueeze(1).to_broadcast([P, 2, NPAIR, C])

        def gram_place(q, k):
            n = 3 * (q % 2) + k // 2
            return bank_pair[3 - n % 4], 256 * (k % 2)

        def both(ap):
            return ap.rearrange("p (a m) -> p a m", a=2)

        o = 2 * UNIT
        rows = [S2[0:TB, o + D * i:o + D * i + D] for i in range(2)]
        o += 2 * D
        xT = [S2[:, o + NC * TB * i:o + NC * TB * (i + 1)].rearrange("p (c t) -> p c t", c=NC) for i in range(2)]
        o += 2 * NC * TB
        th = [S2[0:TB, o + FF * i:o + FF * i + FF] for i in range(2)]
        o += 2 * FF
        h1 = S2[0:TB, o:o + FF]
        o += FF
        hid = [S2[0:TB, o + FF * i:o + FF * i + FF] for i in range(2)]
        o += 2 * FF
        hidT = [S2[:, o + 4 * TB * i:o + 4 * TB * (i + 1)].rearrange("p (c t) -> p c t", c=4) for i in range(2)]
        o += 8 * TB
        yrow = [S2[0:TB, o + D * i:o + D * i + D] for i in range(2)]
        rt0 = o
        o += 2 * D
        w_router = S2[:, o:o + NC * 36].rearrange("p (c n) -> p c n", c=NC)
        o += NC * 36
        assert o + 1280 <= 9 * SLAB
        got = [[S2[:, k * UNIT + D * i:k * UNIT + D * i + D] for i in range(NT)] for k in range(2)]
        th_at = 2 * UNIT + 2 * D + 2 * NC * TB
        e2_at = rt0 + ROUTER_E2
        slot_ix = sb("slot_ix", [P, 2, NT], I32)
        extra_tab = sb("extra_tab", [1, 1 + EXTRA], I32)
        wts = sb("wts", [P, 2, NT])

        rope_sb = S2[:, 9 * SLAB - 1280:9 * SLAB]
        cosT, sinT = rope_sb[:, 0:T], rope_sb[:, T:2 * T]
        swap, mask = rope_sb[:, 2 * T:2 * T + P], rope_sb[:, 2 * T + P:2 * T + 2 * P]
        v_att = hn
        qT = S2[:, 2 * UNIT:3 * UNIT].rearrange("p (h t) -> p h t", h=H)
        kaT = S2[:, 3 * UNIT:4 * UNIT].rearrange("p (h t) -> p h t", h=H)
        oT = S1[:, 0:UNIT].rearrange("p (h t) -> p h t", h=H)
        raw = [S1[:, UNIT + T * i:UNIT + T * i + T] for i in range(2)]
        rot = [S1[:, UNIT + 1024 + T * i:UNIT + 1024 + T * i + T] for i in range(2)]
        pe_ = [S1[:, UNIT + 2048 + 1024 * i:UNIT + 2048 + 1024 * i + 1024].rearrange("p (c k) -> p c k", c=2) for i in range(2)]
        prob = [S1[:, UNIT + 4096 + T * i:UNIT + 4096 + T * i + T] for i in range(2)]
        probT = [S1[:, UNIT + 5120 + T * i:UNIT + 5120 + T * i + T] for i in range(2)]
        osq = [S1[:, UNIT + 6144 + T * i:UNIT + 6144 + T * i + T] for i in range(2)]
        mask16 = sb("mask16", [P, 2 * P], BF16)
        stat = sb("stat", [P, 2, 8])
        fn_row = S2[0:1, 2 * UNIT:2 * UNIT + D]
        fin = [S2[:, k * D:k * D + D] for k in range(NT)]

        block = ctx.enter_context(nc.Block())

        TILES = [(0, 0, 12), (0, 128, 13)] + [(1, 128 * j, 4 + j) for j in range(4)] \
            + [(2, 128 * j, j) for j in range(4)] + [(3, 128 * j, 8 + j) for j in range(4)] \
            + [(4, 128 * j, None) for j in range(4)]
        Z_OUT = [z_l0, gateT_in[:, :]] + [kT[:, j, :] for j in range(4)] + [rT[:, j, :] for j in range(4)] \
            + [vT[:, j, :] for j in range(4)]
        LEVELS = (2, 4, 8, 16, 32)
        n_setup = 14
        NL = len(LEVELS)

        def moe_before(l, s):
            return before[f"moe{l}"][s]

        def experts_sp(sp, l):
            if stop <= 1 + 2 * l:
                return

            def load_expert(e, half, n):
                srcs = [a["moe_w_gate"][l, bass.ds(e, 1)].rearrange("o (p c) n -> (o p) c n", c=NC),
                        a["moe_w_up"][l, bass.ds(e, 1)].rearrange("o (p c) n -> (o p) c n", c=NC),
                        a["moe_w_down"][l, bass.ds(e, 1)].rearrange("o (p c) n -> (o p) c n", c=4)]
                for k, used_up in enumerate((s_gate, s_up, s_down)):
                    s = 3 * half + k
                    if not (isinstance(n, int) and n == 0):
                        sp.wait_ge(used_up, EXPERTS * l + e - 1)
                    sp.dma_start(slot_w(s, NC if k < 2 else 4), srcs[k]).then_inc(s_full[s], 16)

            sp.wait_ge(s_om, 8 * l + 8)
            load_expert(0, 0, 0)
            load_expert(1, 1, 0)
            with sp.Fori(1, EXPERTS // 2) as i:
                load_expert(2 * i, 0, i)
                load_expert(2 * i + 1, 1, i)

        @block.sync
        def _(sp):
            for i in range(NT):
                sp.dma_start(x_sb[:, i, :], a["x"][0, P * i:P * i + P, :]).then_inc(s_x, 16)
            sp.dma_start(cst[:, :], consts).then_inc(s_cst, 16)

            used_A = [(s_proj, 2), (s_proj, 6), (s_proj, 10), (s_proj, 14), (s_proj, 18), (s_om, 4), (s_om, 8)]
            used_C = [(s_qm, 4), (s_qm, 8), (s_qm, 12), (s_qm, 16), (s_vm, 4), (s_vm, 8), (s_om, 12), (s_om, 16)]

            def load_unit(used_up, slots, src, u):
                s = slots[u]
                for v in range(u - 1, -1, -1):
                    if slots[v] == s:
                        sp.wait_ge(*used_up[v])
                        break
                w = src[u].shape[2]
                sp.dma_start(slot_w(s)[:, :, 0:w], src[u]).then_inc(s_full[s], 16)

            for u in range(7):
                load_unit(used_A, A_SLOTS, A_SRC, u)
            experts_sp(sp, 0)
            if stop > 2:
                sp.dma_start(rope_sb, ropes).then_inc(s_rope, 16)
                for used_up in (s_gate, s_up, s_down):
                    sp.wait_ge(used_up, EXPERTS - 1)
                for u in range(8):
                    load_unit(used_C, C_SLOTS, C_SRC, u)
            if stop > 3:
                experts_sp(sp, 1)
            if stop > 4:
                sp.wait_ge(s_y1, 64)
                sp.dma_start(fn_row, a["final_norm"].rearrange("(o d) -> o d", o=1)).then_inc(s_rope, 16)
                for i in range(NT):
                    sp.wait_ge(s_fin, i + 1)
                    sp.dma_start(out[0, P * i:P * i + P, :], fin[i]).then_inc(s_out, 16)
                sp.wait_ge(s_out, 16 * NT)
            if dbg is not None:
                sp.wait_ge(s_res, 8) if stop == 1 else sp.wait_ge(s_comb, 4) if stop == 2 else sp.wait_ge(s_res, 16) if stop == 3 else sp.wait_ge(s_comb, 8)
                sp.dma_start(out[0].rearrange("(i p) d -> p i d", p=P), x_sb[:, :, :]).then_inc(s_out, 16)
                sp.wait_ge(s_out, 16 * (5 if stop > 4 else 1))

        @block.tensor
        def _(pe):
            def norm_transposes(n):
                cut = hn.rearrange("p i (q c) -> p i c q", c=NC)
                for c in range(NC):
                    if c >= 4:
                        pe.wait_ge(s_trv if c % 2 == 0 else s_tra, 4 * n + (c - 4) // 2 + 1)
                    for i in range(NT):
                        if c == 0:
                            pe.wait_ge(s_hn, 4 * n + i + 1)
                        ins = pe.transpose(bank(c % 4)[:, P * i:P * i + P], cut[:, i, c, :], ident)
                    ins.then_inc(s_tr, 1)
                pe.wait_ge(s_trv, 4 * n + 4)
                pe.wait_ge(s_tra, 4 * n + 4)

            def quarter_mms(out_of, l_of, r_of, per=1):
                ins = None
                for h0 in range(0, H, 2):
                    for flip in range(2):
                        for s in range(2):
                            h = h0 + (s ^ flip)
                            ins = pe.matmul(out_of(h, s), l_of(h, s), r_of(h, s), start=True, stop=True)
                return ins

            pe.wait_ge(s_cst, 16)
            norm_transposes(0)

            def project(m):
                u, col, _ = TILES[m]
                s = A_SLOTS[u]
                if col == 0:
                    pe.wait_ge(s_full[s], 16 * use("A", A_SLOTS, u))
                if m >= 4:
                    pe.wait_ge(s_z, m - 3)
                for c in range(NC):
                    ins = pe.matmul(bank(4 + m % 4), slot_w(s)[:, c, col:col + P], hnT[:, c, :], start=(c == 0), stop=(c == NC - 1))
                ins.then_inc(s_proj, 1)

            for m in range(6):
                project(m)
            pe.wait_ge(s_vec, n_vec)
            pe.wait_ge(s_tanh, 1)
            for j in range(NPAIR):
                if j >= 2:
                    pe.wait_ge(s_am, j - 1)
                b = 2 * (j % 2)
                pe.matmul(bank(b), lora_w[0:64, P * j:P * j + P], z_l0[0:64, :], start=True, stop=True)
                pe.matmul(bank(b + 1), lora_w[64:128, P * j:P * j + P], z_l0[64:128, :], start=True, stop=True).then_inc(s_lora, 1)
            for m in range(6, 10):
                project(m)
            pe.wait_ge(s_am, 4)
            for j in range(NPAIR):
                pe.wait_ge(s_sq, j + 1)
                pe.matmul(bank(0)[0:H, :], K("head_sel")[:, H * j:H * j + H], sq_tmp[j % 2], start=(j == 0), stop=(j == 3)).then_inc(s_hsum, 1)
            for m in range(10, 14):
                project(m)
            pe.wait_ge(s_hinv, 1)
            for j in range(NPAIR):
                pe.matmul(bank(j), K("head_spread", H)[:, P * j:P * j + P], hs, start=True, stop=True).then_inc(s_hb, 1)
            for m in range(14, 18):
                project(m)
            pe.wait_ge(s_rkp, 4)
            pe.wait_ge(s_kk, 4)
            for j in range(NPAIR):
                ins = pe.matmul(bank(0)[0:H, :], K("head_sel")[:, H * j:H * j + H], rk_tmp[:, j, :], start=(j == 0), stop=(j == 3))
            ins.then_inc(s_hsum, 1)
            for g in range(4):
                pe.wait_ge(s_pd, g + 1)
                pe.matmul(bank(4 + (18 + g) % 4), wpool[:, g, :], ybT[:, g, :], start=True, stop=True).then_inc(s_pmm, 1)
            pe.wait_ge(s_rs, 1)
            for j in range(NPAIR):
                pe.matmul(bank(j), K("head_spread", H)[:, P * j:P * j + P], hs, start=True, stop=True).then_inc(s_hb, 1)

            pe.wait_ge(s_prep, 4)
            pe.wait_ge(s_prepp, 4)
            pe.wait_ge(s_bon, 4)
            pe.wait_ge(s_yb, 4)
            for g in range(16):
                q, arr = g // 4, (vT, alT, kT, aT)[g % 4]
                if g >= 8:
                    pe.wait_ge(s_tev if g % 2 == 0 else s_tea, (g - 8) // 2 + 1)
                for j in range(NPAIR):
                    ins = pe.transpose(bank(g % 8)[:, P * j:P * j + P], arr[:, j, P * q:P * q + P], ident)
                ins.then_inc(s_tt, 1)
            pe.wait_ge(s_tev, 8)
            pe.wait_ge(s_tea, 8)

            def ch(arr, h, c):
                po = N * (h % 2)
                return arr[po:po + N, h // 2, C * c:C * c + C]

            def mat(ap, h, s):
                o_ = C * (NPAIR * (h % 2) + h // 2)
                return ap[C * s:C * s + C, o_:o_ + C]

            def tok(ap, h, s):
                return ap[C * s:C * s + C, N * h:N * h + N]

            def local(pr):
                for b in range(2):
                    q = 2 * pr + b
                    for k, (l, r) in enumerate(((aT, alT), (alT, aT), (kT, alT), (kT, rT), (aT, rT))):
                        if b == 1 and k // 2 >= 1:
                            pe.wait_ge(s_gv, 5 * (q - 1) + 2 if k // 2 == 1 else 5 * (q - 1) + 4)
                        bk, o_ = gram_place(q, k)
                        quarter_mms(lambda h, s: bk[C * s:C * s + C, h % 2, o_ + C * (h // 2):o_ + C * (h // 2) + C], lambda h, s: ch(l, h, 2 * q + s), lambda h, s: ch(r, h, 2 * q + s)).then_inc(s_gm, 1)
                pe.wait_ge(s_gv, 10 * pr + 10)
                for lv in range(NL):
                    for b in range(2):
                        q, w, n = 2 * pr + b, wk[b], 2 * NL * pr + 2 * lv + b
                        pe.wait_ge(s_jb, n + 1)
                        if lv > 0:
                            pe.wait_ge(s_jtv, n - 1)
                        quarter_mms(lambda h, s: mat(bank(b), h, s), lambda h, s: mat(w["Bm"], h, s), lambda h, s: mat(w["Tm"], h, s)).then_inc(s_jx, 1)
                    for b in range(2):
                        q, w, n = 2 * pr + b, wk[b], 2 * NL * pr + 2 * lv + b
                        pe.wait_ge(s_jxa, n + 1)
                        if lv < NL - 1:
                            quarter_mms(lambda h, s: mat(bank(2 + b), h, s), lambda h, s: mat(w["TT"], h, s), lambda h, s: mat(w["X"], h, s))
                        quarter_mms(lambda h, s: mat(bank(4 + b), h, s), lambda h, s: mat(w["X"], h, s), lambda h, s: mat(w["TT"], h, s)).then_inc(s_jt, 1)
                for b in range(2):
                    q, w = 2 * pr + b, wk[b]
                    pe.wait_ge(s_jtv, 2 * NL * pr + 2 * NL - 1 + b)
                    quarter_mms(lambda h, s: mat(bank(b), h, s), lambda h, s: mat(w["AK"], h, s), lambda h, s: tok(v_tok[:, q, :], h, s)).then_inc(s_lx, 1)
                    ob = bank_pair[1 + 2 * b]
                    quarter_mms(lambda h, s: ob[N * (h % 2):N * (h % 2) + N, s, C * (h // 2):C * (h // 2) + C], lambda h, s: tok(al_tok[:, q, :], h, s), lambda h, s: mat(w["TT"], h, s)).then_inc(s_lw, 1)
                for b in range(2):
                    q, w = 2 * pr + b, wk[b]
                    pe.wait_ge(s_lxa, q + 1)
                    quarter_mms(lambda h, s: mat(bank(4 + b), h, s), lambda h, s: mat(w["TT"], h, s), lambda h, s: mat(w["X"], h, s)).then_inc(s_lu, 1)

            def sequence(c):
                q, s, kp = c // 2, c % 2, keep[c // 2]
                st = ST[c % 2]
                pe.wait_ge(s_sv, c + 1)
                wt = kp["WT"].rearrange("p (s j t) -> p s j t", s=2, j=NPAIR)
                for h in range(H):
                    po = N * (h % 2)
                    ins = pe.matmul(bank_pair[3][C * s:C * s + C, h % 2, C * (h // 2):C * (h // 2) + C], wt[po:po + N, s, h // 2, :],
                                    st[po:po + N, h // 2, :], start=True, stop=True)
                ins.then_inc(s_um, 1)
                if c >= 2:
                    pe.wait_ge(s_ya, c - 1)
                y_at = lambda h: bank(s)[N * (h % 2):N * (h % 2) + N, C * (h // 2):C * (h // 2) + C]
                for h in range(H):
                    ins = pe.matmul(y_at(h), st[N * (h % 2):N * (h % 2) + N, h // 2, :], ch(rT, h, c), start=(h < 2), stop=False, skip_group_check=True)
                ins.then_inc(s_y0m, 1)
                pe.wait_ge(s_ua, c + 1)
                for h in range(H):
                    po = N * (h % 2)
                    o_ = bank(5)[po:po + N, N * (h // 2):N * (h // 2) + N]
                    pe.matmul(o_, tok(k_tok[:, q, :], h, s), tok(v_tok[:, q, :], h, s), start=True, stop=False)
                    ins = pe.matmul(o_, tok(b_tok[:, q, :], h, s), mat(u_neg, h, s), start=False, stop=True)
                ins.then_inc(s_sm, 1)
                pe.wait_ge(s_y0m, c + 1)
                for h in range(H):
                    pe.matmul(y_at(h), tok(v_tok[:, q, :], h, s), mat(kp["RK"], h, s), start=False, stop=False, skip_group_check=True)
                    ins = pe.matmul(y_at(h), mat(u_neg, h, s), mat(kp["RB"], h, s), start=False, stop=(h >= 6), skip_group_check=True)
                ins.then_inc(s_ym, 1)

            local(0)
            pe.wait_ge(s_luv, 2)
            pe.wait_ge(s_lwa, 2)
            sequence(0)
            sequence(1)
            pe.wait_ge(s_ya, 2)
            pe.wait_ge(s_sv, 3)
            local(1)
            pe.wait_ge(s_luv, 4)
            pe.wait_ge(s_lwa, 4)
            for c in range(2, NCH):
                sequence(c)
            pe.wait_ge(s_ya, NCH)
            pe.wait_ge(s_g, 1)
            for j in range(NPAIR):
                pe.matmul(bank(j), K("head_mean"), yT[:, j, :], start=True, stop=True).then_inc(s_gn, 1)
            pe.wait_ge(s_sv, NCH + 1)
            for j in range(NPAIR):
                ins = pe.matmul(bank(4 + j), gate_w2[:, P * j:P * j + P], gateT_in[:, :], start=True, stop=True)
            ins.then_inc(s_gmm, 1)
            pe.wait_ge(s_gnv, 4)
            for j in range(NPAIR):
                pe.wait_ge(s_gna, j + 1)
                ins = pe.matmul(bank(0)[0:H, :], K("head_sel")[:, H * j:H * j + H], yc_sq[:, T * j:T * j + T], start=(j == 0), stop=(j == 3))
            ins.then_inc(s_gn, 1)
            pe.wait_ge(s_gnv, 6)
            for j in range(NPAIR):
                pe.matmul(bank(j), K("head_spread", H)[:, P * j:P * j + P], hs, start=True, stop=True).then_inc(s_gn, 1)

            def out_project(n, phase, slots, u0, part):
                for half in range(2):
                    s = slots[u0 + half]
                    pe.wait_ge(s_full[s], 16 * use(phase, slots, u0 + half))
                    for i in range(NT):
                        for c in range(NC):
                            ins = pe.matmul(bank(4 * half + i), part(c)[:, P * i:P * i + P], slot_w(s)[:, c, :], start=(c == 0), stop=(c == NC - 1))
                        ins.then_inc(s_om, 1)

            pe.wait_ge(s_yav, 4)
            out_project(0, "A", A_SLOTS, 5, lambda c: yT[:, c, :] if c < 4 else ybT[:, c - 4, :])

            def router_mms(l):
                pe.wait_ge(s_rw, 32 * (l + 1))
                for i in range(NT):
                    o_ = bank(4)[:, 64 * i:64 * i + 36]
                    for c in range(NC):
                        pe.matmul(o_, hnT[:, c, P * i:P * i + P], w_router[:, c, :], start=(c == 0), stop=False)
                    ins = pe.matmul(o_, K("ones", 1), rowv[0:1, 36 * l:36 * l + 36], start=False, stop=True)
                ins.then_inc(s_lg, 1)
                pe.wait_ge(s_oh, l + 1)
                hot = S2[:, rt0 + 1536:rt0 + 1664].rearrange("p (i e) -> p i e", i=NT)
                for i in range(NT):
                    o_ = bank(5)[:, 32 * i:32 * i + 32]
                    for i2 in range(i):
                        pe.matmul(o_, K("ones"), hot[:, i2, :], start=(i2 == 0), stop=False)
                    pe.matmul(o_, K("earlier"), hot[:, i, :], start=(i == 0), stop=True)
                for i in range(NT):
                    ins = pe.matmul(bank(5)[:, 128:160], K("ones"), hot[:, i, :], start=(i == 0), stop=(i == 3))
                ins.then_inc(s_rk, 1)

            XTB, GB, UB, HTB, YB = bank67, bank(0), bank(1), bank(2), (bank(3), bank(4))

            def block_transposes(par, n_wait):
                n_wait()
                cut = rows[par].rearrange("p (q c) -> p c q", c=NC)
                for c in range(NC):
                    ins = pe.transpose(XTB[:, c // 4, TB * (c % 4):TB * (c % 4) + TB], cut[:, c, :], ident[0:TB, 0:TB])
                return ins

            def mm_in(o_, par, w):
                for c in range(NC):
                    ins = pe.matmul(o_[0:TB, :], xT[par][:, c, :], w[:, c, :], start=(c == 0), stop=(c == NC - 1))
                return ins

            def hidden_transposes(par):
                cut = hid[par].rearrange("p (q c) -> p c q", c=4)
                for c in range(4):
                    ins = pe.transpose(HTB[:, TB * c:TB * c + TB], cut[:, c, :], ident[0:TB, 0:TB])
                return ins

            def mm_down(par, w):
                for half in range(2):
                    for c in range(4):
                        ins = pe.matmul(YB[half][0:TB, :], hidT[par][:, c, :], w[:, c, 512 * half:512 * half + 512], start=(c == 0), stop=(c == 3))
                return ins

            def experts(l):
                B = EXPERTS * l

                def step(e, par, n, first=False, last=False):
                    sl = 3 * par
                    n1 = n if par == 1 else n - 1
                    pe.wait_ge(s_xtv, B + e + 1)
                    if not (first and l == 0):
                        pe.wait_ge(s_h1, B + e)
                    pe.wait_ge(s_full[sl], 16 * (moe_before(l, sl) + n + 1))
                    mm_in(GB, par, slot_w(sl)).then_inc(s_gate, 1)
                    if not first:
                        pe.wait_ge(s_h, B + e)
                        hidden_transposes(1 - par).then_inc(s_ht, 1)
                    pe.wait_ge(s_full[sl + 1], 16 * (moe_before(l, sl + 1) + n + 1))
                    mm_in(UB, par, slot_w(sl + 1)).then_inc(s_up, 1)
                    if not last:
                        pe.wait_ge(s_rows[1 - par], 16 * (16 * l + (n + 1 if par == 1 else n) + 1))
                        block_transposes(1 - par, lambda: None).then_inc(s_xt, 1)
                    if not first:
                        down(e, 1 - par, n1)

                def down(e, par, n):
                    sl = 3 * par + 2
                    pe.wait_ge(s_hta, B + e)
                    if not (l == 0 and isinstance(e, int) and e == 1):
                        pe.wait_ge(s_y0, B + e - 1)
                        pe.wait_ge(s_y1, B + e - 1)
                    pe.wait_ge(s_full[sl], 16 * (moe_before(l, sl) + n + 1))
                    mm_down(par, slot_w(sl, 4)).then_inc(s_down, 1)

                pe.wait_ge(s_slot, 4 * l + 4)
                pe.wait_ge(s_rows[0], 16 * (16 * l + 1))
                block_transposes(0, lambda: None).then_inc(s_xt, 1)
                step(0, 0, 0, first=True)
                with pe.Fori(0, EXPERTS // 2 - 1) as i:
                    step(2 * i + 1, 1, i)
                    step(2 * i + 2, 0, i + 1)
                step(EXPERTS - 1, 1, EXPERTS // 2 - 1, last=True)
                pe.wait_ge(s_h, B + EXPERTS)
                hidden_transposes(1).then_inc(s_ht, 1)
                down(EXPERTS, 1, EXPERTS // 2 - 1)
                pe.wait_ge(s_y0, B + EXPERTS)
                pe.wait_ge(s_y1, B + EXPERTS)
                v = s_ov[l]
                n = pe.value_load(extra_tab[0:1, 0:1], min_val=0, max_val=EXTRA)
                with pe.If(n > 0):
                    with pe.Fori(0, n) as b:
                        pe.wait_ge(v["rows"], 16 * b + 16)
                        block_transposes(0, lambda: None).then_inc(v["pe"], 1)
                        wait_extra(pe, l, "xtv", b)
                        pe.wait_ge(v["w"], 48 * b + 48)
                        mm_in(GB, 0, slot_w(3))
                        mm_in(UB, 0, slot_w(4)).then_inc(v["pe"], 1)
                        wait_extra(pe, l, "h", b)
                        hidden_transposes(0).then_inc(v["pe"], 1)
                        wait_extra(pe, l, "hta", b)
                        mm_down(0, slot_w(5, 4)).then_inc(v["pe"], 1)
                        wait_extra(pe, l, "y1", b)
                        wait_extra(pe, l, "y0", b)

            def experts_phase(l):
                norm_transposes(1 + 2 * l)
                router_mms(l)
                experts(l)

            def mixer_c():
                norm_transposes(2)
                for m in range(16):
                    u = m // 4
                    s = C_SLOTS[u]
                    if m % 4 == 0:
                        pe.wait_ge(s_full[s], 16 * use("C", C_SLOTS, u))
                    if m >= 4:
                        pe.wait_ge(s_qa, m - 3)
                    for c in range(NC):
                        ins = pe.matmul(bank(4 + m % 4), slot_w(s)[:, c, P * (m % 4):P * (m % 4) + P], hnT[:, c, :], start=(c == 0), stop=(c == NC - 1))
                    ins.then_inc(s_qm, 1)
                    if m >= 1:
                        rotate(m - 1)
                rotate(15)
                pe.wait_ge(s_qa, 16)
                for half in range(2):
                    s = C_SLOTS[4 + half]
                    pe.wait_ge(s_full[s], 16 * use("C", C_SLOTS, 4 + half))
                    for i in range(NT):
                        for c in range(NC):
                            ins = pe.matmul(bank(4 + i), hnT[:, c, P * i:P * i + P], slot_w(s)[:, c, :], start=(c == 0), stop=(c == NC - 1))
                            if half == 1 and c == 0:
                                pass
                        ins.then_inc(s_vm, 1)
                        if half == 0 and i == NT - 1:
                            pass
                    pe.wait_ge(s_va, NT * (half + 1))
                pe.wait_ge(s_lamm_in, 1)
                pe.matmul(bank(4)[:, 0:2], K("ones", 64), cols["lam"][0:64, 0:2], start=True, stop=True).then_inc(s_lamm, 1)
                pe.wait_ge(s_mk, 2)
                pe.wait_ge(s_qv, 16)
                for k in range(H * NT):
                    scores(k)
                    if k >= 1:
                        values(k - 1)
                values(H * NT - 1)
                for h in range(H):
                    pe.wait_ge(s_osq, h + 1)
                    if h >= 2:
                        pe.wait_ge(s_ort, h - 1)
                    pe.matmul(bank(h % 2), K("ones"), osq[h % 2], start=True, stop=True).then_inc(s_osm, 1)
                pe.wait_ge(s_on, 8)
                out_project(1, "C", C_SLOTS, 6, lambda c: oT[:, c, :])

            def rotate(m):
                pe.wait_ge(s_qa, m + 1)
                if m >= 2:
                    pe.wait_ge(s_qv, m - 1)
                if m == 0:
                    pe.wait_ge(s_rope, 16)
                pe.matmul(bank(m % 2), swap, raw[m % 2], start=True, stop=True).then_inc(s_rm, 1)

            SB = [[bank(0), bank(1)], [bank(2), bank(3)]]

            def scores(k):
                h, b = k // NT, k % NT
                w = P * (b + 1)
                if k >= 2:
                    pe.wait_ge(s_ex, 2 * (k - 1))
                for c in range(2):
                    pe.matmul(SB[k % 2][c][:, 0:w], qT[64 * c:64 * c + 64, h, P * b:P * b + P], kaT[64 * c:64 * c + 64, h, 0:w], start=True, stop=False)
                for c in range(2):
                    ins = pe.matmul(SB[k % 2][c][:, w - P:w], mask16[:, 0:P], mask16[:, P:2 * P], start=False, stop=True)
                ins.then_inc(s_sc, 1)

            def values(k):
                h, b = k // NT, k % NT
                pe.wait_ge(s_pr, k + 1)
                if k >= 2:
                    pe.wait_ge(s_pta, k - 1)
                for t in range(b + 1):
                    ins = pe.transpose(bank(4 + k % 2)[:, P * t:P * t + P], prob[k % 2][:, P * t:P * t + P], ident)
                ins.then_inc(s_pt, 1)
                pe.wait_ge(s_pta, k + 1)
                if b == 0 and h >= 2:
                    pe.wait_ge(s_oc, h - 1)
                for t in range(b + 1):
                    ins = pe.matmul(bank(6 + h % 2)[:, P * b:P * b + P], v_att[:, t, P * h:P * h + P], probT[k % 2][:, P * t:P * t + P], start=(t == 0), stop=(t == b))
                if b == NT - 1:
                    ins.then_inc(s_ov_, 1)

            if stop > 1:
                experts_phase(0)
            if stop > 2:
                mixer_c()
            if stop > 3:
                experts_phase(1)
            if stop > 4:
                pe.wait_ge(s_rope, 32)
                for half in range(2):
                    ins = pe.matmul(bank67[:, half, :], K("ones", 1), fn_row[:, 512 * half:512 * half + 512], start=True, stop=True)
                ins.then_inc(s_fnb, 1)

        @block.vector
        def _(dve):
            own = Steps(dve, s_dve)

            def norm(n):
                for i in range(NT):
                    if i == 0:
                        dve.wait_ge(s_rstd, n + 1)
                    dve.tensor_scalar(hn[:, i, :], x_sb[:, i, :], cols["rstd"][:, i:i + 1], None, ALU.mult).then_inc(s_hn, 1)
                g = cols[("g_mix0", "g_ffn0", "g_mix1", "g_ffn1")[n]]
                for c in range(0, NC, 2):
                    dve.wait_ge(s_tr, 8 * n + c + 1)
                    dve.tensor_scalar(hnT[:, c, :], bank(c % 4), g[:, c:c + 1], None, ALU.mult).then_inc(s_trv, 1)

            own.next(dve.memset(zeros, 0.0))
            dve.nop().then_inc(s_zero, 1)
            dve.memset(ST[0][:, :, :], 0.0).then_inc(s_sv, 1)
            own.mark(dve.memset(cols["sub_eps"], SUBLN_EPS))
            own.mark(dve.memset(cols["half_decay"], -0.5 * math.exp(-0.5)))
            dve.wait_ge(s_vec, n_vec)
            own.mark(dve.tensor_scalar(cols["one_minus_mu"], cols["mu"], -1.0, 1.0, ALU.mult, ALU.add))
            own.mark(dve.tensor_scalar(cols["half_w0"], cols["w0"], 0.5, None, ALU.mult))
            own.mark(dve.tensor_scalar(cols["half_a0"], cols["a0"], 0.5, None, ALU.mult))
            own.mark(dve.tensor_tensor(cols["lam"][0:64, 0:1], cols["lq"][0:64, 0:1], cols["lq"][0:64, 1:2], ALU.mult))
            own.mark(dve.tensor_tensor(cols["lam"][0:64, 1:2], cols["lq"][0:64, 2:3], cols["lq"][0:64, 3:4], ALU.mult))
            own.mark(dve.tensor_scalar(cols["subln_s"], cols["subln"], 1.0 - LAMBDA_INIT, None, ALU.mult))
            own.hold()
            dve.nop().then_inc(s_lamm_in, 1)
            norm(0)
            dve.wait_ge(s_tr, 8)
            for i in range(3):
                own.mark(dve.memset(upad[i][:, 0:PAD], 0.0))
            for i in range(2):
                own.mark(dve.memset(shift[i][:, 0:1], 0.0))
            own.hold()

            def z(m):
                dve.wait_ge(s_sh, m + 1)
                col = TILES[m][2]
                dve.scalar_tensor_tensor(out=Z_OUT[m], in0=bank(4 + m % 4), scalar=cols["one_minus_mu"][:, col:col + 1], in1=shift[m % 2][:, 0:T],
                                         op0=ALU.mult, op1=ALU.add).then_inc(s_z, 1)

            for m in range(6):
                z(m)
            dve.wait_ge(s_tanh, 2)
            dve.tensor_scalar(gateT_in[:, :], gateT_in[:, :], 0.5, 0.5, ALU.mult, ALU.add).then_inc(s_g, 1)
            for j in range(NPAIR):
                z(6 + j)
                dve.wait_ge(s_wdec, j + 1)
                dve.wait_ge(s_sq, j + 1)
                own.mark(dve.tensor_scalar(kkT[:, j, :], kT[:, j, :], cols["k_k"][:, j:j + 1], None, ALU.mult))
                own.next(dve.tensor_scalar(aT[:, j, :], aT[:, j, :], 0.5, 0.5, ALU.mult, ALU.add))
                own.next(dve.tensor_scalar(alT[:, j, :], aT[:, j, :], -1.0, cols["k_a"][:, j:j + 1], ALU.add, ALU.mult))
                own.next(dve.scalar_tensor_tensor(out=kT[:, j, :], in0=alT[:, j, :], scalar=1.0, in1=kT[:, j, :], op0=ALU.add, op1=ALU.mult))
                if j == 0:
                    own.mark(dve.memset(scan_in, 0.0))
                    own.hold()
                own.next(dve.tensor_copy(scan_in[:, 0:T:C], wT[:, j, 0:T:C]))
                own.next(dve.memset(wT[:, j, 0:T:C], 0.0))
                own.next(dve.tensor_tensor_scan(pT[:, j, :], wT[:, j, :], scan_in, 0.0, ALU.mult, ALU.add))
                own.mark(dve.tensor_copy(pc[:, j, :], pT[:, j, C - 1:T:C]))
                own.mark(dve.scalar_tensor_tensor(out=rk_tmp[:, j, :], in0=rT[:, j, :], scalar=cols["r_k"][:, j:j + 1], in1=kT[:, j, :], op0=ALU.mult, op1=ALU.mult))
            own.hold()
            dve.nop().then_inc(s_rkp, 4)
            for j in range(NPAIR):
                z(10 + j)
                own.mark(dve.reciprocal(piT[:, j, :], pT[:, j, :]))
                if j == 0:
                    dve.wait_ge(s_hroot, 1)
                    own.next(dve.tensor_scalar(hs, hs, 1e-12, None, ALU.max))
                    own.next(dve.reciprocal(hs, hs))
                    dve.nop().then_inc(s_hinv, 1)
            own.hold()
            for j in range(NPAIR):
                dve.wait_ge(s_hb, j + 1)
                own.next(dve.tensor_tensor(kkT[:, j, :], kkT[:, j, :], bank(j), ALU.mult))
                dve.nop().then_inc(s_kk, 1)
                c3 = lambda ap: ap.rearrange("p (c t) -> p c t", c=NCH)
                own.mark(dve.tensor_tensor(c3(alT[:, j, :])[:, :, 1:C], c3(kkT[:, j, :])[:, :, 1:C], c3(pT[:, j, :])[:, :, 0:C - 1], ALU.mult))
                own.mark(dve.tensor_copy(alT[:, j, 0:T:C], kkT[:, j, 0:T:C]))
                own.next(dve.tensor_tensor(aT[:, j, :], aT[:, j, :], kkT[:, j, :], ALU.mult))
                own.next(dve.tensor_tensor(aT[:, j, :], aT[:, j, :], piT[:, j, :], ALU.mult))
                dve.nop().then_inc(s_prep, 1)
            for g in range(4):
                dve.wait_ge(s_win, g + 1)
                dve.scalar_tensor_tensor(out=ybT[:, g, :], in0=upad[1 + g % 2][:, PAD:PAD + T], scalar=1.0 / WINDOWS[g], in1=upad[0][:, PAD:PAD + T],
                                         op0=ALU.mult, op1=ALU.subtract).then_inc(s_pd, 1)
            dve.wait_ge(s_zrows, 16 * n_zero)
            for j in range(NPAIR):
                dve.wait_ge(s_hb, 5 + j)
                dve.tensor_tensor(bonT[:, j, :], bank(j), vT[:, j, :], ALU.mult).then_inc(s_bon, 1)
            for g in range(0, 16, 2):
                dve.wait_ge(s_tt, g + 1)
                dve.tensor_copy((v_tok, al_tok, k_tok, b_tok)[g % 4][:, g // 4, :], bank(g % 8)).then_inc(s_tev, 1)

            def masked(o_, src, m):
                return dve.tensor_tensor(heads(o_), heads(src), per_head(K(m)), ALU.mult)

            def plus_eye(o_):
                return dve.tensor_tensor(heads(o_), heads(o_), per_head(K("eye64")), ALU.add)

            def grams(q):
                w, kp = wk[q % 2], keep[q]

                def finish(k):
                    dve.nop().then_inc(s_gv, 1)


                def b_(k):
                    bk, o_ = gram_place(q, k)
                    return bk[:, :, o_:o_ + 256]

                dve.wait_ge(s_gm, 5 * q + 2)
                own.next(masked(w["LT"], b_(0), "strict"))
                own.next(masked(w["TT"], w["LT"], "up1"))
                own.next(plus_eye(w["TT"]))
                finish(0)
                own.next(masked(w["Tm"], b_(1), "low1"))
                own.next(plus_eye(w["Tm"]))
                finish(1)
                for k, name, m in ((2, "AK", "strict"), (3, "RK", "upto"), (4, "RB", "upto")):
                    dve.wait_ge(s_gm, 5 * q + (4 if k < 4 else 5))
                    masked(w[name] if name == "AK" else kp[name], b_(k), m).then_inc(s_gv, 1)

            def local(pr):
                grams(2 * pr)
                grams(2 * pr + 1)
                dve.wait_ge(s_gv, 10 * pr + 10)
                for lv in range(NL):
                    for b in range(2):
                        w = wk[b]
                        dve.wait_ge(s_jt, 2 * NL * pr + 2 * lv + b + 1)
                        if lv < NL - 1:
                            own.mark(dve.tensor_tensor(w["Tm"], w["Tm"], bank(2 + b), ALU.subtract))
                        own.next(dve.tensor_tensor(w["TT"], w["TT"], bank(4 + b), ALU.subtract))
                        dve.nop().then_inc(s_jtv, 1)
                for b in range(2):
                    q = 2 * pr + b
                    dve.wait_ge(s_lu, q + 1)
                    dve.tensor_scalar(keep[q]["UV"], bank(4 + b), -1.0, None, ALU.mult).then_inc(s_luv, 1)
                dve.wait_ge(s_luv, 2 * pr + 2)

            def sequence(c):
                q, s = c // 2, c % 2
                r = slice(C * s, C * s + C)
                dve.wait_ge(s_um, c + 1)
                if c >= 2:
                    dve.wait_ge(s_ym, c - 1)
                dve.scalar_tensor_tensor(out=both(u_neg[r, :]), in0=bank_pair[3][r, :, 0:256], scalar=-1.0, in1=both(keep[q]["UV"][r, :]), op0=ALU.mult, op1=ALU.add).then_inc(s_ua, 1)
                dve.wait_ge(s_sm, c + 1)
                if c >= 1:
                    dve.wait_ge(s_ym, c)
                own.next(dve.tensor_tensor(STs[:, :, :], ST[c % 2][:, :, :], bank(5)[:, 0:256].rearrange("p (j i) -> p j i", j=NPAIR), ALU.add))
                dve.tensor_tensor(ST[(c + 1) % 2][:, :, :], STs[:, :, :], pc[:, :, c:c + 1].to_broadcast([P, NPAIR, N]), ALU.mult).then_inc(s_sv, 1)
                dve.wait_ge(s_sv, c + 2)

            local(0)
            sequence(0)
            sequence(1)
            local(1)
            for c in range(2, NCH):
                sequence(c)
            for j in range(NPAIR):
                dve.wait_ge(s_gn, j + 1)
                dve.tensor_tensor(yT[:, j, :], yT[:, j, :], bank(j), ALU.subtract).then_inc(s_gnv, 1)
            dve.wait_ge(s_gn, 5)
            own.next(dve.tensor_scalar(hs, bank(0)[0:H, :], 1.0 / N, GN_EPS, ALU.mult, ALU.add))
            dve.nop().then_inc(s_gnv, 1)
            dve.wait_ge(s_gna, 5)
            own.next(dve.reciprocal(hs, hs))
            dve.nop().then_inc(s_gnv, 1)
            for j in range(NPAIR):
                dve.wait_ge(s_gn, 6 + j)
                y = yT[:, j, :]
                own.next(dve.tensor_tensor(y, y, bank(j), ALU.mult))
                own.next(dve.tensor_scalar(y, y, cols["ln_w"][:, j:j + 1], cols["ln_b"][:, j:j + 1], ALU.mult, ALU.add))
                own.next(dve.tensor_tensor(y, y, bonT[:, j, :], ALU.add))
                if j == 0:
                    dve.wait_ge(s_gmm, 1)
                dve.tensor_tensor(y, y, bank(4 + j), ALU.mult).then_inc(s_yav, 1)

            def residual(n):
                for o8 in range(8):
                    half, i = o8 // 4, o8 % 4
                    dve.wait_ge(s_om, 8 * n + o8 + 1)
                    xs = x_sb[:, i, 512 * half:512 * half + 512]
                    dve.tensor_tensor(xs, xs, bank(o8), ALU.add).then_inc(s_res, 1)
                dve.wait_ge(s_res, 8 * n + 8)

            residual(0)

            def router(l):
                at_ = [rt0]

                def tmp(*shape):
                    n = int(np.prod(shape))
                    v = S2[:, at_[0]:at_[0] + n]
                    at_[0] += n
                    return v.rearrange("p (a b) -> p a b", a=shape[0]) if len(shape) == 2 else v

                n4 = lambda name, k: K(name).unsqueeze(1).to_broadcast([P, NT, k])
                over = lambda ap, k: ap.unsqueeze(2).to_broadcast([P, NT, k])
                gl, el, gm, gd = tmp(NT, 4), tmp(NT, 32), tmp(4), tmp(NT, 4)
                cand, cmin, og = tmp(NT, 4), tmp(4), tmp(NT, 4)
                gsum, gw = tmp(4), tmp(4)
                em, cd, oh1, oh2 = tmp(NT, 32), tmp(NT, 32), tmp(NT, 32), tmp(NT, 32)
                m1, m2, cm, e2, den = tmp(4), tmp(4), tmp(4), tmp(4), tmp(4)
                rank, sl, ex, rv = tmp(NT, 32), tmp(NT, 32), tmp(NT, 32), tmp(NT, 32)
                cnt, nov, incl, bo = tmp(32), tmp(32), tmp(32), tmp(32)
                sf = tmp(2, NT)
                assert at_[0] <= rt0 + 1536
                at_[0] = rt0 + 1536
                hot = tmp(NT, 32)
                tab = S2[:, th_at:th_at + EXTRA * 32].rearrange("p (b e) -> p b e", b=EXTRA)
                tabf = S2[:, th_at + EXTRA * 32:th_at + EXTRA * 32 + 1 + EXTRA]
                lgv = bank(4)[:, 0:256].rearrange("p (i n) -> p i n", i=NT)

                dve.wait_ge(s_lg, l + 1)
                own.mark(dve.tensor_copy(gl, lgv[:, :, 0:4]))
                own.next(dve.tensor_copy(el, lgv[:, :, 4:36]))
                own.next(dve.tensor_reduce(gm, gl, AX, ALU.max))
                own.next(dve.tensor_tensor(gd, gl, over(gm, 4), ALU.subtract))
                dve.nop().then_inc(s_rt, 1)
                own.next(dve.tensor_tensor(cand, gl, over(gm, 4), ALU.is_ge))
                own.next(dve.scalar_tensor_tensor(out=cand, in0=cand, scalar=-100.0, in1=n4("iota4", 4), op0=ALU.mult, op1=ALU.add))
                own.next(dve.tensor_reduce(cmin, cand, AX, ALU.min))
                own.next(dve.tensor_tensor(og, cand, over(cmin, 4), ALU.is_equal))
                own.next(dve.tensor_scalar(cand, og, BIG, -BIG, ALU.mult, ALU.add))
                g16 = lambda ap: ap.rearrange("p i g -> p (i g)").unsqueeze(2).to_broadcast([P, NT * GROUPS, PER_GROUP])
                e16 = lambda ap: ap.rearrange("p i (g e) -> p (i g) e", g=GROUPS)
                own.next(dve.tensor_tensor(e16(em), e16(el), g16(og), ALU.mult))
                own.next(dve.tensor_tensor(e16(em), e16(em), g16(cand), ALU.add))

                def first_largest(v, m, oh):
                    own.next(dve.tensor_reduce(m, v, AX, ALU.max))
                    own.next(dve.tensor_tensor(cd, v, over(m, 32), ALU.is_ge))
                    own.next(dve.scalar_tensor_tensor(out=cd, in0=cd, scalar=-100.0, in1=n4("iota32", 32), op0=ALU.mult, op1=ALU.add))
                    own.next(dve.tensor_reduce(cm, cd, AX, ALU.min))
                    own.next(dve.tensor_tensor(oh, cd, over(cm, 32), ALU.is_equal))

                first_largest(em, m1, oh1)
                own.next(dve.scalar_tensor_tensor(out=em, in0=oh1, scalar=-2 * BIG, in1=em, op0=ALU.mult, op1=ALU.add))
                first_largest(em, m2, oh2)
                own.next(dve.tensor_tensor(hot, oh1, oh2, ALU.add))
                dve.nop().then_inc(s_oh, 1)
                own.next(dve.tensor_tensor(e2, m2, m1, ALU.subtract))
                dve.nop().then_inc(s_rt, 1)
                dve.wait_ge(s_re, 2 * l + 1)
                own.next(dve.tensor_reduce(gsum, gd, AX, ALU.add))
                own.next(dve.reciprocal(gw, gsum))
                dve.wait_ge(s_re, 2 * l + 2)
                own.next(dve.tensor_scalar(den, e2, 1.0, None, ALU.add))
                own.next(dve.reciprocal(den, den))
                own.next(dve.tensor_tensor(wts[:, 0, :], gw, den, ALU.mult))
                own.next(dve.tensor_tensor(wts[:, 1, :], wts[:, 0, :], e2, ALU.mult))
                dve.wait_ge(s_rk, l + 1)
                own.mark(dve.tensor_copy(rank, bank(5)[:, 0:128].rearrange("p (i e) -> p i e", i=NT)))
                own.next(dve.tensor_copy(cnt, bank(5)[:, 128:160]))
                own.next(dve.tensor_scalar(nov, cnt, float(TB), None, ALU.is_gt))
                for k in range(2, (T - 1) // TB + 1):
                    own.next(dve.scalar_tensor_tensor(out=nov, in0=cnt, scalar=float(TB * k), in1=nov, op0=ALU.is_gt, op1=ALU.add))
                own.next(dve.tensor_tensor_scan(incl, K("ones")[:, 0:32], nov, 0.0, ALU.mult, ALU.add))
                own.next(dve.tensor_tensor(bo, incl, nov, ALU.subtract))
                own.next(dve.tensor_scalar(bo, bo, float(TB), float(MAIN_SLOTS - TB), ALU.mult, ALU.add))
                own.next(dve.tensor_tensor(bo, bo, K("first_slot"), ALU.subtract))
                own.next(dve.tensor_scalar(ex, rank, float(TB), None, ALU.is_ge))
                own.next(dve.tensor_tensor(ex, ex, bo.unsqueeze(1).to_broadcast([P, NT, 32]), ALU.mult))
                own.next(dve.tensor_tensor(sl, rank, n4("first_slot", 32), ALU.add))
                own.next(dve.tensor_tensor(sl, sl, ex, ALU.add))
                for k, oh in enumerate((oh1, oh2)):
                    own.next(dve.tensor_tensor(rv, sl, oh, ALU.mult))
                    own.next(dve.tensor_reduce(sf[:, k, :], rv, AX, ALU.add))
                if l > 0:
                    dve.wait_ge(s_comb, NT * l)
                own.next(dve.tensor_copy(slot_ix[:, :, :], sf))
                own.next(dve.tensor_tensor(tab, incl.unsqueeze(1).to_broadcast([P, EXTRA, 32]), K("iota_extra").unsqueeze(2).to_broadcast([P, EXTRA, 32]), ALU.is_le))
                own.next(dve.tensor_reduce(tabf[:, 1:1 + EXTRA], tab, AX, ALU.add))
                own.next(dve.tensor_scalar(tabf[:, 1:1 + EXTRA], tabf[:, 1:1 + EXTRA], float(EXPERTS - 1), None, ALU.min))
                own.next(dve.tensor_copy(tabf[:, 0:1], incl[:, 31:32]))
                own.next(dve.tensor_copy(extra_tab[0:1, :], tabf[0:1, :]))
                dve.nop().then_inc(s_slot, 4)

            def block_scale(l, par):
                g = cols[f"g_ffn{l}"].rearrange("p (a c) -> p a c", a=2).unsqueeze(3).to_broadcast([P, 2, 4, TB])
                return dve.tensor_tensor(xT[par].rearrange("p (a c) t -> p a c t", a=2),
                                         bank67[:, :, 0:4 * TB].rearrange("p a (c t) -> p a c t", c=4), g, ALU.mult)

            def hidden1(par):
                return dve.scalar_tensor_tensor(out=h1, in0=th[par], scalar=1.0, in1=bank(0)[0:TB, :], op0=ALU.add, op1=ALU.mult)

            def hidden2(par):
                return dve.scalar_tensor_tensor(out=hid[par], in0=h1, scalar=0.5, in1=bank(1)[0:TB, :], op0=ALU.mult, op1=ALU.mult)

            def out1(par):
                return dve.tensor_copy(yrow[par][:, 512:1024], bank(4)[0:TB, :])

            def experts(l):
                B = EXPERTS * l

                def y1(e, par, n):
                    dve.wait_ge(s_down, B + e)
                    if not (isinstance(n, int) and n == 0 and l == 0):
                        dve.wait_ge(s_yw[par], 16 * (16 * l + n))
                    out1(par).then_inc(s_y1, 1)

                def step(e, par, n, first=False, last=False):
                    dve.wait_ge(s_th, B + e + 1)
                    if not (first and l == 0):
                        dve.wait_ge(s_h, B + e)
                    hidden1(par).then_inc(s_h1, 1)
                    dve.wait_ge(s_up, B + e + 1)
                    dve.wait_ge(s_h1, B + e + 1)
                    if not (first or (isinstance(e, int) and e == 1)):
                        dve.wait_ge(s_ht, B + e - 1)
                    hidden2(par).then_inc(s_h, 1)
                    if not last:
                        dve.wait_ge(s_xt, B + e + 2)
                        block_scale(l, 1 - par).then_inc(s_xtv, 1)
                    if not first:
                        y1(e, 1 - par, n if par == 1 else n - 1)

                dve.wait_ge(s_xt, B + 1)
                block_scale(l, 0).then_inc(s_xtv, 1)
                step(0, 0, 0, first=True)
                step(1, 1, 0)
                step(2, 0, 1)
                with dve.Fori(1, EXPERTS // 2 - 1) as i:
                    step(2 * i + 1, 1, i)
                    step(2 * i + 2, 0, i + 1)
                step(EXPERTS - 1, 1, EXPERTS // 2 - 1, last=True)
                y1(EXPERTS, 1, EXPERTS // 2 - 1)
                v = s_ov[l]
                dve.wait_ge(s_y1, B + EXPERTS)
                dve.wait_ge(s_yw[0], 16 * 16 * (l + 1))
                n = dve.value_load(extra_tab[0:1, 0:1], min_val=0, max_val=EXTRA)
                with dve.If(n > 0):
                    with dve.Fori(0, n) as b:
                        wait_extra(dve, l, "xt", b)
                        block_scale(l, 0).then_inc(v["dve"], 1)
                        wait_extra(dve, l, "th", b)
                        hidden1(0).then_inc(v["dve"], 1)
                        wait_extra(dve, l, "h1", b)
                        hidden2(0).then_inc(v["dve"], 1)
                        wait_extra(dve, l, "down", b)
                        out1(0).then_inc(v["dve"], 1)
                        dve.wait_ge(v["written"], 16 * b + 16)

            def combine(l):
                for i in range(NT):
                    dve.wait_ge(s_got[i], 32 * (l + 1))
                    for k in range(2):
                        ins = dve.scalar_tensor_tensor(out=x_sb[:, i, :], in0=got[k][i], scalar=wts[:, k, i:i + 1], in1=x_sb[:, i, :], op0=ALU.mult, op1=ALU.add)
                        if k == 0:
                            own.next(ins)
                    ins.then_inc(s_comb, 1)

            def mixer_c():
                dve.wait_ge(s_rope, 16)
                own.mark(dve.tensor_copy(mask16[:, 0:P], ident))
                own.next(dve.tensor_copy(mask16[:, P:2 * P], mask))
                dve.nop().then_inc(s_mk, 2)
                for m in range(16):
                    dst = (qT if m < 8 else kaT)[:, m % 8, :]
                    dve.wait_ge(s_qa, m + 1)
                    own.mark(dve.tensor_tensor(dst, raw[m % 2], cosT, ALU.mult))
                    dve.wait_ge(s_rm, m + 1)
                    own.next(dve.tensor_tensor(rot[m % 2], bank(m % 2), sinT, ALU.mult))
                    dve.tensor_tensor(dst, dst, rot[m % 2], ALU.add).then_inc(s_qv, 1)
                    dve.wait_ge(s_qv, m + 1)
                dve.wait_ge(s_lam, 1)
                own.next(dve.tensor_tensor(cols["lam"][:, 4:5], cols["lam"][:, 3:4], cols["lam"][:, 2:3], ALU.subtract))
                own.next(dve.tensor_scalar(cols["lam"][:, 4:5], cols["lam"][:, 4:5], -LAMBDA_INIT, None, ALU.add))

                def maxima(k):
                    w = P * (k % NT + 1)
                    st = stat[:, k % 2, :]
                    dve.wait_ge(s_sc, k + 1)
                    if k >= 2:
                        dve.wait_ge(s_pr, k - 1)
                    for c in range(2):
                        own.mark(dve.tensor_reduce(st[:, c:c + 1], bank(2 * (k % 2) + c)[:, 0:w], AX, ALU.max))
                    own.hold()
                    own.next(dve.tensor_scalar(st[:, 2:4], st[:, 0:2], -SCALE, None, ALU.mult))
                    dve.nop().then_inc(s_mx, 1)

                def probabilities(k):
                    w = P * (k % NT + 1)
                    st, p = stat[:, k % 2, :], pe_[k % 2]
                    dve.wait_ge(s_ex, 2 * k + 2)
                    own.next(dve.reciprocal(st[:, 6:8], st[:, 4:6]))
                    own.next(dve.tensor_tensor(st[:, 7:8], st[:, 7:8], cols["lam"][:, 4:5], ALU.mult))
                    if k >= 2:
                        dve.wait_ge(s_pt, k - 1)
                    own.next(dve.tensor_scalar(prob[k % 2][:, 0:w], p[:, 0, 0:w], st[:, 6:7], None, ALU.mult))
                    dve.scalar_tensor_tensor(out=prob[k % 2][:, 0:w], in0=p[:, 1, 0:w], scalar=st[:, 7:8], in1=prob[k % 2][:, 0:w], op0=ALU.mult, op1=ALU.add).then_inc(s_pr, 1)

                for k in range(H * NT):
                    maxima(k)
                    if k >= 1:
                        probabilities(k - 1)
                probabilities(H * NT - 1)
                for h in range(H):
                    dve.wait_ge(s_ort, h + 1)
                    r = osq[h % 2]
                    own.next(dve.reciprocal(r, r))
                    own.next(dve.tensor_tensor(oT[:, h, :], oT[:, h, :], r, ALU.mult))
                    dve.tensor_scalar(oT[:, h, :], oT[:, h, :], cols["subln_s"], None, ALU.mult).then_inc(s_on, 1)
                residual(1)

            if stop > 1:
                norm(1)
                router(0)
                experts(0)
                combine(0)
            if stop > 2:
                dve.wait_ge(s_comb, 4)
                norm(2)
                mixer_c()
            if stop > 3:
                norm(3)
                router(1)
                experts(1)
                combine(1)
            if stop > 4:
                dve.wait_ge(s_comb, 8)
                dve.wait_ge(s_rstd, 5)
                dve.wait_ge(s_fnb, 1)
                for i in range(NT):
                    dve.scalar_tensor_tensor(out=fin[i], in0=x_sb[:, i, :], scalar=cols["rstd"][:, i:i + 1], in1=bank67.rearrange("p a b -> p (a b)"),
                                             op0=ALU.mult, op1=ALU.mult).then_inc(s_fin, 1)

        @block.scalar
        def _(act):
            for dst, src in vec_loads:
                act.dma_start(dst, src, allow_slow_non_contiguous=True).then_inc(s_vec, 16)

            def router_weights(l):
                act.dma_start(w_router[:, :, 0:4], a["moe_w_group"][l].rearrange("(p c) n -> p c n", c=NC), allow_slow_non_contiguous=True).then_inc(s_rw, 16)
                act.dma_start(w_router[:, :, 4:36], a["moe_w_expert"][l].rearrange("(p c) n -> p c n", c=NC), allow_slow_non_contiguous=True).then_inc(s_rw, 16)

            own = Steps(act, s_act)

            def norm(n):
                src = {0: (s_x, 16 * NT, 0), 1: (s_res, 4, 1), 2: (s_comb, 0, 1), 3: (s_res, 12, 1), 4: (s_comb, 4, 1)}[n]
                for i in range(NT):
                    act.wait_ge(src[0], src[1] + src[2] * (i + 1))
                    act.activation(hn[:, i, :], x_sb[:, i, :], ACT.Square, accum_out=cols["ss"][:, i:i + 1]).then_inc(s_ss, 1)
                if n == 4:
                    return
                g = cols[("g_mix0", "g_ffn0", "g_mix1", "g_ffn1")[n]]
                if n == 0:
                    act.wait_ge(s_vec, n_vec)
                for c in range(1, NC, 2):
                    act.wait_ge(s_tr, 8 * n + c + 1)
                    act.activation(hnT[:, c, :], bank(c % 4), ACT.Copy, scale=g[:, c:c + 1]).then_inc(s_tra, 1)

            norm(0)

            def shifted(m):
                act.wait_ge(s_proj, m + 1)
                if m >= 2:
                    act.wait_ge(s_z, m - 1)
                if m == 0:
                    act.wait_ge(s_trv, 4)
                    act.wait_ge(s_dve, n_setup)
                col = TILES[m][2]
                act.activation(shift[m % 2][:, 1:T + 1], bank(4 + m % 4), ACT.Copy, scale=cols["mu"][:, col:col + 1]).then_inc(s_sh, 1)

            shifted(0)
            shifted(1)
            act.wait_ge(s_z, 1)
            act.activation(z_l0[0:64, :], z_l0[0:64, :], ACT.Tanh).then_inc(s_tanh, 1)
            act.wait_ge(s_z, 2)
            act.activation(gateT_in[:, :], gateT_in[:, :], ACT.Tanh, scale=0.5).then_inc(s_tanh, 1)
            for m in range(2, 6):
                shifted(m)
            for j in range(NPAIR):
                act.wait_ge(s_lora, j + 1)
                b = 2 * (j % 2)
                act.activation(wT[:, j, :], bank(b), ACT.Tanh, scale=0.5, bias=cols["half_w0"][:, j:j + 1]).then_inc(s_act, 1)
                act.activation(aT[:, j, :], bank(b + 1), ACT.Tanh, scale=0.5, bias=cols["half_a0"][:, j:j + 1]).then_inc(s_am, 1)
                act.wait_ge(s_am, j + 1)
                act.activation(wT[:, j, :], wT[:, j, :], ACT.Exp, scale=-0.5 * math.exp(-0.5), bias=cols["half_decay"]).then_inc(s_wdec, 1)
            for j in range(NPAIR):
                shifted(6 + j)
                if j >= 2:
                    act.wait_ge(s_hsum, j - 1)
                act.activation(sq_tmp[j % 2], kT[:, j, :], ACT.Square, scale=cols["k_k"][:, j:j + 1]).then_inc(s_sq, 1)
            act.wait_ge(s_hsum, 4)
            act.activation(hs, bank(0)[0:H, :], ACT.Sqrt).then_inc(s_hroot, 1)
            for m in range(10, 14):
                shifted(m)
            for g in range(4):
                act.wait_ge(s_proj, 15 + g)
                if g >= 1:
                    act.wait_ge(s_pd, g)
                act.activation(upad[0][:, PAD:PAD + T], bank(4 + (14 + g) % 4), ACT.Copy).then_inc(s_u, 1)
            act.wait_ge(s_hsum, 5)
            act.activation(hs, bank(0)[0:H, :], ACT.Copy).then_inc(s_rs, 1)
            for g in range(4):
                act.wait_ge(s_pmm, g + 1)
                act.activation(ybT[:, g, :], bank(4 + (18 + g) % 4), ACT.Copy, scale=cols["pool_scale"][:, g:g + 1]).then_inc(s_yb, 1)
            for g in range(1, 16, 2):
                act.wait_ge(s_tt, g + 1)
                act.activation((v_tok, al_tok, k_tok, b_tok)[g % 4][:, g // 4, :], bank(g % 8), ACT.Copy).then_inc(s_tea, 1)

            def local(pr):
                for lv in range(NL):
                    for b in range(2):
                        n = 2 * NL * pr + 2 * lv + b
                        act.wait_ge(s_jx, n + 1)
                        if lv >= 1:
                            act.wait_ge(s_jt, n - 1)
                        act.activation(wk[b]["X"], bank(b), ACT.Copy).then_inc(s_jxa, 1)
                for b in range(2):
                    q = 2 * pr + b
                    act.wait_ge(s_lx, q + 1)
                    act.wait_ge(s_jxa, 2 * NL * pr + 2 * NL)
                    act.activation(wk[b]["X"], bank(b), ACT.Copy).then_inc(s_lxa, 1)
                    act.wait_ge(s_lw, q + 1)
                    act.activation(both(keep[q]["WT"]), bank_pair[1 + 2 * b][:, :, 0:256], ACT.Copy).then_inc(s_lwa, 1)

            def sequence(c):
                q, s = c // 2, c % 2
                act.wait_ge(s_ym, c + 1)
                act.activation(yT[:, :, C * c:C * c + C], bank(s)[:, 0:256].rearrange("p (j t) -> p j t", j=NPAIR), ACT.Copy).then_inc(s_ya, 1)

            local(0)
            sequence(0)
            sequence(1)
            local(1)
            for c in range(2, NCH):
                sequence(c)
            for j in range(NPAIR):
                act.wait_ge(s_gnv, j + 1)
                act.activation(yc_sq[:, T * j:T * j + T], yT[:, j, :], ACT.Square).then_inc(s_gna, 1)
            act.wait_ge(s_gnv, 5)
            act.activation(hs, hs, ACT.Sqrt).then_inc(s_gna, 1)
            act.wait_ge(s_yav, 4)
            if stop > 1:
                router_weights(0)

            def tanh_half(par):
                return act.activation(th[par], bank(0)[0:TB, :], ACT.Tanh, scale=0.5)

            def hidden_copy(par):
                return act.activation(hidT[par], bank(2)[:, 0:4 * TB].rearrange("p (c t) -> p c t", c=4), ACT.Copy)

            def out0(par):
                return act.activation(yrow[par][:, 0:512], bank(3)[0:TB, :], ACT.Copy)

            def experts(l):
                B = EXPERTS * l
                act.wait_ge(s_rt, 2 * l + 1)
                gd = S2[:, rt0 + 16 + 128 + 4:rt0 + 16 + 128 + 4 + 16]
                act.activation(gd, gd, ACT.Exp).then_inc(s_re, 1)
                act.wait_ge(s_rt, 2 * l + 2)
                e2 = S2[:, e2_at:e2_at + 4]
                act.activation(e2, e2, ACT.Exp).then_inc(s_re, 1)

                def y0(e, par, n):
                    act.wait_ge(s_hta, B + e)
                    act.wait_ge(s_down, B + e)
                    if not (isinstance(n, int) and n == 0 and l == 0):
                        act.wait_ge(s_yw[par], 16 * (16 * l + n))
                    out0(par).then_inc(s_y0, 1)

                def hidden(e, par):
                    act.wait_ge(s_ht, B + e)
                    if not (isinstance(e, int) and e <= 2):
                        act.wait_ge(s_down, B + e - 2)
                    hidden_copy(par).then_inc(s_hta, 1)

                def load_rows(e, par):
                    act.dma_start(rows[par], xp[bass.ds(TB * e, TB), :]).then_inc(s_rows[par], 16)

                def store(e, par):
                    act.wait_ge(s_y0, B + e)
                    act.wait_ge(s_y1, B + e)
                    act.dma_start(yp[bass.ds(TB * (e - 1), TB), :], yrow[par]).then_inc(s_yw[par], 16)

                act.wait_ge(s_disp, 16 * 2 * NT * (l + 1))
                load_rows(0, 0)
                load_rows(1, 1)

                def step(e, par, n, first=False, last=False):
                    act.wait_ge(s_gate, B + e + 1)
                    if not (isinstance(e, int) and e <= 1):
                        act.wait_ge(s_h1, B + e - 1)
                    tanh_half(par).then_inc(s_th, 1)
                    if not last and not (isinstance(e, int) and e == EXPERTS - 2):
                        load_rows(e + 2, par)
                    if not first:
                        hidden(e, 1 - par)
                        y0(e, 1 - par, n if par == 1 else n - 1)
                        store(e, 1 - par)

                step(0, 0, 0, first=True)
                step(1, 1, 0)
                step(2, 0, 1)
                with act.Fori(1, EXPERTS // 2 - 2) as i:
                    step(2 * i + 1, 1, i)
                    step(2 * i + 2, 0, i + 1)
                step(EXPERTS - 3, 1, EXPERTS // 2 - 2)
                step(EXPERTS - 2, 0, EXPERTS // 2 - 1)
                step(EXPERTS - 1, 1, EXPERTS // 2 - 1, last=True)
                hidden(EXPERTS, 1)
                y0(EXPERTS, 1, EXPERTS // 2 - 1)
                store(EXPERTS, 1)
                v = s_ov[l]
                act.wait_ge(s_down, B + EXPERTS)
                act.wait_ge(s_y0, B + EXPERTS)
                act.wait_ge(s_yw[0], 16 * 16 * (l + 1))
                n = act.value_load(extra_tab[0:1, 0:1], min_val=0, max_val=EXTRA)
                with act.If(n > 0):
                    with act.Fori(0, n) as b:
                        e = act.value_load(extra_tab[0:1, bass.ds(b + 1, 1)], min_val=0, max_val=EXPERTS - 1)
                        act.dma_start(slot_w(3), a["moe_w_gate"][l, bass.ds(e, 1)].rearrange("o (p c) n -> (o p) c n", c=NC)).then_inc(v["w"], 16)
                        act.dma_start(slot_w(4), a["moe_w_up"][l, bass.ds(e, 1)].rearrange("o (p c) n -> (o p) c n", c=NC)).then_inc(v["w"], 16)
                        act.dma_start(slot_w(5, 4), a["moe_w_down"][l, bass.ds(e, 1)].rearrange("o (p c) n -> (o p) c n", c=4)).then_inc(v["w"], 16)
                        act.dma_start(rows[0], xp[bass.ds(TB * b + MAIN_SLOTS, TB), :]).then_inc(v["rows"], 16)
                        wait_extra(act, l, "up", b)
                        tanh_half(0).then_inc(v["act"], 1)
                        wait_extra(act, l, "ht", b)
                        hidden_copy(0).then_inc(v["act"], 1)
                        wait_extra(act, l, "down", b)
                        out0(0).then_inc(v["act"], 1)
                        wait_extra(act, l, "y0", b)
                        wait_extra(act, l, "y1", b)
                        act.dma_start(yp[bass.ds(TB * b + MAIN_SLOTS, TB), :], yrow[0]).then_inc(v["written"], 16)
                        act.wait_ge(v["written"], 16 * b + 16)
                if l == 0 and stop > 3:
                    router_weights(1)

            def mixer_c():
                for m in range(16):
                    act.wait_ge(s_qm, m + 1)
                    if m >= 2:
                        act.wait_ge(s_qv, m - 1)
                    act.activation(raw[m % 2], bank(4 + m % 4), ACT.Copy).then_inc(s_qa, 1)
                for n in range(2 * NT):
                    half, i = n // NT, n % NT
                    act.wait_ge(s_vm, n + 1)
                    act.activation(v_att[:, i, 512 * half:512 * half + 512], bank(4 + i), ACT.Copy).then_inc(s_va, 1)
                act.wait_ge(s_lamm, 1)
                act.activation(cols["lam"][:, 2:4], bank(4)[:, 0:2], ACT.Exp).then_inc(s_lam, 1)

                def exps(k):
                    w = P * (k % NT + 1)
                    st = stat[:, k % 2, :]
                    act.wait_ge(s_mx, k + 1)
                    for c in range(2):
                        act.activation(pe_[k % 2][:, c, 0:w], bank(2 * (k % 2) + c)[:, 0:w], ACT.Exp, scale=SCALE, bias=st[:, 2 + c:3 + c],
                                       accum_out=st[:, 4 + c:5 + c]).then_inc(s_ex, 1)

                def evac(k):
                    h, b = k // NT, k % NT
                    w = P * (b + 1)
                    act.wait_ge(s_pt, k + 1)
                    if k >= 2:
                        act.wait_ge(s_pta, k - 1)
                    act.activation(probT[k % 2][:, 0:w], bank(4 + k % 2)[:, 0:w], ACT.Copy).then_inc(s_pta, 1)
                    if b == NT - 1:
                        act.wait_ge(s_ov_, h + 1)
                        act.activation(oT[:, h, :], bank(6 + h % 2), ACT.Copy).then_inc(s_oc, 1)

                for k in range(H * NT):
                    exps(k)
                    if k >= 1:
                        evac(k - 1)
                evac(H * NT - 1)
                for h in range(H):
                    if h >= 2:
                        act.wait_ge(s_on, h - 1)
                    act.wait_ge(s_oc, h + 1)
                    act.activation(osq[h % 2], oT[:, h, :], ACT.Square, scale=128 ** -0.5).then_inc(s_osq, 1)
                    act.wait_ge(s_osm, h + 1)
                    act.activation(osq[h % 2], bank(h % 2), ACT.Sqrt, bias=cols["sub_eps"]).then_inc(s_ort, 1)

            if stop > 1:
                norm(1)
                experts(0)
            if stop > 2:
                norm(2)
                mixer_c()
            if stop > 3:
                norm(3)
                experts(1)
            if stop > 4:
                norm(4)

        @block.gpsimd
        def _(pool):
            own = Steps(pool, s_pool)

            def rstd(n):
                if n == 0:
                    pool.wait_ge(s_cst, 16)
                pool.wait_ge(s_ss, 4 * n + 4)
                if n >= 1 and n < 4:
                    pool.wait_ge(s_hn, 4 * n)
                own.next(pool.tensor_scalar(cols["ms"], cols["ss"], 1.0 / D, RMS_EPS, ALU.mult, ALU.add))
                own.next(pool.tensor_tensor(cols["rstd"], cols["ms"], K("minus_half"), ALU.pow))
                pool.nop().then_inc(s_rstd, 1)

            rstd(0)
            pool.wait_ge(s_zero, 1)
            pool.wait_ge(s_full[1], 16)
            zr = xp.rearrange("(p r) d -> p (r d)", p=TB)
            for k in range(SLOTS // TB // 2):
                pool.dma_start(zr[:, 2 * D * k:2 * D * k + 2 * D], zeros[0:TB, :]).then_inc(s_zrows, 16)
            ze = yp[MAIN_SLOTS:SLOTS, :].rearrange("(p r) d -> p (r d)", p=TB)
            for k in range(EXTRA // 2):
                pool.dma_start(ze[:, 2 * D * k:2 * D * k + 2 * D], zeros[0:TB, :]).then_inc(s_zrows, 16)
            for g in range(4):
                pool.wait_ge(s_u, g + 1)
                src = upad[0]
                for k in range(g + 1):
                    dst = upad[1 + k % 2]
                    own.next(pool.tensor_tensor(dst[:, PAD:PAD + T], src[:, PAD:PAD + T], src[:, PAD - 2 ** k:PAD + T - 2 ** k], ALU.add))
                    src = dst
                own.next(pool.tensor_tensor(src[:, PAD:2 * PAD], src[:, PAD:2 * PAD], K("short_window")[:, 16 * g:16 * g + 16], ALU.mult))
                pool.nop().then_inc(s_win, 1)
            pool.wait_ge(s_prep, 4)
            pool.wait_ge(s_hsum, 5)
            for j in range(NPAIR):
                own.mark(pool.tensor_tensor(kT[:, j, :], kT[:, j, :], piT[:, j, :], ALU.mult))
                own.next(pool.tensor_tensor(rT[:, j, :], rT[:, j, :], pT[:, j, :], ALU.mult))
                pool.nop().then_inc(s_prepp, 1)

            def local(pr):
                for lv, m in enumerate(LEVELS):
                    for b in range(2):
                        q, w, n = 2 * pr + b, wk[b], 2 * NL * pr + 2 * lv + b
                        pool.wait_ge(s_gv, 5 * q + 1)
                        if lv >= 1:
                            pool.wait_ge(s_jx, n - 1)
                        pool.tensor_tensor(heads(w["Bm"]), heads(w["LT"]), per_head(K(f"join{m}")), ALU.mult).then_inc(s_jb, 1)

            local(0)
            local(1)

            def experts(l):
                B = 16 * l
                pool.wait_ge(s_slot, 4 * l + 4)
                pool.wait_ge(s_hn, 4 * (1 + 2 * l) + 4)
                for k in range(2):
                    for i in range(NT):
                        pool.indirect_dma_start(out=xp, out_offset=bass.IndirectOffsetOnAxis(ap=slot_ix[:, k, i:i + 1], axis=0),
                                                in_=hn[:, i, :], in_offset=None).then_inc(s_disp, 16)
                for par in range(2):
                    pool.wait_ge(s_yw[par], 16 * 16 * (l + 1))
                pool.wait_ge(s_xt, EXPERTS * (l + 1))
                v = s_ov[l]
                n = pool.value_load(extra_tab[0:1, 0:1], min_val=0, max_val=EXTRA)
                with pool.If(n > 0):
                    with pool.Fori(0, n) as b:
                        pool.wait_ge(v["written"], 16 * b + 16)
                for i in range(NT):
                    for k in range(2):
                        pool.indirect_dma_start(out=got[k][i], out_offset=None, in_=yp,
                                                in_offset=bass.IndirectOffsetOnAxis(ap=slot_ix[:, k, i:i + 1], axis=0)).then_inc(s_got[i], 16)

            if stop > 1:
                rstd(1)
                experts(0)
            if stop > 2:
                rstd(2)
            if stop > 3:
                rstd(3)
                experts(1)
            if stop > 4:
                rstd(4)


_INS = ["x", "norm_mix", "norm_ffn", "final_norm", "a_w_in", "a_mu", "a_w0", "a_w2", "a_a0", "a_a2", "a_g2",
        "a_k_k", "a_k_a", "a_r_k", "a_ln_w", "a_ln_b", "b_w_pool", "b_pool_scale", "ab_w_out",
        "c_w_qkv", "c_lambda_q1", "c_lambda_k1", "c_lambda_q2", "c_lambda_k2", "c_subln", "c_w_out",
        "moe_w_group", "moe_b_group", "moe_w_expert", "moe_b_expert", "moe_w_gate", "moe_w_up", "moe_w_down"]


def kernel(**inputs):
    import numpy as _np
    import concourse.bacc as _bacc
    from concourse import mybir as _mybir
    from concourse.bass_utils import run_bass_kernel_spmd as _run

    nc = _bacc.Bacc("TRN2", target_bir_lowering=False, num_devices=1)
    arrays, args = {}, {}
    for name in _INS:
        arr = _np.ascontiguousarray(inputs[name])
        arrays[f"in_{name}"] = arr
        args[name] = nc.dram_tensor(f"in_{name}", arr.shape, _mybir.dt.from_np(arr.dtype), kind="ExternalInput").ap()
    tables = {"constants": constant_table()[1], "rope": rope_table()}
    aps = {}
    for name, arr in tables.items():
        arrays[name] = arr
        aps[name] = nc.dram_tensor(name, arr.shape, _mybir.dt.from_np(arr.dtype), kind="ExternalInput").ap()
    out = nc.dram_tensor("out", (1, T, D), _mybir.dt.float32, kind="ExternalOutput").ap()
    build(nc, args, aps["constants"], aps["rope"], out)
    r = _run(nc, [arrays], core_ids=[0])
    return r.results[0]["out"]
```

```python
from contextlib import ExitStack
import math

import numpy as np

import concourse.bass as bass
from concourse import mybir

F32 = mybir.dt.float32
F32R = mybir.dt.float32r
BF16 = mybir.dt.bfloat16
I32 = mybir.dt.int32
ALU = mybir.AluOpType
ACT = mybir.ActivationFunctionType
AX = mybir.AxisListType.X

P = 128
T = 512
D = 1024
NT = T // P
NC = D // P
H = 8
N = 64
C = 64
NCH = T // C
NPAIR = H // 2
GN_EPS = 64e-5
RMS_EPS = 1e-6
SUBLN_EPS = 1e-5
WINDOWS = (2, 4, 8, 16)
EXPERTS = 32
GROUPS = 4
PER_GROUP = 8
FF = 512
TB = 80
EXTRA = (2 * T - 1) // TB
MAIN_SLOTS = EXPERTS * TB
SLOTS = MAIN_SLOTS + EXTRA * TB
LAMBDA_INIT = 0.8 - 0.6 * math.exp(-0.3)
ROPE_DIMS = 16
ROPE_THETA = 500000.0
SCALE = 64 ** -0.5
BIG = 1e30
ROUTER_E2 = 732
UNIT = 4096
SLAB = 2048


def constant_table():
    p = np.arange(P)
    f = np.arange(P)
    blocks = {}
    blocks["ident"] = np.eye(P)
    blocks["earlier"] = (p[:, None] < f[None, :])
    blocks["ones"] = np.ones((P, P))
    blocks["head_mean"] = (p[:, None] // N == f[None, :] // N) / N
    sel = np.zeros((P, NPAIR, H))
    for j in range(NPAIR):
        sel[p, j, 2 * j + p // N] = 1
    blocks["head_sel"] = sel.reshape(P, -1)
    spread = np.zeros((P, NPAIR, P))
    for j in range(NPAIR):
        spread[2 * j + p // N, j, p] = 1
    blocks["head_spread"] = spread.reshape(P, -1)
    r, c = (p % C)[:, None], np.arange(C)[None, :]
    blocks["eye64"] = (r == c)
    blocks["low1"] = -((r // 2 == c // 2) & (r > c)).astype(float)
    blocks["up1"] = -((r // 2 == c // 2) & (r < c)).astype(float)
    for m in (2, 4, 8, 16, 32):
        blocks[f"join{m}"] = (r // (2 * m) == c // (2 * m)) & (r % (2 * m) < m) & (c % (2 * m) >= m)
    blocks["strict"] = (r < c)
    blocks["upto"] = (r <= c)
    win = np.ones((P, 4, 16))
    for g, w in enumerate(WINDOWS):
        t = np.arange(16)
        win[:, g] = w / np.minimum(t + 1, w)
    blocks["short_window"] = win.reshape(P, -1)
    blocks["iota4"] = np.tile(np.arange(4), (P, 1))
    blocks["iota32"] = np.tile(np.arange(32), (P, 1))
    blocks["iota_extra"] = np.tile(np.arange(EXTRA), (P, 1))
    blocks["first_slot"] = np.tile(TB * np.arange(EXPERTS), (P, 1))
    one_col = np.zeros((P, 2 * H - 1))
    one_col[:, H - 1] = 1
    blocks["one_col"] = one_col
    blocks["minus_half"] = np.full((P, 4), -0.5)
    at, n = {}, 0
    for k, v in blocks.items():
        at[k] = (n, n + v.shape[1])
        n += v.shape[1]
    return at, np.concatenate([np.asarray(v, np.float32) for v in blocks.values()], axis=1)


def rope_table():
    inv = ROPE_THETA ** (-np.arange(0, ROPE_DIMS, 2, dtype=np.float32) / ROPE_DIMS)
    ang = np.arange(T, dtype=np.float32)[:, None] * inv.astype(np.float32)[None, :]
    cos, sin = np.ones((P, T)), np.zeros((P, T))
    swap = np.zeros((P, P))
    half = ROPE_DIMS // 2
    for base in (0, 64):
        for i in range(half):
            a, b = base + i, base + half + i
            cos[a] = cos[b] = np.cos(ang[:, i])
            sin[a] = sin[b] = np.sin(ang[:, i])
            swap[b, a] = -1
            swap[a, b] = 1
    q, k = np.arange(P)[:, None], np.arange(P)[None, :]
    mask = np.where(k <= q, 0.0, -BIG)
    return np.concatenate([cos, sin, swap, mask], axis=1).astype(np.float32)


class Steps:

    def __init__(self, eng, sem):
        self.eng, self.sem, self.n = eng, sem, 0

    def mark(self, ins):
        self.n += 1
        ins.then_inc(self.sem, 1)

    def hold(self):
        self.eng.wait_ge(self.sem, self.n)

    def next(self, ins):
        self.mark(ins)
        self.hold()


def build(nc, a, consts, ropes, out, stop=99, dbg=None):
    at, _ = constant_table()
    xp = nc.dram_tensor("expert_rows", [SLOTS, D], F32, kind="Internal").ap()
    yp = nc.dram_tensor("expert_out", [SLOTS, D], F32, kind="Internal").ap()
    ctx = ExitStack()
    with ctx:
        def sb(name, shape, dt=F32):
            return ctx.enter_context(nc.sbuf_tensor(name, shape, dt))

        def sem(name):
            return ctx.enter_context(nc.semaphore(name))

        x_sb = sb("x_sb", [P, NT, D])
        ring = sb("ring", [P, 2, UNIT])

        def twice(name, n):
            with nc.sbuf_tensor(name + "_r", [P, n], F32R) as r:
                pass
            return sb(name, [P, n]), r

        S1, S1r = twice("shared_scratch", 3 * UNIT)
        S4, S4r = twice("third_slot", UNIT)
        S2, S2r = twice("scratch", 9 * SLAB)
        S3, S3r = twice("small_scratch", 5 * 512)
        cst = sb("cst", [P, consts.shape[1]])
        lora_w = S3[:, 0:512]
        gate_w2 = S3[:, 512:1024]
        wpool = S3[:, 1024:1536].rearrange("p (g n) -> p g n", g=4)
        gateT_in = S3[:, 1536:2048]
        u_neg = S3[:, 2048:2560]
        vec = sb("vec", [P, 160])
        rowv = sb("rowv", [1, 2 * 36])
        small = sb("small", [P, 64])

        bank_pair = [ctx.enter_context(nc.psum_tensor(f"bank_pair{i}", [P, 2, 512], F32)) for i in range(4)]
        bank67 = bank_pair[3]

        def bank(i):
            return bank_pair[i // 2][:, i % 2, :]

        def K(name, rows=P):
            return cst[0:rows, at[name][0]:at[name][1]]

        ident = K("ident")

        def slab(n, cols=SLAB):
            if n < 9:
                return S2[:, n * SLAB:n * SLAB + cols]
            if n < 16:
                return S1[:, (n - 10) * SLAB:(n - 10) * SLAB + cols]
            return S4[:, (n - 16) * SLAB:(n - 16) * SLAB + cols]

        def slot(s):
            return ring[:, s, :] if s < 2 else S4[:, :] if s == 2 else S1[:, (s - 3) * UNIT:(s - 2) * UNIT]

        hnT = S2[:, 0:UNIT].rearrange("p (c t) -> p c t", c=NC)
        hn = S2[:, UNIT:2 * UNIT].rearrange("p (i d) -> p i d", i=NT)

        cols = {}
        used = [0]

        def column(name, n):
            cols[name] = vec[:, used[0]:used[0] + n]
            used[0] += n

        for nm, n in (("g_mix0", 8), ("g_mix1", 8), ("mu", 14), ("w0", 4), ("a0", 4),
                      ("k_k", 4), ("k_a", 4), ("r_k", 4), ("ln_w", 4), ("ln_b", 4), ("pool_scale", 4), ("subln", 1),
                      ("lq", 4), ("one_minus_mu", 14), ("half_w0", 4), ("half_a0", 4), ("lam", 6), ("subln_s", 1),
                      ("ss", 4), ("ms", 4), ("rstd", 4), ("half_decay", 1), ("sub_eps", 1)):
            column(nm, n)
        vec_loads = [
            (cols["g_mix0"], a["norm_mix"][0].rearrange("(p c) -> p c", c=8)),
            (cols["g_mix1"], a["norm_mix"][1].rearrange("(p c) -> p c", c=8)),
            (cols["mu"], a["a_mu"][0].rearrange("(c p) -> p c", p=P)),
            (cols["w0"], a["a_w0"][0].rearrange("(c p) -> p c", p=P)),
            (cols["a0"], a["a_a0"][0].rearrange("(c p) -> p c", p=P)),
            (cols["k_k"], a["a_k_k"][0].rearrange("(c p) -> p c", p=P)),
            (cols["k_a"], a["a_k_a"][0].rearrange("(c p) -> p c", p=P)),
            (cols["r_k"], a["a_r_k"][0].rearrange("(c h) n -> (h n) c", h=2)),
            (cols["ln_w"], a["a_ln_w"][0].rearrange("(c p) -> p c", p=P)),
            (cols["ln_b"], a["a_ln_b"][0].rearrange("(c p) -> p c", p=P)),
            (cols["pool_scale"], a["b_pool_scale"][0].rearrange("(c p) -> p c", p=P)),
            (cols["subln"], a["c_subln"].rearrange("o p -> p o")),
            (cols["lq"][0:64, 0:1], a["c_lambda_q1"].rearrange("o p -> p o")),
            (cols["lq"][0:64, 1:2], a["c_lambda_k1"].rearrange("o p -> p o")),
            (cols["lq"][0:64, 2:3], a["c_lambda_q2"].rearrange("o p -> p o")),
            (cols["lq"][0:64, 3:4], a["c_lambda_k2"].rearrange("o p -> p o")),
            (lora_w[0:64, :], a["a_w2"][0]),
            (lora_w[64:128, :], a["a_a2"][0]),
            (gate_w2[:, :], a["a_g2"][0]),
            (rowv[0:1, 0:4], a["moe_b_group"][0:1]),
            (rowv[0:1, 4:36], a["moe_b_expert"][0:1]),
            (rowv[0:1, 36:40], a["moe_b_group"][1:2]),
            (rowv[0:1, 40:72], a["moe_b_expert"][1:2]),
            (wpool[:, :, :], a["b_w_pool"][0].rearrange("g c d -> c g d")),
        ]

        s_x = sem("x_loaded")
        s_cst = sem("constants_loaded")
        s_vec = sem("vectors_loaded")
        s_zero = sem("zeros_made")
        s_zrows = sem("rows_zeroed")
        s_full = [sem(f"slot_full{i}") for i in range(6)]
        s_dve = sem("vector_order")
        s_act = sem("scalar_order")
        s_pool = sem("pool_order")
        s_ss = sem("square_sums")
        s_rstd = sem("rstd_made")
        s_hn = sem("rows_normed")
        s_tr = sem("norm_transposed")
        s_trv = sem("norm_evac_vector")
        s_tra = sem("norm_evac_scalar")
        s_proj = sem("proj_done")
        s_sh = sem("shift_part_made")
        s_z = sem("shifted_made")
        s_tanh = sem("lora_inner_made")
        s_lora = sem("lora_mm")
        s_wdec = sem("decay_made")
        s_am = sem("iclr_tanh_made")
        s_sq = sem("k_squares_made")
        s_hsum = sem("head_sums")
        s_hroot = sem("head_roots")
        s_hinv = sem("head_inverse")
        s_hb = sem("head_spread_mm")
        s_kk = sem("kk_made")
        s_rkp = sem("rk_products")
        s_rs = sem("bonus_sum_copied")
        s_bon = sem("bonus_made")
        s_prep = sem("prep_made")
        s_prepp = sem("prep_pool_made")
        s_u = sem("pool_input_copied")
        s_win = sem("window_sums")
        s_pd = sem("pool_diff")
        s_pmm = sem("pool_mm")
        s_yb = sem("pool_out")
        s_pw = sem("pool_weights_loaded")
        s_tt = sem("token_transposed")
        s_tev = sem("token_evac_vector")
        s_tea = sem("token_evac_scalar")
        s_gm = sem("gram_mm")
        s_gv = sem("gram_masked")
        s_jb = sem("join_blocks")
        s_jx = sem("join_x_mm")
        s_jxa = sem("join_x_copied")
        s_jt = sem("join_t_mm")
        s_jtv = sem("join_t_updated")
        s_lx = sem("ak_v_mm")
        s_lxa = sem("ak_v_copied")
        s_lw = sem("w_mm")
        s_lwa = sem("w_copied")
        s_lu = sem("uv_mm")
        s_luv = sem("uv_copied")
        s_um = sem("u_mm")
        s_ua = sem("u_made")
        s_y0m = sem("y_state_part_mm")
        s_sm = sem("state_mm")
        s_sv = sem("state_made")
        s_ym = sem("y_mm")
        s_ya = sem("y_copied")
        s_gn = sem("gn_mm")
        s_gnv = sem("gn_vector")
        s_gna = sem("gn_scalar")
        s_g = sem("gate_made")
        s_gmm = sem("gate_out_mm")
        s_yav = sem("ya_made")
        s_om = sem("out_mm")
        s_res = sem("residual_added")
        s_rw = sem("router_weights")
        s_lg = sem("logits_mm")
        s_rt = sem("router_vector")
        s_re = sem("router_exp")
        s_oh = sem("choices_made")
        s_rk = sem("ranks_mm")
        s_slot = sem("slots_made")
        s_disp = sem("rows_dispatched")
        s_rows = [sem(f"rows_loaded{i}") for i in range(2)]
        s_xt = sem("block_transposed")
        s_xr = sem("block_rounded")
        s_xl = sem("block_rest")
        s_wr = sem("weights_rounded")
        s_wl = sem("weights_rest_vector")
        s_wlp = sem("weights_rest_pool")
        s_wu = sem("split_weights_used")
        s_gate = sem("gate_mm")
        s_th = sem("gate_tanh")
        s_h1 = sem("gate_used")
        s_up = sem("up_mm")
        s_h = sem("hidden_made")
        s_ht = sem("hidden_transposed")
        s_hr = sem("hidden_rounded")
        s_hl = sem("hidden_rest")
        s_down = sem("down_mm")
        s_y0 = sem("expert_out_scalar")
        s_y1 = sem("expert_out_vector")
        s_yw = [sem(f"expert_out_written{i}") for i in range(2)]
        s_ov = [{k: sem(f"extra{l}_{k}") for k in ("w", "rows", "pe", "dve", "act", "written")} for l in range(2)]
        EXTRA_MARKS = {"xt": ("pe", 4, 1), "up": ("pe", 4, 2), "ht": ("pe", 4, 3), "down": ("pe", 4, 4),
                       "xl": ("dve", 5, 1), "h1": ("dve", 5, 2), "h": ("dve", 5, 3), "hl": ("dve", 5, 4), "y1": ("dve", 5, 5),
                       "xr": ("act", 4, 1), "th": ("act", 4, 2), "hr": ("act", 4, 3), "y0": ("act", 4, 4)}

        def wait_extra(eng, l, what, b):
            name, per, at_ = EXTRA_MARKS[what]
            eng.wait_ge(s_ov[l][name], b * per + at_)

        s_got = [sem(f"expert_out_gathered{i}") for i in range(NT)]
        s_comb = sem("combined")
        s_rope = sem("rope_loaded")
        s_lam = sem("lambda_steps")
        s_lamm_in = sem("lambda_products")
        s_lamm = sem("lambda_mm")
        s_qm = sem("qk_mm")
        s_qa = sem("qk_copied")
        s_rm = sem("rot_mm")
        s_qv = sem("qk_roped")
        s_vm = sem("v_mm")
        s_va = sem("v_copied")
        s_cr = sem("chunk_rounded")
        s_cl = sem("chunk_rest")
        s_cu = sem("chunk_used")
        s_or = sem("o_rounded")
        s_ol = sem("o_rest")
        s_mk = sem("mask_cast")
        s_sc = sem("scores_mm")
        s_mx = sem("scores_max")
        s_ex = sem("scores_exp")
        s_pr = sem("probs_made")
        s_pt = sem("probs_transposed")
        s_pta = sem("probs_evac")
        s_ov_ = sem("values_mm")
        s_oc = sem("values_copied")
        s_osq = sem("o_squares")
        s_osm = sem("o_mean_mm")
        s_ort = sem("o_root")
        s_oi = sem("o_inverse")
        s_on = sem("o_normed")
        s_fnb = sem("final_weight_mm")
        s_fin = sem("final_rows")
        s_out = sem("stored")

        n_vec = 16 * len(vec_loads)
        n_zero = SLOTS // TB // 2 + EXTRA // 2

        A_SLOTS = [0, 1, 0, 1, 0, 1, 0]
        C_SLOTS = [0, 1, 0, 1, 0, 1, 0, 1]
        before = {"A": [0] * 6}
        before["moe0"] = [A_SLOTS.count(s) for s in range(6)]
        before["C"] = [n + EXPERTS // 2 for n in before["moe0"]]
        before["moe1"] = [n + C_SLOTS.count(s) for s, n in enumerate(before["C"])]

        def use(phase, slots, u):
            return before[phase][slots[u]] + slots[:u + 1].count(slots[u])

        wA = a["a_w_in"][0].rearrange("(p c) n -> p c n", c=NC)
        A_COLS = [(1536, 1792), (512, 1024), (0, 512), (1024, 1536), (1792, 2304)]
        A_SRC = [wA[:, :, lo:hi] for lo, hi in A_COLS]
        woA = a["ab_w_out"][0].rearrange("(c p) n -> p c n", p=P)
        A_SRC += [woA[:, :, 0:512], woA[:, :, 512:1024]]
        wC = a["c_w_qkv"][0].rearrange("(p c) n -> p c n", c=NC)
        woC = a["c_w_out"][0].rearrange("(c p) n -> p c n", p=P)
        C_SRC = [wC[:, :, 512 * u:512 * u + 512] for u in range(6)] + [woC[:, :, 0:512], woC[:, :, 512:1024]]

        def slot_w(s, c=NC):
            return slot(s).rearrange("p (c n) -> p c n", c=c)

        def pairs(n):
            return slab(n).rearrange("p (j t) -> p j t", j=NPAIR)

        kT, rT, vT, ybT = pairs(4), pairs(5), pairs(6), pairs(7)
        wT, pT, aT, kkT, alT = pairs(16), pairs(17), pairs(10), pairs(11), pairs(12)
        bonT, piT = pairs(13), pairs(14)
        rk_tmp = pairs(8)
        zeros = slab(13)
        v_tok, al_tok, k_tok, b_tok = pairs(0), pairs(1), pairs(14), pairs(11)
        shift = [slab(2)[:, 520 * i:520 * i + T + 1] for i in range(2)]
        z_l0 = slab(2)[:, 1040:1040 + T]
        PAD = 16
        upad = [slab(3)[:, 528 * i:528 * i + PAD + T] for i in range(3)]
        sq_tmp = [slab(15)[:, T * i:T * i + T] for i in range(2)]
        scan_in = slab(15)[:, 1024:1024 + T]
        hs = slab(15)[0:H, 1536:1536 + T]
        wk = [{}, {}]
        for q in range(2):
            for n, name in enumerate(("Tm", "TT", "X", "LT", "Bm", "AK")):
                k = q * 6 + n
                wk[q][name] = slab((2, 3, 15)[k // 4])[:, (k % 4) * 512:(k % 4) * 512 + 512]
        keep = [{name: slab(n)[:, k * 512:k * 512 + 512] for k, name in enumerate(("RK", "RB", "UV", "WT"))}
                for n in (8, 16, 17, 8)]
        yT = vT
        yc_sq = slab(16)
        ST = [sb(f"state{i}", [P, NPAIR, N]) for i in range(2)]
        STs = sb("state_sum", [P, NPAIR, N])
        pc = sb("chunk_decay", [P, NPAIR, NCH])

        def heads(ap):
            if len(ap.shape) == 3:
                return ap.rearrange("p a (j n) -> p a j n", j=NPAIR)
            return ap.rearrange("p (a j n) -> p a j n", a=2, j=NPAIR)

        def per_head(ap):
            return ap.unsqueeze(1).unsqueeze(1).to_broadcast([P, 2, NPAIR, C])

        def gram_place(q, k):
            n = 3 * (q % 2) + k // 2
            return bank_pair[3 - n % 4], 256 * (k % 2)

        def both(ap):
            return ap.rearrange("p (a m) -> p a m", a=2)

        o = 2 * UNIT
        rows = [S2[0:TB, o + D * i:o + D * i + D] for i in range(2)]
        o += 2 * D
        x_at = o
        o += 4 * NC * TB
        hid = [S2[0:TB, o + FF * i:o + FF * i + FF] for i in range(2)]
        tab_at = o
        o += 2 * FF
        yrow = [S2[0:TB, o + D * i:o + D * i + D] for i in range(2)]
        rt0 = o
        o += 2 * D
        rw_at = 9 * SLAB - 1280 - NC * 36
        w_router = S2[:, rw_at:rw_at + NC * 36].rearrange("p (c n) -> p c n", c=NC)
        assert o <= rw_at

        def split_views(buf, start, c):
            return [[buf[:, start + c * TB * (2 * i + k):start + c * TB * (2 * i + k + 1)].rearrange("p (c t) -> p c t", c=c) for i in range(2)]
                    for k in range(2)]

        xR, xL = split_views(S2r, x_at, NC)
        xR32, xL32 = split_views(S2, x_at, NC)
        hR, hL = split_views(S3r, 0, 4)
        hR32, hL32 = split_views(S3, 0, 4)
        th = [S3[0:TB, 16 * TB + FF * i:16 * TB + FF * i + FF] for i in range(2)]
        g_row = S3[:, 16 * TB:16 * TB + D]
        assert 16 * TB + D <= 5 * 512
        GROUP = UNIT // 4
        wR = [S2r[:, 2 * GROUP * j:2 * GROUP * j + GROUP] for j in range(4)]
        wL = [S2r[:, 2 * GROUP * j + GROUP:2 * GROUP * j + 2 * GROUP] for j in range(4)]
        BATCHES = 3 * EXPERTS

        def q_gate(e):
            return 0 if isinstance(e, int) and e == 0 else 3 * e - 1

        def q_up(e):
            return 1 if isinstance(e, int) and e == 0 else 3 * e

        def q_down(e):
            return BATCHES - 1 if isinstance(e, int) and e == EXPERTS - 1 else 3 * e + 4

        got = [[S2[:, k * UNIT + D * i:k * UNIT + D * i + D] for i in range(NT)] for k in range(2)]
        e2_at = rt0 + ROUTER_E2
        slot_ix = sb("slot_ix", [P, 2, NT], I32)
        extra_tab = sb("extra_tab", [1, 1 + EXTRA], I32)
        wts = sb("wts", [P, 2, NT])

        rope_sb = S2[:, 9 * SLAB - 1280:9 * SLAB]
        cosT, sinT = rope_sb[:, 0:T], rope_sb[:, T:2 * T]
        swap, mask = rope_sb[:, 2 * T:2 * T + P], rope_sb[:, 2 * T + P:2 * T + 2 * P]
        v_att = hn
        kaT = S2[:, 3 * UNIT:4 * UNIT].rearrange("p (h t) -> p h t", h=H)
        q_half = [S2[:, 2 * UNIT:3 * UNIT].rearrange("p (h t) -> p h t", h=H), S1[:, UNIT:2 * UNIT].rearrange("p (h t) -> p h t", h=H)]
        oT = S1[:, 0:UNIT].rearrange("p (h t) -> p h t", h=H)
        o = 2 * UNIT
        raw = [S1[:, o + T * i:o + T * i + T] for i in range(4)]
        rot = [S1[:, o + 2048 + T * i:o + 2048 + T * i + T] for i in range(4)]
        pe_ = [S1[:, o + 1024 * i:o + 1024 * i + 1024].rearrange("p (c k) -> p c k", c=2) for i in range(2)]
        prob = [S1[:, o + 2048 + T * i:o + 2048 + T * i + T] for i in range(2)]
        probT = [S1[:, o + 3072 + T * i:o + 3072 + T * i + T] for i in range(2)]
        osq = S2[:, 0:UNIT].rearrange("p (h t) -> p h t", h=H)
        hnR, hnL = (b[:, 0:UNIT].rearrange("p (c t) -> p c t", c=NC) for b in (S2r, S1r))
        oR, oL = (S2r[:, k * UNIT:(k + 1) * UNIT].rearrange("p (c t) -> p c t", c=NC) for k in (2, 3))
        cR = [S4r[:, 1024 * i:1024 * i + 512] for i in range(4)]
        cL = [S4r[:, 1024 * i + 512:1024 * i + 1024] for i in range(4)]
        o_inv = prob[0][0:H, :]
        mask16 = sb("mask16", [P, 2 * P], BF16)
        stat = sb("stat", [P, 2, 8])
        fn_row = S2[0:1, 2 * UNIT:2 * UNIT + D]
        fin = [S2[:, k * D:k * D + D] for k in range(NT)]

        block = ctx.enter_context(nc.Block())

        TILES = [(0, 0, 12), (0, 128, 13)] + [(1, 128 * j, 4 + j) for j in range(4)] \
            + [(2, 128 * j, j) for j in range(4)] + [(3, 128 * j, 8 + j) for j in range(4)] \
            + [(4, 128 * j, None) for j in range(4)]
        Z_OUT = [z_l0, gateT_in[:, :]] + [kT[:, j, :] for j in range(4)] + [rT[:, j, :] for j in range(4)] \
            + [vT[:, j, :] for j in range(4)]
        LEVELS = (2, 4, 8, 16, 32)
        n_setup = 14
        NL = len(LEVELS)

        def evac_before(n):
            return 4 * n + (4 if n > 2 else 0)

        def moe_before(l, s):
            return before[f"moe{l}"][s]

        def experts_sp(sp, l):
            if stop <= 1 + 2 * l:
                return

            def load_one(e, half, n, k):
                srcs = [a["moe_w_gate"][l, bass.ds(e, 1)].rearrange("o (p c) n -> (o p) c n", c=NC),
                        a["moe_w_up"][l, bass.ds(e, 1)].rearrange("o (p c) n -> (o p) c n", c=NC),
                        a["moe_w_down"][l, bass.ds(e, 1)].rearrange("o (p c) n -> (o p) c n", c=4)]
                s = 3 * half + k
                if not (isinstance(n, int) and n == 0):
                    q = (q_gate, q_up, q_down)[k]
                    sp.wait_ge(s_wl, 3 * (BATCHES * l + q(e - 2) + 1))
                    sp.wait_ge(s_wlp, BATCHES * l + q(e - 2) + 1)
                sp.dma_start(slot_w(s, NC if k < 2 else 4), srcs[k]).then_inc(s_full[s], 16)

            def load_expert(e, half, n):
                for k in range(3):
                    load_one(e, half, n, k)

            if l == 0:
                sp.wait_ge(s_yav, 4)
                load_one(0, 0, 0, 2)
                for k in range(3):
                    load_one(1, 1, 0, k)
                sp.wait_ge(s_om, 4)
                load_one(0, 0, 0, 1)
                sp.wait_ge(s_om, 8)
                load_one(0, 0, 0, 0)
            else:
                sp.wait_ge(s_ol, 8)
                for k in range(3):
                    load_one(1, 1, 0, k)
                sp.wait_ge(s_cl, 56)
                load_one(0, 0, 0, 0)
                sp.wait_ge(s_cl, 64)
                load_one(0, 0, 0, 1)
                sp.wait_ge(s_om, 16)
                load_one(0, 0, 0, 2)
            for e in (2, 3):
                load_expert(e, e % 2, 1)
            with sp.Fori(2, EXPERTS // 2) as i:
                load_expert(2 * i, 0, i)
                load_expert(2 * i + 1, 1, i)

        @block.sync
        def _(sp):
            for i in range(NT):
                sp.dma_start(x_sb[:, i, :], a["x"][0, P * i:P * i + P, :]).then_inc(s_x, 16)
            sp.dma_start(cst[:, :], consts).then_inc(s_cst, 16)

            used_A = [(s_proj, 2), (s_proj, 6), (s_proj, 10), (s_proj, 14), (s_proj, 18), (s_om, 4), (s_om, 8)]
            used_C = [(s_cl, 8 * (u + 1)) for u in range(8)]

            def load_unit(used_up, slots, src, u):
                s = slots[u]
                for v in range(u - 1, -1, -1):
                    if slots[v] == s:
                        sp.wait_ge(*used_up[v])
                        break
                w = src[u].shape[2]
                sp.dma_start(slot_w(s)[:, :, 0:w], src[u]).then_inc(s_full[s], 16)

            for u in range(7):
                load_unit(used_A, A_SLOTS, A_SRC, u)
            experts_sp(sp, 0)
            if stop > 2:
                sp.dma_start(rope_sb, ropes).then_inc(s_rope, 16)
                sp.wait_ge(s_wl, 3 * (q_up(EXPERTS - 2) + 1))
                sp.wait_ge(s_wlp, q_up(EXPERTS - 2) + 1)
                for u in range(8):
                    load_unit(used_C, C_SLOTS, C_SRC, u)
            if stop > 3:
                experts_sp(sp, 1)
            if stop > 4:
                sp.wait_ge(s_y1, 64)
                sp.dma_start(fn_row, a["final_norm"].rearrange("(o d) -> o d", o=1)).then_inc(s_rope, 16)
                for i in range(NT):
                    sp.wait_ge(s_fin, i + 1)
                    sp.dma_start(out[0, P * i:P * i + P, :], fin[i]).then_inc(s_out, 16)
                sp.wait_ge(s_out, 16 * NT)
            if dbg is not None:
                sp.wait_ge(s_res, 8) if stop == 1 else sp.wait_ge(s_comb, 4) if stop == 2 else sp.wait_ge(s_res, 16) if stop == 3 else sp.wait_ge(s_comb, 8)
                sp.dma_start(out[0].rearrange("(i p) d -> p i d", p=P), x_sb[:, :, :]).then_inc(s_out, 16)
                sp.wait_ge(s_out, 16 * (5 if stop > 4 else 1))

        @block.tensor
        def _(pe):
            def norm_transposes(n):
                cut = hn.rearrange("p i (q c) -> p i c q", c=NC)
                for c in range(NC):
                    if c >= 4:
                        if n == 2:
                            pe.wait_ge(s_trv, evac_before(n) + c - 3)
                        else:
                            pe.wait_ge(s_trv if c % 2 == 0 else s_tra, evac_before(n) + (c - 4) // 2 + 1)
                    for i in range(NT):
                        if c == 0:
                            pe.wait_ge(s_hn, 4 * n + i + 1)
                        ins = pe.transpose(bank(c % 4)[:, P * i:P * i + P], cut[:, i, c, :], ident)
                    ins.then_inc(s_tr, 1)
                pe.wait_ge(s_trv, evac_before(n + 1))
                pe.wait_ge(s_tra, evac_before(n + 1))

            def quarter_mms(out_of, l_of, r_of, per=1):
                ins = None
                for h0 in range(0, H, 2):
                    for flip in range(2):
                        for s in range(2):
                            h = h0 + (s ^ flip)
                            ins = pe.matmul(out_of(h, s), l_of(h, s), r_of(h, s), start=True, stop=True)
                return ins

            pe.wait_ge(s_cst, 16)
            norm_transposes(0)

            def project(m):
                u, col, _ = TILES[m]
                s = A_SLOTS[u]
                if col == 0:
                    pe.wait_ge(s_full[s], 16 * use("A", A_SLOTS, u))
                if m >= 4:
                    pe.wait_ge(s_z, m - 3)
                for c in range(NC):
                    ins = pe.matmul(bank(4 + m % 4), slot_w(s)[:, c, col:col + P], hnT[:, c, :], start=(c == 0), stop=(c == NC - 1))
                ins.then_inc(s_proj, 1)

            for m in range(6):
                project(m)
            pe.wait_ge(s_vec, n_vec)
            pe.wait_ge(s_tanh, 1)
            for j in range(NPAIR):
                if j >= 2:
                    pe.wait_ge(s_am, j - 1)
                b = 2 * (j % 2)
                pe.matmul(bank(b), lora_w[0:64, P * j:P * j + P], z_l0[0:64, :], start=True, stop=True)
                pe.matmul(bank(b + 1), lora_w[64:128, P * j:P * j + P], z_l0[64:128, :], start=True, stop=True).then_inc(s_lora, 1)
            for m in range(6, 10):
                project(m)
            pe.wait_ge(s_am, 4)
            for j in range(NPAIR):
                pe.wait_ge(s_sq, j + 1)
                pe.matmul(bank(0)[0:H, :], K("head_sel")[:, H * j:H * j + H], sq_tmp[j % 2], start=(j == 0), stop=(j == 3)).then_inc(s_hsum, 1)
            for m in range(10, 14):
                project(m)
            pe.wait_ge(s_hinv, 1)
            for j in range(NPAIR):
                pe.matmul(bank(j), K("head_spread", H)[:, P * j:P * j + P], hs, start=True, stop=True).then_inc(s_hb, 1)
            for m in range(14, 18):
                project(m)
            pe.wait_ge(s_rkp, 4)
            pe.wait_ge(s_kk, 4)
            for j in range(NPAIR):
                ins = pe.matmul(bank(0)[0:H, :], K("head_sel")[:, H * j:H * j + H], rk_tmp[:, j, :], start=(j == 0), stop=(j == 3))
            ins.then_inc(s_hsum, 1)
            for g in range(4):
                pe.wait_ge(s_pd, g + 1)
                pe.matmul(bank(4 + (18 + g) % 4), wpool[:, g, :], ybT[:, g, :], start=True, stop=True).then_inc(s_pmm, 1)
            pe.wait_ge(s_rs, 1)
            for j in range(NPAIR):
                pe.matmul(bank(j), K("head_spread", H)[:, P * j:P * j + P], hs, start=True, stop=True).then_inc(s_hb, 1)

            pe.wait_ge(s_prep, 4)
            pe.wait_ge(s_prepp, 4)
            pe.wait_ge(s_bon, 4)
            pe.wait_ge(s_yb, 4)
            for g in range(16):
                q, arr = g // 4, (vT, alT, kT, aT)[g % 4]
                if g >= 8:
                    pe.wait_ge(s_tev if g % 2 == 0 else s_tea, (g - 8) // 2 + 1)
                for j in range(NPAIR):
                    ins = pe.transpose(bank(g % 8)[:, P * j:P * j + P], arr[:, j, P * q:P * q + P], ident)
                ins.then_inc(s_tt, 1)
            pe.wait_ge(s_tev, 8)
            pe.wait_ge(s_tea, 8)

            def ch(arr, h, c):
                po = N * (h % 2)
                return arr[po:po + N, h // 2, C * c:C * c + C]

            def mat(ap, h, s):
                o_ = C * (NPAIR * (h % 2) + h // 2)
                return ap[C * s:C * s + C, o_:o_ + C]

            def tok(ap, h, s):
                return ap[C * s:C * s + C, N * h:N * h + N]

            def local(pr):
                for b in range(2):
                    q = 2 * pr + b
                    for k, (l, r) in enumerate(((aT, alT), (alT, aT), (kT, alT), (kT, rT), (aT, rT))):
                        if b == 1 and k // 2 >= 1:
                            pe.wait_ge(s_gv, 5 * (q - 1) + 2 if k // 2 == 1 else 5 * (q - 1) + 4)
                        bk, o_ = gram_place(q, k)
                        quarter_mms(lambda h, s: bk[C * s:C * s + C, h % 2, o_ + C * (h // 2):o_ + C * (h // 2) + C], lambda h, s: ch(l, h, 2 * q + s), lambda h, s: ch(r, h, 2 * q + s)).then_inc(s_gm, 1)
                pe.wait_ge(s_gv, 10 * pr + 10)
                for lv in range(NL):
                    for b in range(2):
                        q, w, n = 2 * pr + b, wk[b], 2 * NL * pr + 2 * lv + b
                        pe.wait_ge(s_jb, n + 1)
                        if lv > 0:
                            pe.wait_ge(s_jtv, n - 1)
                        quarter_mms(lambda h, s: mat(bank(b), h, s), lambda h, s: mat(w["Bm"], h, s), lambda h, s: mat(w["Tm"], h, s)).then_inc(s_jx, 1)
                    for b in range(2):
                        q, w, n = 2 * pr + b, wk[b], 2 * NL * pr + 2 * lv + b
                        pe.wait_ge(s_jxa, n + 1)
                        if lv < NL - 1:
                            quarter_mms(lambda h, s: mat(bank(2 + b), h, s), lambda h, s: mat(w["TT"], h, s), lambda h, s: mat(w["X"], h, s))
                        quarter_mms(lambda h, s: mat(bank(4 + b), h, s), lambda h, s: mat(w["X"], h, s), lambda h, s: mat(w["TT"], h, s)).then_inc(s_jt, 1)
                for b in range(2):
                    q, w = 2 * pr + b, wk[b]
                    pe.wait_ge(s_jtv, 2 * NL * pr + 2 * NL - 1 + b)
                    quarter_mms(lambda h, s: mat(bank(b), h, s), lambda h, s: mat(w["AK"], h, s), lambda h, s: tok(v_tok[:, q, :], h, s)).then_inc(s_lx, 1)
                    ob = bank_pair[1 + 2 * b]
                    quarter_mms(lambda h, s: ob[N * (h % 2):N * (h % 2) + N, s, C * (h // 2):C * (h // 2) + C], lambda h, s: tok(al_tok[:, q, :], h, s), lambda h, s: mat(w["TT"], h, s)).then_inc(s_lw, 1)
                for b in range(2):
                    q, w = 2 * pr + b, wk[b]
                    pe.wait_ge(s_lxa, q + 1)
                    quarter_mms(lambda h, s: mat(bank(4 + b), h, s), lambda h, s: mat(w["TT"], h, s), lambda h, s: mat(w["X"], h, s)).then_inc(s_lu, 1)

            def sequence(c):
                q, s, kp = c // 2, c % 2, keep[c // 2]
                st = ST[c % 2]
                pe.wait_ge(s_sv, c + 1)
                wt = kp["WT"].rearrange("p (s j t) -> p s j t", s=2, j=NPAIR)
                for h in range(H):
                    po = N * (h % 2)
                    ins = pe.matmul(bank_pair[3][C * s:C * s + C, h % 2, C * (h // 2):C * (h // 2) + C], wt[po:po + N, s, h // 2, :],
                                    st[po:po + N, h // 2, :], start=True, stop=True)
                ins.then_inc(s_um, 1)
                if c >= 2:
                    pe.wait_ge(s_ya, c - 1)
                y_at = lambda h: bank(s)[N * (h % 2):N * (h % 2) + N, C * (h // 2):C * (h // 2) + C]
                for h in range(H):
                    ins = pe.matmul(y_at(h), st[N * (h % 2):N * (h % 2) + N, h // 2, :], ch(rT, h, c), start=(h < 2), stop=False, skip_group_check=True)
                ins.then_inc(s_y0m, 1)
                pe.wait_ge(s_ua, c + 1)
                for h in range(H):
                    po = N * (h % 2)
                    o_ = bank(5)[po:po + N, N * (h // 2):N * (h // 2) + N]
                    pe.matmul(o_, tok(k_tok[:, q, :], h, s), tok(v_tok[:, q, :], h, s), start=True, stop=False)
                    ins = pe.matmul(o_, tok(b_tok[:, q, :], h, s), mat(u_neg, h, s), start=False, stop=True)
                ins.then_inc(s_sm, 1)
                pe.wait_ge(s_y0m, c + 1)
                for h in range(H):
                    pe.matmul(y_at(h), tok(v_tok[:, q, :], h, s), mat(kp["RK"], h, s), start=False, stop=False, skip_group_check=True)
                    ins = pe.matmul(y_at(h), mat(u_neg, h, s), mat(kp["RB"], h, s), start=False, stop=(h >= 6), skip_group_check=True)
                ins.then_inc(s_ym, 1)

            local(0)
            pe.wait_ge(s_luv, 2)
            pe.wait_ge(s_lwa, 2)
            sequence(0)
            sequence(1)
            pe.wait_ge(s_ya, 2)
            pe.wait_ge(s_sv, 3)
            local(1)
            pe.wait_ge(s_luv, 4)
            pe.wait_ge(s_lwa, 4)
            for c in range(2, NCH):
                sequence(c)
            pe.wait_ge(s_ya, NCH)
            pe.wait_ge(s_g, 1)
            for j in range(NPAIR):
                pe.matmul(bank(j), K("head_mean"), yT[:, j, :], start=True, stop=True).then_inc(s_gn, 1)
            pe.wait_ge(s_sv, NCH + 1)
            for j in range(NPAIR):
                ins = pe.matmul(bank(4 + j), gate_w2[:, P * j:P * j + P], gateT_in[:, :], start=True, stop=True)
            ins.then_inc(s_gmm, 1)
            pe.wait_ge(s_gnv, 4)
            for j in range(NPAIR):
                pe.wait_ge(s_gna, j + 1)
                ins = pe.matmul(bank(0)[0:H, :], K("head_sel")[:, H * j:H * j + H], yc_sq[:, T * j:T * j + T], start=(j == 0), stop=(j == 3))
            ins.then_inc(s_gn, 1)
            pe.wait_ge(s_gnv, 6)
            for j in range(NPAIR):
                pe.matmul(bank(j), K("head_spread", H)[:, P * j:P * j + P], hs, start=True, stop=True).then_inc(s_gn, 1)

            def out_project(n, phase, slots, u0, part):
                for half in range(2):
                    s = slots[u0 + half]
                    pe.wait_ge(s_full[s], 16 * use(phase, slots, u0 + half))
                    for i in range(NT):
                        for c in range(NC):
                            ins = pe.matmul(bank(4 * half + i), part(c)[:, P * i:P * i + P], slot_w(s)[:, c, :], start=(c == 0), stop=(c == NC - 1))
                        ins.then_inc(s_om, 1)

            pe.wait_ge(s_yav, 4)
            out_project(0, "A", A_SLOTS, 5, lambda c: yT[:, c, :] if c < 4 else ybT[:, c - 4, :])

            def router_mms(l):
                pe.wait_ge(s_rw, 48 * (l + 1))
                for i in range(NT):
                    o_ = bank(4)[:, 64 * i:64 * i + 36]
                    for c in range(NC):
                        pe.matmul(o_, hnT[:, c, P * i:P * i + P], w_router[:, c, :], start=(c == 0), stop=False)
                    ins = pe.matmul(o_, K("ones", 1), rowv[0:1, 36 * l:36 * l + 36], start=False, stop=True)
                ins.then_inc(s_lg, 1)
                pe.wait_ge(s_oh, l + 1)
                hot = S2[:, rt0 + 1536:rt0 + 1664].rearrange("p (i e) -> p i e", i=NT)
                for i in range(NT):
                    o_ = bank(5)[:, 32 * i:32 * i + 32]
                    for i2 in range(i):
                        pe.matmul(o_, K("ones"), hot[:, i2, :], start=(i2 == 0), stop=False)
                    pe.matmul(o_, K("earlier"), hot[:, i, :], start=(i == 0), stop=True)
                for i in range(NT):
                    ins = pe.matmul(bank(5)[:, 128:160], K("ones"), hot[:, i, :], start=(i == 0), stop=(i == 3))
                ins.then_inc(s_rk, 1)

            XTB, GB, UB, HTB, YB = bank67, bank(0), bank(1), bank(2), (bank(3), bank(4))

            def block_transposes(par, n_wait):
                n_wait()
                cut = rows[par].rearrange("p (q c) -> p c q", c=NC)
                for c in range(NC):
                    ins = pe.transpose(XTB[:, c // 4, TB * (c % 4):TB * (c % 4) + TB], cut[:, c, :], ident[0:TB, 0:TB])
                return ins

            def mm_in(o_, par, q, used_up):
                for j in range(4):
                    wait_split(q, j)
                    for c in (2 * j, 2 * j + 1):
                        r, rest = (w[j][:, 512 * (c % 2):512 * (c % 2) + 512] for w in (wR, wL))
                        pe.matmul(o_[0:TB, :], xR[par][:, c, :], r, start=(c == 0), stop=False)
                        pe.matmul(o_[0:TB, :], xR[par][:, c, :], rest, start=False, stop=False)
                        ins = pe.matmul(o_[0:TB, :], xL[par][:, c, :], r, start=False, stop=(c == NC - 1))
                    ins.then_inc(s_wu, 1)
                pe.wait_ge(s_wu, 4 * q + 4)
                pe.nop().then_inc(used_up, 1)

            def wait_split(q, j):
                if j < 3:
                    pe.wait_ge(s_wl, 3 * q + j + 1)
                else:
                    pe.wait_ge(s_wlp, q + 1)

            def mm_in32(o_, w):
                for c in range(NC):
                    pe.matmul(o_[0:TB, :], xR32[0][:, c, :], w[:, c, :], start=(c == 0), stop=False)
                    ins = pe.matmul(o_[0:TB, :], xL32[0][:, c, :], w[:, c, :], start=False, stop=(c == NC - 1))
                return ins

            def hidden_transposes(par):
                cut = hid[par].rearrange("p (q c) -> p c q", c=4)
                for c in range(4):
                    ins = pe.transpose(HTB[:, TB * c:TB * c + TB], cut[:, c, :], ident[0:TB, 0:TB])
                return ins

            def mm_down(par, q, used_up):
                for c in range(4):
                    wait_split(q, c)
                    for half in range(2):
                        o_ = YB[half][0:TB, :]
                        r, rest = (w[c][:, 512 * half:512 * half + 512] for w in (wR, wL))
                        pe.matmul(o_, hR[par][:, c, :], r, start=(c == 0), stop=False)
                        pe.matmul(o_, hR[par][:, c, :], rest, start=False, stop=False)
                        ins = pe.matmul(o_, hL[par][:, c, :], r, start=False, stop=(c == 3))
                    ins.then_inc(s_wu, 1)
                pe.wait_ge(s_wu, 4 * q + 4)
                pe.nop().then_inc(used_up, 1)

            def mm_down32(w):
                for half in range(2):
                    for c in range(4):
                        w_ = w[:, c, 512 * half:512 * half + 512]
                        pe.matmul(YB[half][0:TB, :], hR32[0][:, c, :], w_, start=(c == 0), stop=False)
                        ins = pe.matmul(YB[half][0:TB, :], hL32[0][:, c, :], w_, start=False, stop=(c == 3))
                return ins

            def experts(l):
                B = EXPERTS * l

                Q = BATCHES * l

                def step(e, par, n, first=False, last=False):
                    pe.wait_ge(s_xl, B + e + 1)
                    if not (first and l == 0):
                        pe.wait_ge(s_h1, B + e)
                    mm_in(GB, par, Q + q_gate(e), s_gate)
                    if not first:
                        pe.wait_ge(s_h, B + e)
                        hidden_transposes(1 - par).then_inc(s_ht, 1)
                    mm_in(UB, par, Q + q_up(e), s_up)
                    if not last:
                        pe.wait_ge(s_rows[1 - par], 16 * (16 * l + (n + 1 if par == 1 else n) + 1))
                        block_transposes(1 - par, lambda: None).then_inc(s_xt, 1)
                    if not first:
                        down(e, 1 - par, Q + 3 * e + 1)

                def down(e, par, q):
                    pe.wait_ge(s_hl, B + e)
                    if not (l == 0 and isinstance(e, int) and e == 1):
                        pe.wait_ge(s_y0, B + e - 1)
                        pe.wait_ge(s_y1, B + e - 1)
                    mm_down(par, q, s_down)

                pe.wait_ge(s_slot, 4 * l + 4)
                pe.wait_ge(s_rows[0], 16 * (16 * l + 1))
                block_transposes(0, lambda: None).then_inc(s_xt, 1)
                step(0, 0, 0, first=True)
                with pe.Fori(0, EXPERTS // 2 - 1) as i:
                    step(2 * i + 1, 1, i)
                    step(2 * i + 2, 0, i + 1)
                step(EXPERTS - 1, 1, EXPERTS // 2 - 1, last=True)
                pe.wait_ge(s_h, B + EXPERTS)
                hidden_transposes(1).then_inc(s_ht, 1)
                down(EXPERTS, 1, Q + q_down(EXPERTS - 1))
                pe.wait_ge(s_y0, B + EXPERTS)
                pe.wait_ge(s_y1, B + EXPERTS)
                v = s_ov[l]
                n = pe.value_load(extra_tab[0:1, 0:1], min_val=0, max_val=EXTRA)
                with pe.If(n > 0):
                    with pe.Fori(0, n) as b:
                        pe.wait_ge(v["rows"], 16 * b + 16)
                        block_transposes(0, lambda: None).then_inc(v["pe"], 1)
                        wait_extra(pe, l, "xl", b)
                        pe.wait_ge(v["w"], 48 * b + 48)
                        mm_in32(GB, slot_w(3))
                        mm_in32(UB, slot_w(4)).then_inc(v["pe"], 1)
                        wait_extra(pe, l, "h", b)
                        hidden_transposes(0).then_inc(v["pe"], 1)
                        wait_extra(pe, l, "hl", b)
                        mm_down32(slot_w(5, 4)).then_inc(v["pe"], 1)
                        wait_extra(pe, l, "y1", b)
                        wait_extra(pe, l, "y0", b)

            def experts_phase(l):
                norm_transposes(1 + 2 * l)
                router_mms(l)
                experts(l)

            def mixer_c():
                norm_transposes(2)
                pe.wait_ge(s_lamm_in, 1)
                pe.matmul(bank(7)[:, 0:2], K("ones", 64), cols["lam"][0:64, 0:2], start=True, stop=True).then_inc(s_lamm, 1)
                for u in range(6):
                    for c in range(NC):
                        pe.wait_ge(s_cl, 8 * u + c + 1)
                        for t in range(4):
                            if c == 0 and u == 1 and t == 3:
                                pe.wait_ge(s_lam, 1)
                            if c == 0 and u >= 2:
                                pe.wait_ge(s_qv, 4 * (u - 2) + t + 1)
                            ins = split_mms(bank(4 * (u % 2) + t), 8 * u + c, hnR[:, c, :], hnL[:, c, :], t, u < 4)
                            if c == NC - 1:
                                ins.then_inc(s_qm if u < 4 else s_vm, 1)
                        if c == NC - 1:
                            pe.wait_ge(s_qm if u < 4 else s_vm, 4 * u + 4 if u < 4 else 4 * (u - 4) + 4)
                            pe.nop().then_inc(s_cu, 1)
                        else:
                            ins.then_inc(s_cu, 1)
                        if 1 <= u <= 4 and 3 <= c < 7:
                            rotate(4 * (u - 1) + c - 3)
                pe.wait_ge(s_va, 4)
                pe.wait_ge(s_mk, 2)
                pe.wait_ge(s_qv, 16)
                for k in range(H * NT + 3):
                    if k < H * NT:
                        scores(k)
                    if k == H * NT:
                        pe.wait_ge(s_ex, 2 * k - 2)
                        for h in range(H - 1):
                            square_sum(h)
                    if 2 <= k < H * NT + 2:
                        if k == 2:
                            pe.wait_ge(s_va, 8)
                        transposes(k - 2)
                    if k >= 3:
                        values(k - 3)
                square_sum(H - 1).then_inc(s_osm, 1)
                pe.wait_ge(s_oi, 1)
                pe.wait_ge(s_oc, H)
                for h in range(H):
                    if h >= 4:
                        pe.wait_ge(s_on, h - 3)
                    pe.matmul(bank(4 + h % 4), ident[0:H, h:h + 1].to_broadcast([H, P]), o_inv, start=True, stop=True).then_inc(s_osm, 1)
                for half in range(2):
                    for c in range(NC):
                        g = 8 * (6 + half) + c
                        pe.wait_ge(s_cl, g + 1)
                        pe.wait_ge(s_ol, c + 1)
                        if half == 1:
                            pe.wait_ge(s_on, 8)
                        for i in range(NT):
                            ins = split_mms(bank(4 * half + i), g, oR[:, c, :], oL[:, c, :], i, False)
                            if c == NC - 1:
                                ins.then_inc(s_om, 1)
                        if c < NC - 1:
                            ins.then_inc(s_cu, 1)
                        elif half == 0:
                            pe.wait_ge(s_om, 12)
                            pe.nop().then_inc(s_cu, 1)

            def split_mms(o_, g, xr, xl, t, channels):
                first, last = g % NC == 0, g % NC == NC - 1
                r, rest = cR[g % 4], cL[g % 4]
                tile_ = slice(P * t, P * t + P)
                if channels:
                    terms = ((r[:, tile_], xr), (r[:, tile_], xl), (rest[:, tile_], xr))
                else:
                    terms = ((xr[:, tile_], r), (xr[:, tile_], rest), (xl[:, tile_], r))
                for k, (l_, r_) in enumerate(terms):
                    ins = pe.matmul(o_, l_, r_, start=(first and k == 0), stop=(last and k == 2))
                return ins

            def rotate(m):
                pe.wait_ge(s_qa, m + 1)
                if m == 0:
                    pe.wait_ge(s_rope, 16)
                pe.matmul(bank(m % 8), swap, raw[m % 4], start=True, stop=True).then_inc(s_rm, 1)

            def square_sum(h):
                pe.wait_ge(s_osq, h + 1)
                return pe.matmul(bank(0)[0:H, :], K("one_col")[:, H - 1 - h:2 * H - 1 - h], osq[:, h, :], start=(h == 0), stop=(h == H - 1))

            SB = [[bank(0), bank(1)], [bank(2), bank(3)]]

            def scores(k):
                h, b = k // NT, k % NT
                w = P * (b + 1)
                if k >= 2:
                    pe.wait_ge(s_ex, 2 * (k - 1))
                for c in range(2):
                    pe.matmul(SB[k % 2][c][:, 0:w], q_half[c][:, h, P * b:P * b + P], kaT[:, h, 0:w], start=True, stop=False)
                for c in range(2):
                    ins = pe.matmul(SB[k % 2][c][:, w - P:w], mask16[:, 0:P], mask16[:, P:2 * P], start=False, stop=True)
                ins.then_inc(s_sc, 1)

            def transposes(k):
                b = k % NT
                pe.wait_ge(s_pr, k + 1)
                if k >= 2:
                    pe.wait_ge(s_pta, k - 1)
                for t in range(b + 1):
                    ins = pe.transpose(bank(4 + k % 2)[:, P * t:P * t + P], prob[k % 2][:, P * t:P * t + P], ident)
                ins.then_inc(s_pt, 1)

            def values(k):
                h, b = k // NT, k % NT
                pe.wait_ge(s_pta, k + 1)
                if b == 0 and h >= 2:
                    pe.wait_ge(s_osq, h - 1)
                for t in range(b + 1):
                    ins = pe.matmul(bank(6 + h % 2)[:, P * b:P * b + P], v_att[:, t, P * h:P * h + P], probT[k % 2][:, P * t:P * t + P], start=(t == 0), stop=(t == b))
                if b == NT - 1:
                    ins.then_inc(s_ov_, 1)

            if stop > 1:
                experts_phase(0)
            if stop > 2:
                mixer_c()
            if stop > 3:
                experts_phase(1)
            if stop > 4:
                pe.wait_ge(s_rope, 32)
                for half in range(2):
                    ins = pe.matmul(bank67[:, half, :], K("ones", 1), fn_row[:, 512 * half:512 * half + 512], start=True, stop=True)
                ins.then_inc(s_fnb, 1)

        @block.vector
        def _(dve):
            own = Steps(dve, s_dve)

            def norm(n):
                for i in range(NT):
                    if i == 0:
                        dve.wait_ge(s_rstd, n + 1)
                    if n % 2 == 0:
                        ins = dve.tensor_scalar(hn[:, i, :], x_sb[:, i, :], cols["rstd"][:, i:i + 1], None, ALU.mult)
                    else:
                        if i == 0:
                            dve.wait_ge(s_rw, 48 * (n // 2 + 1))
                        ins = dve.scalar_tensor_tensor(out=hn[:, i, :], in0=x_sb[:, i, :], scalar=cols["rstd"][:, i:i + 1], in1=g_row, op0=ALU.mult, op1=ALU.mult)
                    ins.then_inc(s_hn, 1)
                g = cols["g_mix0" if n == 0 else "g_mix1"]
                if n == 2:
                    for c in range(NC):
                        dve.wait_ge(s_tra, evac_before(n) + c + 1)
                        dve.scalar_tensor_tensor(out=hnL[:, c, :], in0=bank(c % 4), scalar=g[:, c:c + 1], in1=hnR[:, c, :],
                                                 op0=ALU.mult, op1=ALU.subtract).then_inc(s_trv, 1)
                    return
                for c in range(0, NC, 2):
                    dve.wait_ge(s_tr, 8 * n + c + 1)
                    if n % 2 == 0:
                        ins = dve.tensor_scalar(hnT[:, c, :], bank(c % 4), g[:, c:c + 1], None, ALU.mult)
                    else:
                        ins = dve.tensor_copy(hnT[:, c, :], bank(c % 4))
                    ins.then_inc(s_trv, 1)

            own.next(dve.memset(zeros, 0.0))
            dve.nop().then_inc(s_zero, 1)
            dve.memset(ST[0][:, :, :], 0.0).then_inc(s_sv, 1)
            own.mark(dve.memset(cols["sub_eps"], SUBLN_EPS))
            own.mark(dve.memset(cols["half_decay"], -0.5 * math.exp(-0.5)))
            dve.wait_ge(s_vec, n_vec)
            own.mark(dve.tensor_scalar(cols["one_minus_mu"], cols["mu"], -1.0, 1.0, ALU.mult, ALU.add))
            own.mark(dve.tensor_scalar(cols["half_w0"], cols["w0"], 0.5, None, ALU.mult))
            own.mark(dve.tensor_scalar(cols["half_a0"], cols["a0"], 0.5, None, ALU.mult))
            own.mark(dve.tensor_tensor(cols["lam"][0:64, 0:1], cols["lq"][0:64, 0:1], cols["lq"][0:64, 1:2], ALU.mult))
            own.mark(dve.tensor_tensor(cols["lam"][0:64, 1:2], cols["lq"][0:64, 2:3], cols["lq"][0:64, 3:4], ALU.mult))
            own.mark(dve.tensor_scalar(cols["subln_s"], cols["subln"], 1.0 - LAMBDA_INIT, None, ALU.mult))
            own.hold()
            dve.nop().then_inc(s_lamm_in, 1)
            norm(0)
            dve.wait_ge(s_tr, 8)
            for i in range(3):
                own.mark(dve.memset(upad[i][:, 0:PAD], 0.0))
            for i in range(2):
                own.mark(dve.memset(shift[i][:, 0:1], 0.0))
            own.hold()

            def z(m):
                dve.wait_ge(s_sh, m + 1)
                col = TILES[m][2]
                dve.scalar_tensor_tensor(out=Z_OUT[m], in0=bank(4 + m % 4), scalar=cols["one_minus_mu"][:, col:col + 1], in1=shift[m % 2][:, 0:T],
                                         op0=ALU.mult, op1=ALU.add).then_inc(s_z, 1)

            for m in range(6):
                z(m)
            dve.wait_ge(s_tanh, 2)
            dve.tensor_scalar(gateT_in[:, :], gateT_in[:, :], 0.5, 0.5, ALU.mult, ALU.add).then_inc(s_g, 1)
            for j in range(NPAIR):
                z(6 + j)
                dve.wait_ge(s_wdec, j + 1)
                dve.wait_ge(s_sq, j + 1)
                own.mark(dve.tensor_scalar(kkT[:, j, :], kT[:, j, :], cols["k_k"][:, j:j + 1], None, ALU.mult))
                own.next(dve.tensor_scalar(aT[:, j, :], aT[:, j, :], 0.5, 0.5, ALU.mult, ALU.add))
                own.next(dve.tensor_scalar(alT[:, j, :], aT[:, j, :], -1.0, cols["k_a"][:, j:j + 1], ALU.add, ALU.mult))
                own.next(dve.scalar_tensor_tensor(out=kT[:, j, :], in0=alT[:, j, :], scalar=1.0, in1=kT[:, j, :], op0=ALU.add, op1=ALU.mult))
                if j == 0:
                    own.mark(dve.memset(scan_in, 0.0))
                    own.hold()
                own.next(dve.tensor_copy(scan_in[:, 0:T:C], wT[:, j, 0:T:C]))
                own.next(dve.memset(wT[:, j, 0:T:C], 0.0))
                own.next(dve.tensor_tensor_scan(pT[:, j, :], wT[:, j, :], scan_in, 0.0, ALU.mult, ALU.add))
                own.mark(dve.tensor_copy(pc[:, j, :], pT[:, j, C - 1:T:C]))
                own.mark(dve.scalar_tensor_tensor(out=rk_tmp[:, j, :], in0=rT[:, j, :], scalar=cols["r_k"][:, j:j + 1], in1=kT[:, j, :], op0=ALU.mult, op1=ALU.mult))
            own.hold()
            dve.nop().then_inc(s_rkp, 4)
            for j in range(NPAIR):
                z(10 + j)
                own.mark(dve.reciprocal(piT[:, j, :], pT[:, j, :]))
                if j == 0:
                    dve.wait_ge(s_hroot, 1)
                    own.next(dve.tensor_scalar(hs, hs, 1e-12, None, ALU.max))
                    own.next(dve.reciprocal(hs, hs))
                    dve.nop().then_inc(s_hinv, 1)
            own.hold()
            for j in range(NPAIR):
                dve.wait_ge(s_hb, j + 1)
                own.next(dve.tensor_tensor(kkT[:, j, :], kkT[:, j, :], bank(j), ALU.mult))
                dve.nop().then_inc(s_kk, 1)
                c3 = lambda ap: ap.rearrange("p (c t) -> p c t", c=NCH)
                own.mark(dve.tensor_tensor(c3(alT[:, j, :])[:, :, 1:C], c3(kkT[:, j, :])[:, :, 1:C], c3(pT[:, j, :])[:, :, 0:C - 1], ALU.mult))
                own.mark(dve.tensor_copy(alT[:, j, 0:T:C], kkT[:, j, 0:T:C]))
                own.next(dve.tensor_tensor(aT[:, j, :], aT[:, j, :], kkT[:, j, :], ALU.mult))
                own.next(dve.tensor_tensor(aT[:, j, :], aT[:, j, :], piT[:, j, :], ALU.mult))
                dve.nop().then_inc(s_prep, 1)
            for g in range(4):
                dve.wait_ge(s_win, g + 1)
                dve.scalar_tensor_tensor(out=ybT[:, g, :], in0=upad[1 + g % 2][:, PAD:PAD + T], scalar=1.0 / WINDOWS[g], in1=upad[0][:, PAD:PAD + T],
                                         op0=ALU.mult, op1=ALU.subtract).then_inc(s_pd, 1)
            dve.wait_ge(s_zrows, 16 * n_zero)
            for j in range(NPAIR):
                dve.wait_ge(s_hb, 5 + j)
                dve.tensor_tensor(bonT[:, j, :], bank(j), vT[:, j, :], ALU.mult).then_inc(s_bon, 1)
            for g in range(0, 16, 2):
                dve.wait_ge(s_tt, g + 1)
                dve.tensor_copy((v_tok, al_tok, k_tok, b_tok)[g % 4][:, g // 4, :], bank(g % 8)).then_inc(s_tev, 1)

            def masked(o_, src, m):
                return dve.tensor_tensor(heads(o_), heads(src), per_head(K(m)), ALU.mult)

            def plus_eye(o_):
                return dve.tensor_tensor(heads(o_), heads(o_), per_head(K("eye64")), ALU.add)

            def grams(q):
                w, kp = wk[q % 2], keep[q]

                def finish(k):
                    dve.nop().then_inc(s_gv, 1)


                def b_(k):
                    bk, o_ = gram_place(q, k)
                    return bk[:, :, o_:o_ + 256]

                dve.wait_ge(s_gm, 5 * q + 2)
                own.next(masked(w["LT"], b_(0), "strict"))
                own.next(masked(w["TT"], w["LT"], "up1"))
                own.next(plus_eye(w["TT"]))
                finish(0)
                own.next(masked(w["Tm"], b_(1), "low1"))
                own.next(plus_eye(w["Tm"]))
                finish(1)
                for k, name, m in ((2, "AK", "strict"), (3, "RK", "upto"), (4, "RB", "upto")):
                    dve.wait_ge(s_gm, 5 * q + (4 if k < 4 else 5))
                    masked(w[name] if name == "AK" else kp[name], b_(k), m).then_inc(s_gv, 1)

            def local(pr):
                grams(2 * pr)
                grams(2 * pr + 1)
                dve.wait_ge(s_gv, 10 * pr + 10)
                for lv in range(NL):
                    for b in range(2):
                        w = wk[b]
                        dve.wait_ge(s_jt, 2 * NL * pr + 2 * lv + b + 1)
                        if lv < NL - 1:
                            own.mark(dve.tensor_tensor(w["Tm"], w["Tm"], bank(2 + b), ALU.subtract))
                        own.next(dve.tensor_tensor(w["TT"], w["TT"], bank(4 + b), ALU.subtract))
                        dve.nop().then_inc(s_jtv, 1)
                for b in range(2):
                    q = 2 * pr + b
                    dve.wait_ge(s_lu, q + 1)
                    dve.tensor_scalar(keep[q]["UV"], bank(4 + b), -1.0, None, ALU.mult).then_inc(s_luv, 1)
                dve.wait_ge(s_luv, 2 * pr + 2)

            def sequence(c):
                q, s = c // 2, c % 2
                r = slice(C * s, C * s + C)
                dve.wait_ge(s_um, c + 1)
                if c >= 2:
                    dve.wait_ge(s_ym, c - 1)
                dve.scalar_tensor_tensor(out=both(u_neg[r, :]), in0=bank_pair[3][r, :, 0:256], scalar=-1.0, in1=both(keep[q]["UV"][r, :]), op0=ALU.mult, op1=ALU.add).then_inc(s_ua, 1)
                dve.wait_ge(s_sm, c + 1)
                if c >= 1:
                    dve.wait_ge(s_ym, c)
                own.next(dve.tensor_tensor(STs[:, :, :], ST[c % 2][:, :, :], bank(5)[:, 0:256].rearrange("p (j i) -> p j i", j=NPAIR), ALU.add))
                dve.tensor_tensor(ST[(c + 1) % 2][:, :, :], STs[:, :, :], pc[:, :, c:c + 1].to_broadcast([P, NPAIR, N]), ALU.mult).then_inc(s_sv, 1)
                dve.wait_ge(s_sv, c + 2)

            local(0)
            sequence(0)
            sequence(1)
            local(1)
            for c in range(2, NCH):
                sequence(c)
            for j in range(NPAIR):
                dve.wait_ge(s_gn, j + 1)
                dve.tensor_tensor(yT[:, j, :], yT[:, j, :], bank(j), ALU.subtract).then_inc(s_gnv, 1)
            dve.wait_ge(s_gn, 5)
            own.next(dve.tensor_scalar(hs, bank(0)[0:H, :], 1.0 / N, GN_EPS, ALU.mult, ALU.add))
            dve.nop().then_inc(s_gnv, 1)
            dve.wait_ge(s_gna, 5)
            own.next(dve.reciprocal(hs, hs))
            dve.nop().then_inc(s_gnv, 1)
            for j in range(NPAIR):
                dve.wait_ge(s_gn, 6 + j)
                y = yT[:, j, :]
                own.next(dve.tensor_tensor(y, y, bank(j), ALU.mult))
                own.next(dve.tensor_scalar(y, y, cols["ln_w"][:, j:j + 1], cols["ln_b"][:, j:j + 1], ALU.mult, ALU.add))
                own.next(dve.tensor_tensor(y, y, bonT[:, j, :], ALU.add))
                if j == 0:
                    dve.wait_ge(s_gmm, 1)
                dve.tensor_tensor(y, y, bank(4 + j), ALU.mult).then_inc(s_yav, 1)

            def residual(n):
                for o8 in range(8):
                    half, i = o8 // 4, o8 % 4
                    dve.wait_ge(s_om, 8 * n + o8 + 1)
                    xs = x_sb[:, i, 512 * half:512 * half + 512]
                    dve.tensor_tensor(xs, xs, bank(o8), ALU.add).then_inc(s_res, 1)
                dve.wait_ge(s_res, 8 * n + 8)

            residual(0)

            def router(l):
                at_ = [rt0]

                def tmp(*shape):
                    n = int(np.prod(shape))
                    v = S2[:, at_[0]:at_[0] + n]
                    at_[0] += n
                    return v.rearrange("p (a b) -> p a b", a=shape[0]) if len(shape) == 2 else v

                n4 = lambda name, k: K(name).unsqueeze(1).to_broadcast([P, NT, k])
                over = lambda ap, k: ap.unsqueeze(2).to_broadcast([P, NT, k])
                gl, el, gm, gd = tmp(NT, 4), tmp(NT, 32), tmp(4), tmp(NT, 4)
                cand, cmin, og = tmp(NT, 4), tmp(4), tmp(NT, 4)
                gsum, gw = tmp(4), tmp(4)
                em, cd, oh1, oh2 = tmp(NT, 32), tmp(NT, 32), tmp(NT, 32), tmp(NT, 32)
                m1, m2, cm, e2, den = tmp(4), tmp(4), tmp(4), tmp(4), tmp(4)
                rank, sl, ex, rv = tmp(NT, 32), tmp(NT, 32), tmp(NT, 32), tmp(NT, 32)
                cnt, nov, incl, bo = tmp(32), tmp(32), tmp(32), tmp(32)
                sf = tmp(2, NT)
                assert at_[0] <= rt0 + 1536
                at_[0] = rt0 + 1536
                hot = tmp(NT, 32)
                tab = S2[:, tab_at:tab_at + EXTRA * 32].rearrange("p (b e) -> p b e", b=EXTRA)
                tabf = S2[:, tab_at + EXTRA * 32:tab_at + EXTRA * 32 + 1 + EXTRA]
                lgv = bank(4)[:, 0:256].rearrange("p (i n) -> p i n", i=NT)

                dve.wait_ge(s_lg, l + 1)
                own.mark(dve.tensor_copy(gl, lgv[:, :, 0:4]))
                own.next(dve.tensor_copy(el, lgv[:, :, 4:36]))
                own.next(dve.tensor_reduce(gm, gl, AX, ALU.max))
                own.next(dve.tensor_tensor(gd, gl, over(gm, 4), ALU.subtract))
                dve.nop().then_inc(s_rt, 1)
                own.next(dve.tensor_tensor(cand, gl, over(gm, 4), ALU.is_ge))
                own.next(dve.scalar_tensor_tensor(out=cand, in0=cand, scalar=-100.0, in1=n4("iota4", 4), op0=ALU.mult, op1=ALU.add))
                own.next(dve.tensor_reduce(cmin, cand, AX, ALU.min))
                own.next(dve.tensor_tensor(og, cand, over(cmin, 4), ALU.is_equal))
                own.next(dve.tensor_scalar(cand, og, BIG, -BIG, ALU.mult, ALU.add))
                g16 = lambda ap: ap.rearrange("p i g -> p (i g)").unsqueeze(2).to_broadcast([P, NT * GROUPS, PER_GROUP])
                e16 = lambda ap: ap.rearrange("p i (g e) -> p (i g) e", g=GROUPS)
                own.next(dve.tensor_tensor(e16(em), e16(el), g16(og), ALU.mult))
                own.next(dve.tensor_tensor(e16(em), e16(em), g16(cand), ALU.add))

                def first_largest(v, m, oh):
                    own.next(dve.tensor_reduce(m, v, AX, ALU.max))
                    own.next(dve.tensor_tensor(cd, v, over(m, 32), ALU.is_ge))
                    own.next(dve.scalar_tensor_tensor(out=cd, in0=cd, scalar=-100.0, in1=n4("iota32", 32), op0=ALU.mult, op1=ALU.add))
                    own.next(dve.tensor_reduce(cm, cd, AX, ALU.min))
                    own.next(dve.tensor_tensor(oh, cd, over(cm, 32), ALU.is_equal))

                first_largest(em, m1, oh1)
                own.next(dve.scalar_tensor_tensor(out=em, in0=oh1, scalar=-2 * BIG, in1=em, op0=ALU.mult, op1=ALU.add))
                first_largest(em, m2, oh2)
                own.next(dve.tensor_tensor(hot, oh1, oh2, ALU.add))
                dve.nop().then_inc(s_oh, 1)
                own.next(dve.tensor_tensor(e2, m2, m1, ALU.subtract))
                dve.nop().then_inc(s_rt, 1)
                dve.wait_ge(s_re, 2 * l + 1)
                own.next(dve.tensor_reduce(gsum, gd, AX, ALU.add))
                own.next(dve.reciprocal(gw, gsum))
                dve.wait_ge(s_re, 2 * l + 2)
                own.next(dve.tensor_scalar(den, e2, 1.0, None, ALU.add))
                own.next(dve.reciprocal(den, den))
                own.next(dve.tensor_tensor(wts[:, 0, :], gw, den, ALU.mult))
                own.next(dve.tensor_tensor(wts[:, 1, :], wts[:, 0, :], e2, ALU.mult))
                dve.wait_ge(s_rk, l + 1)
                own.mark(dve.tensor_copy(rank, bank(5)[:, 0:128].rearrange("p (i e) -> p i e", i=NT)))
                own.next(dve.tensor_copy(cnt, bank(5)[:, 128:160]))
                own.next(dve.tensor_scalar(nov, cnt, float(TB), None, ALU.is_gt))
                for k in range(2, (T - 1) // TB + 1):
                    own.next(dve.scalar_tensor_tensor(out=nov, in0=cnt, scalar=float(TB * k), in1=nov, op0=ALU.is_gt, op1=ALU.add))
                own.next(dve.tensor_tensor_scan(incl, K("ones")[:, 0:32], nov, 0.0, ALU.mult, ALU.add))
                own.next(dve.tensor_tensor(bo, incl, nov, ALU.subtract))
                own.next(dve.tensor_scalar(bo, bo, float(TB), float(MAIN_SLOTS - TB), ALU.mult, ALU.add))
                own.next(dve.tensor_tensor(bo, bo, K("first_slot"), ALU.subtract))
                own.next(dve.tensor_scalar(ex, rank, float(TB), None, ALU.is_ge))
                own.next(dve.tensor_tensor(ex, ex, bo.unsqueeze(1).to_broadcast([P, NT, 32]), ALU.mult))
                own.next(dve.tensor_tensor(sl, rank, n4("first_slot", 32), ALU.add))
                own.next(dve.tensor_tensor(sl, sl, ex, ALU.add))
                for k, oh in enumerate((oh1, oh2)):
                    own.next(dve.tensor_tensor(rv, sl, oh, ALU.mult))
                    own.next(dve.tensor_reduce(sf[:, k, :], rv, AX, ALU.add))
                if l > 0:
                    dve.wait_ge(s_comb, NT * l)
                own.next(dve.tensor_copy(slot_ix[:, :, :], sf))
                own.next(dve.tensor_tensor(tab, incl.unsqueeze(1).to_broadcast([P, EXTRA, 32]), K("iota_extra").unsqueeze(2).to_broadcast([P, EXTRA, 32]), ALU.is_le))
                own.next(dve.tensor_reduce(tabf[:, 1:1 + EXTRA], tab, AX, ALU.add))
                own.next(dve.tensor_scalar(tabf[:, 1:1 + EXTRA], tabf[:, 1:1 + EXTRA], float(EXPERTS - 1), None, ALU.min))
                own.next(dve.tensor_copy(tabf[:, 0:1], incl[:, 31:32]))
                own.next(dve.tensor_copy(extra_tab[0:1, :], tabf[0:1, :]))
                dve.nop().then_inc(s_slot, 4)

            def block_rest(par):
                return dve.tensor_tensor(xL[par].rearrange("p (a c) t -> p a c t", a=2), bank67[:, :, 0:4 * TB].rearrange("p a (c t) -> p a c t", c=4),
                                         xR[par].rearrange("p (a c) t -> p a c t", a=2), ALU.subtract)

            def hidden_rest(par):
                return dve.tensor_tensor(hL[par], bank(2)[:, 0:4 * TB].rearrange("p (c t) -> p c t", c=4), hR[par], ALU.subtract)

            def hidden1(par):
                return dve.scalar_tensor_tensor(out=th[par], in0=th[par], scalar=1.0, in1=bank(0)[0:TB, :], op0=ALU.add, op1=ALU.mult)

            def hidden2(par):
                return dve.scalar_tensor_tensor(out=hid[par], in0=th[par], scalar=0.5, in1=bank(1)[0:TB, :], op0=ALU.mult, op1=ALU.mult)

            def out1(par):
                return dve.tensor_copy(yrow[par][:, 512:1024], bank(4)[0:TB, :])

            def experts(l):
                B = EXPERTS * l

                def y1(e, par, n):
                    dve.wait_ge(s_down, B + e)
                    if not (isinstance(n, int) and n == 0 and l == 0):
                        dve.wait_ge(s_yw[par], 16 * (16 * l + n))
                    out1(par).then_inc(s_y1, 1)

                Q = BATCHES * l

                def weights_rest(q, slot_):
                    for j in range(3):
                        dve.wait_ge(s_wr, 4 * (Q + q) + j + 1)
                        dve.tensor_tensor(wL[j], slot(slot_)[:, GROUP * j:GROUP * j + GROUP], wR[j], ALU.subtract).then_inc(s_wl, 1)

                def xrest(e, par):
                    dve.wait_ge(s_xr, B + e + 1)
                    block_rest(par).then_inc(s_xl, 1)

                def hrest(e, par):
                    dve.wait_ge(s_hr, B + e + 1)
                    hidden_rest(par).then_inc(s_hl, 1)

                def step(e, par, n, first=False, last=False):
                    if not (first or (isinstance(e, int) and e == 1)):
                        y1(e - 1, par, n - 1)
                    weights_rest(q_up(e), 3 * par + 1)
                    if not first:
                        hrest(e - 1, 1 - par)
                    dve.wait_ge(s_th, B + e + 1)
                    hidden1(par).then_inc(s_h1, 1)
                    if not first:
                        weights_rest(q_down(e - 1), 3 * (1 - par) + 2)
                    if not last:
                        xrest(e + 1, 1 - par)
                    dve.wait_ge(s_up, B + e + 1)
                    dve.wait_ge(s_h1, B + e + 1)
                    if not (first or (isinstance(e, int) and e == 1)):
                        dve.wait_ge(s_ht, B + e - 1)
                    hidden2(par).then_inc(s_h, 1)
                    if not last:
                        weights_rest(q_gate(e + 1), 3 * (1 - par))

                weights_rest(0, 0)
                xrest(0, 0)
                step(0, 0, 0, first=True)
                step(1, 1, 0)
                step(2, 0, 1)
                with dve.Fori(1, EXPERTS // 2 - 1) as i:
                    step(2 * i + 1, 1, i)
                    step(2 * i + 2, 0, i + 1)
                step(EXPERTS - 1, 1, EXPERTS // 2 - 1, last=True)
                y1(EXPERTS - 1, 0, EXPERTS // 2 - 1)
                hrest(EXPERTS - 1, 1)
                weights_rest(q_down(EXPERTS - 1), 5)
                y1(EXPERTS, 1, EXPERTS // 2 - 1)
                v = s_ov[l]
                dve.wait_ge(s_y1, B + EXPERTS)
                dve.wait_ge(s_yw[0], 16 * 16 * (l + 1))
                n = dve.value_load(extra_tab[0:1, 0:1], min_val=0, max_val=EXTRA)
                with dve.If(n > 0):
                    with dve.Fori(0, n) as b:
                        wait_extra(dve, l, "xr", b)
                        block_rest(0).then_inc(v["dve"], 1)
                        wait_extra(dve, l, "th", b)
                        hidden1(0).then_inc(v["dve"], 1)
                        wait_extra(dve, l, "h1", b)
                        hidden2(0).then_inc(v["dve"], 1)
                        wait_extra(dve, l, "hr", b)
                        hidden_rest(0).then_inc(v["dve"], 1)
                        wait_extra(dve, l, "down", b)
                        out1(0).then_inc(v["dve"], 1)
                        dve.wait_ge(v["written"], 16 * b + 16)

            def combine(l):
                for i in range(NT):
                    dve.wait_ge(s_got[i], 32 * (l + 1))
                    for k in range(2):
                        ins = dve.scalar_tensor_tensor(out=x_sb[:, i, :], in0=got[k][i], scalar=wts[:, k, i:i + 1], in1=x_sb[:, i, :], op0=ALU.mult, op1=ALU.add)
                        if k == 0:
                            own.next(ins)
                    ins.then_inc(s_comb, 1)

            def mixer_c():
                dve.wait_ge(s_rope, 16)
                own.mark(dve.tensor_copy(mask16[:, 0:P], ident))
                own.next(dve.tensor_copy(mask16[:, P:2 * P], mask))
                dve.nop().then_inc(s_mk, 2)
                own.mark(dve.memset(q_half[0][64:128], 0.0))
                own.mark(dve.memset(q_half[1][0:64], 0.0))

                def chunk_rest(g):
                    dve.wait_ge(s_cr, g + 1)
                    s = C_SLOTS[g // NC]
                    dve.tensor_tensor(cL[g % 4], slot_w(s)[:, g % NC, :], cR[g % 4], ALU.subtract).then_inc(s_cl, 1)

                def rope(m):
                    w, r = raw[m % 4], rot[m % 4]
                    dve.wait_ge(s_qa, m + 1)
                    dve.wait_ge(s_rm, m + 1)
                    own.mark(dve.tensor_tensor(w, w, cosT, ALU.mult))
                    own.next(dve.tensor_tensor(r, bank(m % 8), sinT, ALU.mult))
                    if m < 8:
                        own.mark(dve.tensor_tensor(q_half[0][0:64, m, :], w[0:64], r[0:64], ALU.add))
                        dve.tensor_tensor(q_half[1][64:128, m, :], w[64:128], r[64:128], ALU.add).then_inc(s_qv, 1)
                    else:
                        dve.tensor_tensor(kaT[:, m - 8, :], w, r, ALU.add).then_inc(s_qv, 1)

                for g in range(48):
                    chunk_rest(g)
                    u, c = g // NC, g % NC
                    if 1 <= u <= 4 and c >= 4:
                        rope(4 * (u - 1) + c - 4)
                for g in range(48, 52):
                    chunk_rest(g)
                dve.wait_ge(s_qv, 16)
                dve.wait_ge(s_lam, 1)
                own.next(dve.tensor_tensor(cols["lam"][:, 4:5], cols["lam"][:, 3:4], cols["lam"][:, 2:3], ALU.subtract))
                own.next(dve.tensor_scalar(cols["lam"][:, 4:5], cols["lam"][:, 4:5], -LAMBDA_INIT, None, ALU.add))

                def maxima(k):
                    w = P * (k % NT + 1)
                    st = stat[:, k % 2, :]
                    dve.wait_ge(s_sc, k + 1)
                    if k >= 2:
                        dve.wait_ge(s_pr, k - 1)
                    own.next(dve.tensor_reduce(st[:, 0:2], bank_pair[k % 2][:, :, 0:w], AX, ALU.max))
                    own.next(dve.tensor_scalar(st[:, 2:4], st[:, 0:2], -SCALE, None, ALU.mult))
                    dve.nop().then_inc(s_mx, 1)

                def probabilities(k):
                    w = P * (k % NT + 1)
                    st, p = stat[:, k % 2, :], pe_[k % 2]
                    dve.wait_ge(s_ex, 2 * k + 2)
                    own.next(dve.reciprocal(st[:, 6:8], st[:, 4:6]))
                    own.next(dve.tensor_tensor(st[:, 7:8], st[:, 7:8], cols["lam"][:, 4:5], ALU.mult))
                    if k >= 2:
                        dve.wait_ge(s_pt, k - 1)
                    own.next(dve.tensor_scalar(prob[k % 2][:, 0:w], p[:, 0, 0:w], st[:, 6:7], None, ALU.mult))
                    dve.scalar_tensor_tensor(out=prob[k % 2][:, 0:w], in0=p[:, 1, 0:w], scalar=st[:, 7:8], in1=prob[k % 2][:, 0:w], op0=ALU.mult, op1=ALU.add).then_inc(s_pr, 1)

                for k in range(H * NT):
                    maxima(k)
                    if k >= 1:
                        probabilities(k - 1)
                probabilities(H * NT - 1)

                def o_rest(h):
                    dve.wait_ge(s_or, h + 1)
                    dve.tensor_tensor(oL[:, h, :], oT[:, h, :], oR[:, h, :], ALU.subtract).then_inc(s_ol, 1)

                dve.wait_ge(s_ort, 1)
                dve.reciprocal(o_inv, o_inv).then_inc(s_oi, 1)
                for h in range(H):
                    dve.wait_ge(s_osm, h + 2)
                    dve.scalar_tensor_tensor(out=oT[:, h, :], in0=oT[:, h, :], scalar=cols["subln_s"], in1=bank(4 + h % 4), op0=ALU.mult, op1=ALU.mult).then_inc(s_on, 1)
                    if h >= 1:
                        o_rest(h - 1)
                o_rest(H - 1)
                for g in range(52, 64):
                    chunk_rest(g)
                residual(1)

            if stop > 1:
                norm(1)
                router(0)
                experts(0)
                combine(0)
            if stop > 2:
                dve.wait_ge(s_comb, 4)
                norm(2)
                mixer_c()
            if stop > 3:
                norm(3)
                router(1)
                experts(1)
                combine(1)
            if stop > 4:
                dve.wait_ge(s_comb, 8)
                dve.wait_ge(s_rstd, 5)
                dve.wait_ge(s_fnb, 1)
                for i in range(NT):
                    dve.scalar_tensor_tensor(out=fin[i], in0=x_sb[:, i, :], scalar=cols["rstd"][:, i:i + 1], in1=bank67.rearrange("p a b -> p (a b)"),
                                             op0=ALU.mult, op1=ALU.mult).then_inc(s_fin, 1)

        @block.scalar
        def _(act):
            for dst, src in vec_loads:
                act.dma_start(dst, src, allow_slow_non_contiguous=True).then_inc(s_vec, 16)

            def router_weights(l):
                act.dma_start(g_row, a["norm_ffn"][l:l + 1, :].to_broadcast([P, D])).then_inc(s_rw, 16)
                act.dma_start(w_router[:, :, 0:4], a["moe_w_group"][l].rearrange("(p c) n -> p c n", c=NC), allow_slow_non_contiguous=True).then_inc(s_rw, 16)
                act.dma_start(w_router[:, :, 4:36], a["moe_w_expert"][l].rearrange("(p c) n -> p c n", c=NC), allow_slow_non_contiguous=True).then_inc(s_rw, 16)

            own = Steps(act, s_act)

            def norm(n):
                src = {0: (s_x, 16 * NT, 0), 1: (s_res, 4, 1), 2: (s_comb, 0, 1), 3: (s_res, 12, 1), 4: (s_comb, 4, 1)}[n]
                for i in range(NT):
                    act.wait_ge(src[0], src[1] + src[2] * (i + 1))
                    act.activation(hn[:, i, :], x_sb[:, i, :], ACT.Square, accum_out=cols["ss"][:, i:i + 1]).then_inc(s_ss, 1)
                if n == 4:
                    return
                g = cols["g_mix0" if n == 0 else "g_mix1"]
                if n == 0:
                    act.wait_ge(s_vec, n_vec)
                if n == 2:
                    for c in range(NC):
                        act.wait_ge(s_tr, 8 * n + c + 1)
                        act.activation(hnR[:, c, :], bank(c % 4), ACT.Copy, scale=g[:, c:c + 1]).then_inc(s_tra, 1)
                    return
                for c in range(1, NC, 2):
                    act.wait_ge(s_tr, 8 * n + c + 1)
                    act.activation(hnT[:, c, :], bank(c % 4), ACT.Copy, scale=(g[:, c:c + 1] if n % 2 == 0 else 1.0)).then_inc(s_tra, 1)

            norm(0)

            def shifted(m):
                act.wait_ge(s_proj, m + 1)
                if m >= 2:
                    act.wait_ge(s_z, m - 1)
                if m == 0:
                    act.wait_ge(s_trv, 4)
                    act.wait_ge(s_dve, n_setup)
                col = TILES[m][2]
                act.activation(shift[m % 2][:, 1:T + 1], bank(4 + m % 4), ACT.Copy, scale=cols["mu"][:, col:col + 1]).then_inc(s_sh, 1)

            shifted(0)
            shifted(1)
            act.wait_ge(s_z, 1)
            act.activation(z_l0[0:64, :], z_l0[0:64, :], ACT.Tanh).then_inc(s_tanh, 1)
            act.wait_ge(s_z, 2)
            act.activation(gateT_in[:, :], gateT_in[:, :], ACT.Tanh, scale=0.5).then_inc(s_tanh, 1)
            for m in range(2, 6):
                shifted(m)
            for j in range(NPAIR):
                act.wait_ge(s_lora, j + 1)
                b = 2 * (j % 2)
                act.activation(wT[:, j, :], bank(b), ACT.Tanh, scale=0.5, bias=cols["half_w0"][:, j:j + 1]).then_inc(s_act, 1)
                act.activation(aT[:, j, :], bank(b + 1), ACT.Tanh, scale=0.5, bias=cols["half_a0"][:, j:j + 1]).then_inc(s_am, 1)
                act.wait_ge(s_am, j + 1)
                act.activation(wT[:, j, :], wT[:, j, :], ACT.Exp, scale=-0.5 * math.exp(-0.5), bias=cols["half_decay"]).then_inc(s_wdec, 1)
            for j in range(NPAIR):
                shifted(6 + j)
                if j >= 2:
                    act.wait_ge(s_hsum, j - 1)
                act.activation(sq_tmp[j % 2], kT[:, j, :], ACT.Square, scale=cols["k_k"][:, j:j + 1]).then_inc(s_sq, 1)
            act.wait_ge(s_hsum, 4)
            act.activation(hs, bank(0)[0:H, :], ACT.Sqrt).then_inc(s_hroot, 1)
            for m in range(10, 14):
                shifted(m)
            for g in range(4):
                act.wait_ge(s_proj, 15 + g)
                if g >= 1:
                    act.wait_ge(s_pd, g)
                act.activation(upad[0][:, PAD:PAD + T], bank(4 + (14 + g) % 4), ACT.Copy).then_inc(s_u, 1)
            act.wait_ge(s_hsum, 5)
            act.activation(hs, bank(0)[0:H, :], ACT.Copy).then_inc(s_rs, 1)
            for g in range(4):
                act.wait_ge(s_pmm, g + 1)
                act.activation(ybT[:, g, :], bank(4 + (18 + g) % 4), ACT.Copy, scale=cols["pool_scale"][:, g:g + 1]).then_inc(s_yb, 1)
            for g in range(1, 16, 2):
                act.wait_ge(s_tt, g + 1)
                act.activation((v_tok, al_tok, k_tok, b_tok)[g % 4][:, g // 4, :], bank(g % 8), ACT.Copy).then_inc(s_tea, 1)

            def local(pr):
                for lv in range(NL):
                    for b in range(2):
                        n = 2 * NL * pr + 2 * lv + b
                        act.wait_ge(s_jx, n + 1)
                        if lv >= 1:
                            act.wait_ge(s_jt, n - 1)
                        act.activation(wk[b]["X"], bank(b), ACT.Copy).then_inc(s_jxa, 1)
                for b in range(2):
                    q = 2 * pr + b
                    act.wait_ge(s_lx, q + 1)
                    act.wait_ge(s_jxa, 2 * NL * pr + 2 * NL)
                    act.activation(wk[b]["X"], bank(b), ACT.Copy).then_inc(s_lxa, 1)
                    act.wait_ge(s_lw, q + 1)
                    act.activation(both(keep[q]["WT"]), bank_pair[1 + 2 * b][:, :, 0:256], ACT.Copy).then_inc(s_lwa, 1)

            def sequence(c):
                q, s = c // 2, c % 2
                act.wait_ge(s_ym, c + 1)
                act.activation(yT[:, :, C * c:C * c + C], bank(s)[:, 0:256].rearrange("p (j t) -> p j t", j=NPAIR), ACT.Copy).then_inc(s_ya, 1)

            local(0)
            sequence(0)
            sequence(1)
            local(1)
            for c in range(2, NCH):
                sequence(c)
            for j in range(NPAIR):
                act.wait_ge(s_gnv, j + 1)
                act.activation(yc_sq[:, T * j:T * j + T], yT[:, j, :], ACT.Square).then_inc(s_gna, 1)
            act.wait_ge(s_gnv, 5)
            act.activation(hs, hs, ACT.Sqrt).then_inc(s_gna, 1)
            act.wait_ge(s_yav, 4)
            if stop > 1:
                router_weights(0)

            def tanh_half(par):
                return act.activation(th[par], bank(0)[0:TB, :], ACT.Tanh, scale=0.5)

            def block_copy(par):
                return act.activation(xR[par].rearrange("p (a c) t -> p a c t", a=2), bank67[:, :, 0:4 * TB].rearrange("p a (c t) -> p a c t", c=4), ACT.Copy)

            def hidden_copy(par):
                return act.activation(hR[par], bank(2)[:, 0:4 * TB].rearrange("p (c t) -> p c t", c=4), ACT.Copy)

            def out0(par):
                return act.activation(yrow[par][:, 0:512], bank(3)[0:TB, :], ACT.Copy)

            def experts(l):
                B = EXPERTS * l
                act.wait_ge(s_rt, 2 * l + 1)
                gd = S2[:, rt0 + 16 + 128 + 4:rt0 + 16 + 128 + 4 + 16]
                act.activation(gd, gd, ACT.Exp).then_inc(s_re, 1)
                act.wait_ge(s_rt, 2 * l + 2)
                e2 = S2[:, e2_at:e2_at + 4]
                act.activation(e2, e2, ACT.Exp).then_inc(s_re, 1)

                Q = BATCHES * l

                def y0(e, par, n):
                    act.wait_ge(s_down, B + e)
                    if not (isinstance(n, int) and n == 0 and l == 0):
                        act.wait_ge(s_yw[par], 16 * (16 * l + n))
                    out0(par).then_inc(s_y0, 1)

                def xround(e, par):
                    act.wait_ge(s_xt, B + e + 1)
                    block_copy(par).then_inc(s_xr, 1)

                def hround(e, par):
                    act.wait_ge(s_ht, B + e + 1)
                    if not (isinstance(e, int) and e <= 1):
                        act.wait_ge(s_down, B + e - 1)
                    hidden_copy(par).then_inc(s_hr, 1)

                def weights_rounded(q, slot_, n, quarters=range(4)):
                    act.wait_ge(s_full[slot_], 16 * (moe_before(l, slot_) + n + 1))
                    for j in quarters:
                        if not (isinstance(q, int) and q == 0):
                            act.wait_ge(s_wu, 4 * (Q + q - 1) + j + 1)
                        act.activation(wR[j], slot(slot_)[:, GROUP * j:GROUP * j + GROUP], ACT.Copy).then_inc(s_wr, 1)

                def load_rows(e, par):
                    act.dma_start(rows[par], xp[bass.ds(TB * e, TB), :]).then_inc(s_rows[par], 16)

                def store(e, par):
                    act.wait_ge(s_y0, B + e)
                    act.wait_ge(s_y1, B + e)
                    act.dma_start(yp[bass.ds(TB * (e - 1), TB), :], yrow[par]).then_inc(s_yw[par], 16)

                act.wait_ge(s_rk, l + 1)
                weights_rounded(0, 0, 0, (0, 1))
                act.wait_ge(s_disp, 16 * 2 * NT * (l + 1))
                load_rows(0, 0)
                load_rows(1, 1)
                weights_rounded(0, 0, 0, (2, 3))

                def step(e, par, n, first=False, last=False):
                    if not (first or (isinstance(e, int) and e == 1)):
                        y0(e - 1, par, n - 1)
                    weights_rounded(q_up(e), 3 * par + 1, n)
                    if not (first or (isinstance(e, int) and e == 1)):
                        store(e - 1, par)
                    if not first:
                        hround(e - 1, 1 - par)
                    act.wait_ge(s_gate, B + e + 1)
                    if not (isinstance(e, int) and e <= 1):
                        act.wait_ge(s_h, B + e - 1)
                    tanh_half(par).then_inc(s_th, 1)
                    if not last and not (isinstance(e, int) and e == EXPERTS - 2):
                        load_rows(e + 2, par)
                    if not first:
                        weights_rounded(q_down(e - 1), 3 * (1 - par) + 2, n if par == 1 else n - 1)
                    if not last:
                        xround(e + 1, 1 - par)
                        weights_rounded(q_gate(e + 1), 3 * (1 - par), n + 1 if par == 1 else n)

                xround(0, 0)
                step(0, 0, 0, first=True)
                step(1, 1, 0)
                step(2, 0, 1)
                with act.Fori(1, EXPERTS // 2 - 2) as i:
                    step(2 * i + 1, 1, i)
                    step(2 * i + 2, 0, i + 1)
                step(EXPERTS - 3, 1, EXPERTS // 2 - 2)
                step(EXPERTS - 2, 0, EXPERTS // 2 - 1)
                step(EXPERTS - 1, 1, EXPERTS // 2 - 1, last=True)
                y0(EXPERTS - 1, 0, EXPERTS // 2 - 1)
                store(EXPERTS - 1, 0)
                hround(EXPERTS - 1, 1)
                weights_rounded(q_down(EXPERTS - 1), 5, EXPERTS // 2 - 1)
                y0(EXPERTS, 1, EXPERTS // 2 - 1)
                store(EXPERTS, 1)
                v = s_ov[l]
                act.wait_ge(s_down, B + EXPERTS)
                act.wait_ge(s_y0, B + EXPERTS)
                act.wait_ge(s_yw[0], 16 * 16 * (l + 1))
                n = act.value_load(extra_tab[0:1, 0:1], min_val=0, max_val=EXTRA)
                with act.If(n > 0):
                    with act.Fori(0, n) as b:
                        e = act.value_load(extra_tab[0:1, bass.ds(b + 1, 1)], min_val=0, max_val=EXPERTS - 1)
                        act.dma_start(slot_w(3), a["moe_w_gate"][l, bass.ds(e, 1)].rearrange("o (p c) n -> (o p) c n", c=NC)).then_inc(v["w"], 16)
                        act.dma_start(slot_w(4), a["moe_w_up"][l, bass.ds(e, 1)].rearrange("o (p c) n -> (o p) c n", c=NC)).then_inc(v["w"], 16)
                        act.dma_start(slot_w(5, 4), a["moe_w_down"][l, bass.ds(e, 1)].rearrange("o (p c) n -> (o p) c n", c=4)).then_inc(v["w"], 16)
                        act.dma_start(rows[0], xp[bass.ds(TB * b + MAIN_SLOTS, TB), :]).then_inc(v["rows"], 16)
                        wait_extra(act, l, "xt", b)
                        block_copy(0).then_inc(v["act"], 1)
                        wait_extra(act, l, "up", b)
                        tanh_half(0).then_inc(v["act"], 1)
                        wait_extra(act, l, "ht", b)
                        hidden_copy(0).then_inc(v["act"], 1)
                        wait_extra(act, l, "down", b)
                        out0(0).then_inc(v["act"], 1)
                        wait_extra(act, l, "y0", b)
                        wait_extra(act, l, "y1", b)
                        act.dma_start(yp[bass.ds(TB * b + MAIN_SLOTS, TB), :], yrow[0]).then_inc(v["written"], 16)
                        act.wait_ge(v["written"], 16 * b + 16)
                if l == 0 and stop > 3:
                    router_weights(1)

            def mixer_c():
                act.wait_ge(s_lamm, 1)
                act.activation(cols["lam"][:, 2:4], bank(7)[:, 0:2], ACT.Exp).then_inc(s_lam, 1)

                def chunk_rounded(g):
                    s = C_SLOTS[g // NC]
                    if g % NC == 0:
                        act.wait_ge(s_full[s], 16 * use("C", C_SLOTS, g // NC))
                    if g >= 4:
                        act.wait_ge(s_cu, g - 3)
                    act.activation(cR[g % 4], slot_w(s)[:, g % NC, :], ACT.Copy).then_inc(s_cr, 1)

                def raw_copy(m):
                    act.wait_ge(s_qm, m + 1)
                    if m >= 4:
                        act.wait_ge(s_qv, m - 3)
                    act.activation(raw[m % 4], bank(m % 8), ACT.Copy).then_inc(s_qa, 1)

                def v_copy(n):
                    half, i = n // NT, n % NT
                    act.wait_ge(s_vm, n + 1)
                    act.activation(v_att[:, i, 512 * half:512 * half + 512], bank(n), ACT.Copy).then_inc(s_va, 1)

                for g in range(48):
                    chunk_rounded(g)
                    u, c = g // NC, g % NC
                    if u >= 1 and 2 <= c < 6:
                        if u < 5:
                            raw_copy(4 * (u - 1) + c - 2)
                        else:
                            v_copy(c - 2)
                for i in range(NT):
                    chunk_rounded(48 + i)
                for i in range(NT):
                    v_copy(NT + i)

                def exps(k):
                    w = P * (k % NT + 1)
                    st = stat[:, k % 2, :]
                    act.wait_ge(s_mx, k + 1)
                    for c in range(2):
                        act.activation(pe_[k % 2][:, c, 0:w], bank(2 * (k % 2) + c)[:, 0:w], ACT.Exp, scale=SCALE, bias=st[:, 2 + c:3 + c],
                                       accum_out=st[:, 4 + c:5 + c]).then_inc(s_ex, 1)

                def evac(k):
                    w = P * (k % NT + 1)
                    act.wait_ge(s_pt, k + 1)
                    if k >= 2:
                        act.wait_ge(s_pta, k - 1)
                    act.activation(probT[k % 2][:, 0:w], bank(4 + k % 2)[:, 0:w], ACT.Copy).then_inc(s_pta, 1)

                def head_out(h):
                    act.wait_ge(s_ov_, h + 1)
                    act.activation(oT[:, h, :], bank(6 + h % 2), ACT.Copy).then_inc(s_oc, 1)
                    act.activation(osq[:, h, :], bank(6 + h % 2), ACT.Square, scale=128 ** -0.5).then_inc(s_osq, 1)

                for k in range(H * NT + 3):
                    if k < H * NT:
                        exps(k)
                    if 2 <= k < H * NT + 2:
                        evac(k - 2)
                    if k >= 3 and (k - 3) % NT == NT - 1:
                        head_out((k - 3) // NT)
                act.wait_ge(s_osm, 1)
                act.activation(o_inv, bank(0)[0:H, :], ACT.Sqrt, bias=cols["sub_eps"][0:H]).then_inc(s_ort, 1)
                for h in range(H):
                    act.wait_ge(s_on, h + 1)
                    act.activation(oR[:, h, :], oT[:, h, :], ACT.Copy).then_inc(s_or, 1)
                for g in range(52, 64):
                    chunk_rounded(g)

            if stop > 1:
                norm(1)
                experts(0)
            if stop > 2:
                norm(2)
                mixer_c()
            if stop > 3:
                norm(3)
                experts(1)
            if stop > 4:
                norm(4)

        @block.gpsimd
        def _(pool):
            own = Steps(pool, s_pool)

            def rstd(n):
                if n == 0:
                    pool.wait_ge(s_cst, 16)
                pool.wait_ge(s_ss, 4 * n + 4)
                if n >= 1 and n < 4:
                    pool.wait_ge(s_hn, 4 * n)
                own.next(pool.tensor_scalar(cols["ms"], cols["ss"], 1.0 / D, RMS_EPS, ALU.mult, ALU.add))
                own.next(pool.tensor_tensor(cols["rstd"], cols["ms"], K("minus_half"), ALU.pow))
                pool.nop().then_inc(s_rstd, 1)

            rstd(0)
            pool.wait_ge(s_zero, 1)
            pool.wait_ge(s_full[1], 16)
            zr = xp.rearrange("(p r) d -> p (r d)", p=TB)
            for k in range(SLOTS // TB // 2):
                pool.dma_start(zr[:, 2 * D * k:2 * D * k + 2 * D], zeros[0:TB, :]).then_inc(s_zrows, 16)
            ze = yp[MAIN_SLOTS:SLOTS, :].rearrange("(p r) d -> p (r d)", p=TB)
            for k in range(EXTRA // 2):
                pool.dma_start(ze[:, 2 * D * k:2 * D * k + 2 * D], zeros[0:TB, :]).then_inc(s_zrows, 16)
            for g in range(4):
                pool.wait_ge(s_u, g + 1)
                src = upad[0]
                for k in range(g + 1):
                    dst = upad[1 + k % 2]
                    own.next(pool.tensor_tensor(dst[:, PAD:PAD + T], src[:, PAD:PAD + T], src[:, PAD - 2 ** k:PAD + T - 2 ** k], ALU.add))
                    src = dst
                own.next(pool.tensor_tensor(src[:, PAD:2 * PAD], src[:, PAD:2 * PAD], K("short_window")[:, 16 * g:16 * g + 16], ALU.mult))
                pool.nop().then_inc(s_win, 1)
            pool.wait_ge(s_prep, 4)
            pool.wait_ge(s_hsum, 5)
            for j in range(NPAIR):
                own.mark(pool.tensor_tensor(kT[:, j, :], kT[:, j, :], piT[:, j, :], ALU.mult))
                own.next(pool.tensor_tensor(rT[:, j, :], rT[:, j, :], pT[:, j, :], ALU.mult))
                pool.nop().then_inc(s_prepp, 1)

            def local(pr):
                for lv, m in enumerate(LEVELS):
                    for b in range(2):
                        q, w, n = 2 * pr + b, wk[b], 2 * NL * pr + 2 * lv + b
                        pool.wait_ge(s_gv, 5 * q + 1)
                        if lv >= 1:
                            pool.wait_ge(s_jx, n - 1)
                        pool.tensor_tensor(heads(w["Bm"]), heads(w["LT"]), per_head(K(f"join{m}")), ALU.mult).then_inc(s_jb, 1)

            local(0)
            local(1)

            def experts(l):
                B = 16 * l
                pool.wait_ge(s_slot, 4 * l + 4)
                pool.wait_ge(s_hn, 4 * (1 + 2 * l) + 4)
                for k in range(2):
                    for i in range(NT):
                        pool.indirect_dma_start(out=xp, out_offset=bass.IndirectOffsetOnAxis(ap=slot_ix[:, k, i:i + 1], axis=0),
                                                in_=hn[:, i, :], in_offset=None).then_inc(s_disp, 16)
                Q = BATCHES * l

                def weights_rest(q, slot_):
                    pool.wait_ge(s_wr, 4 * (Q + q) + 4)
                    pool.tensor_tensor(wL[3], slot(slot_)[:, 3 * GROUP:UNIT], wR[3], ALU.subtract).then_inc(s_wlp, 1)

                def step(e, par):
                    weights_rest(q_up(e), 3 * par + 1)
                    weights_rest(q_down(e - 1), 3 * (1 - par) + 2)
                    weights_rest(q_gate(e + 1), 3 * (1 - par))

                weights_rest(0, 0)
                weights_rest(1, 1)
                weights_rest(2, 3)
                with pool.Fori(0, EXPERTS // 2 - 1) as i:
                    step(2 * i + 1, 1)
                    step(2 * i + 2, 0)
                weights_rest(q_up(EXPERTS - 1), 4)
                weights_rest(q_down(EXPERTS - 2), 2)
                weights_rest(q_down(EXPERTS - 1), 5)
                for par in range(2):
                    pool.wait_ge(s_yw[par], 16 * 16 * (l + 1))
                pool.wait_ge(s_xt, EXPERTS * (l + 1))
                v = s_ov[l]
                n = pool.value_load(extra_tab[0:1, 0:1], min_val=0, max_val=EXTRA)
                with pool.If(n > 0):
                    with pool.Fori(0, n) as b:
                        pool.wait_ge(v["written"], 16 * b + 16)
                for i in range(NT):
                    for k in range(2):
                        pool.indirect_dma_start(out=got[k][i], out_offset=None, in_=yp,
                                                in_offset=bass.IndirectOffsetOnAxis(ap=slot_ix[:, k, i:i + 1], axis=0)).then_inc(s_got[i], 16)

            if stop > 1:
                rstd(1)
                experts(0)
            if stop > 2:
                rstd(2)
            if stop > 3:
                rstd(3)
                experts(1)
            if stop > 4:
                rstd(4)


_INS = ["x", "norm_mix", "norm_ffn", "final_norm", "a_w_in", "a_mu", "a_w0", "a_w2", "a_a0", "a_a2", "a_g2",
        "a_k_k", "a_k_a", "a_r_k", "a_ln_w", "a_ln_b", "b_w_pool", "b_pool_scale", "ab_w_out",
        "c_w_qkv", "c_lambda_q1", "c_lambda_k1", "c_lambda_q2", "c_lambda_k2", "c_subln", "c_w_out",
        "moe_w_group", "moe_b_group", "moe_w_expert", "moe_b_expert", "moe_w_gate", "moe_w_up", "moe_w_down"]


def kernel(**inputs):
    import numpy as _np
    import concourse.bacc as _bacc
    from concourse import mybir as _mybir
    from concourse.bass_utils import run_bass_kernel_spmd as _run

    nc = _bacc.Bacc("TRN2", target_bir_lowering=False, num_devices=1)
    arrays, args = {}, {}
    for name in _INS:
        arr = _np.ascontiguousarray(inputs[name])
        arrays[f"in_{name}"] = arr
        args[name] = nc.dram_tensor(f"in_{name}", arr.shape, _mybir.dt.from_np(arr.dtype), kind="ExternalInput").ap()
    tables = {"constants": constant_table()[1], "rope": rope_table()}
    aps = {}
    for name, arr in tables.items():
        arrays[name] = arr
        aps[name] = nc.dram_tensor(name, arr.shape, _mybir.dt.from_np(arr.dtype), kind="ExternalInput").ap()
    out = nc.dram_tensor("out", (1, T, D), _mybir.dt.float32, kind="ExternalOutput").ap()
    build(nc, args, aps["constants"], aps["rope"], out)
    r = _run(nc, [arrays], core_ids=[0])
    return r.results[0]["out"]
```

```python
from contextlib import ExitStack
import math

import numpy as np

import concourse.bass as bass
from concourse import mybir

F32 = mybir.dt.float32
F32R = mybir.dt.float32r
BF16 = mybir.dt.bfloat16
I32 = mybir.dt.int32
ALU = mybir.AluOpType
ACT = mybir.ActivationFunctionType
AX = mybir.AxisListType.X

P = 128
T = 512
D = 1024
NT = T // P
NC = D // P
H = 8
N = 64
C = 64
NCH = T // C
NPAIR = H // 2
GN_EPS = 64e-5
RMS_EPS = 1e-6
SUBLN_EPS = 1e-5
WINDOWS = (2, 4, 8, 16)
EXPERTS = 32
GROUPS = 4
PER_GROUP = 8
FF = 512
TB = 72
EXTRA = (2 * T - 1) // TB
MORE = (T - 1) // TB
MAIN_SLOTS = EXPERTS * TB
SLOTS = MAIN_SLOTS + EXTRA * TB
LAMBDA_INIT = 0.8 - 0.6 * math.exp(-0.3)
ROPE_DIMS = 16
ROPE_THETA = 500000.0
SCALE = 64 ** -0.5
BIG = 1e30
ROUTER_E2 = 732
UNIT = 4096
SLAB = 2048


def constant_table():
    p = np.arange(P)
    f = np.arange(P)
    blocks = {}
    blocks["ident"] = np.eye(P)
    blocks["earlier"] = (p[:, None] < f[None, :])
    blocks["ones"] = np.ones((P, P))
    blocks["head_mean"] = (p[:, None] // N == f[None, :] // N) / N
    sel = np.zeros((P, NPAIR, H))
    for j in range(NPAIR):
        sel[p, j, 2 * j + p // N] = 1
    blocks["head_sel"] = sel.reshape(P, -1)
    spread = np.zeros((P, NPAIR, P))
    for j in range(NPAIR):
        spread[2 * j + p // N, j, p] = 1
    blocks["head_spread"] = spread.reshape(P, -1)
    r, c = (p % C)[:, None], np.arange(C)[None, :]
    blocks["eye64"] = (r == c)
    blocks["low1"] = -((r // 2 == c // 2) & (r > c)).astype(float)
    blocks["up1"] = -((r // 2 == c // 2) & (r < c)).astype(float)
    for m in (2, 4, 8, 16, 32):
        blocks[f"join{m}"] = (r // (2 * m) == c // (2 * m)) & (r % (2 * m) < m) & (c % (2 * m) >= m)
    blocks["strict"] = (r < c)
    blocks["upto"] = (r <= c)
    win = np.ones((P, 4, 16))
    for g, w in enumerate(WINDOWS):
        t = np.arange(16)
        win[:, g] = w / np.minimum(t + 1, w)
    blocks["short_window"] = win.reshape(P, -1)
    blocks["iota4"] = np.tile(np.arange(4), (P, 1))
    blocks["iota32"] = np.tile(np.arange(32), (P, 1))
    blocks["iota_extra"] = np.tile(np.arange(EXTRA), (P, 1))
    blocks["first_slot"] = np.tile(TB * np.arange(EXPERTS), (P, 1))
    one_col = np.zeros((P, 2 * H - 1))
    one_col[:, H - 1] = 1
    blocks["one_col"] = one_col
    blocks["block_edges"] = np.tile(TB * np.arange(1, MORE + 1), (P, 1))
    blocks["minus_half"] = np.full((P, 4), -0.5)
    at, n = {}, 0
    for k, v in blocks.items():
        at[k] = (n, n + v.shape[1])
        n += v.shape[1]
    return at, np.concatenate([np.asarray(v, np.float32) for v in blocks.values()], axis=1)


def rope_table():
    inv = ROPE_THETA ** (-np.arange(0, ROPE_DIMS, 2, dtype=np.float32) / ROPE_DIMS)
    ang = np.arange(T, dtype=np.float32)[:, None] * inv.astype(np.float32)[None, :]
    cos, sin = np.ones((P, T)), np.zeros((P, T))
    swap = np.zeros((P, P))
    half = ROPE_DIMS // 2
    for base in (0, 64):
        for i in range(half):
            a, b = base + i, base + half + i
            cos[a] = cos[b] = np.cos(ang[:, i])
            sin[a] = sin[b] = np.sin(ang[:, i])
            swap[b, a] = -1
            swap[a, b] = 1
    q, k = np.arange(P)[:, None], np.arange(P)[None, :]
    mask = np.where(k <= q, 0.0, -BIG)
    return np.concatenate([cos, sin, swap, mask], axis=1).astype(np.float32)


class Steps:

    def __init__(self, eng, sem):
        self.eng, self.sem, self.n = eng, sem, 0

    def mark(self, ins):
        self.n += 1
        ins.then_inc(self.sem, 1)

    def hold(self):
        self.eng.wait_ge(self.sem, self.n)

    def next(self, ins):
        self.mark(ins)
        self.hold()


def build(nc, a, consts, ropes, out):
    at, _ = constant_table()
    xp = nc.dram_tensor("expert_rows", [SLOTS, D], F32, kind="Internal").ap()
    yp = nc.dram_tensor("expert_out", [SLOTS, D], F32, kind="Internal").ap()
    ctx = ExitStack()
    with ctx:
        def sb(name, shape, dt=F32):
            return ctx.enter_context(nc.sbuf_tensor(name, shape, dt))

        def sem(name):
            return ctx.enter_context(nc.semaphore(name))

        x_sb = sb("x_sb", [P, NT, D])
        first_slot = sb("first_slot", [P, UNIT])

        def twice(name, n):
            with nc.sbuf_tensor(name + "_r", [P, n], F32R) as r:
                pass
            return sb(name, [P, n]), r

        S1, S1r = twice("shared_scratch", 3 * UNIT)
        S5, S5r = twice("second_slot", UNIT)
        S4, S4r = twice("third_slot", UNIT)
        S2, S2r = twice("scratch", 9 * SLAB)
        S3, S3r = twice("small_scratch", 5 * 512)
        cst = sb("cst", [P, consts.shape[1]])
        lora_w = S3[:, 0:512]
        gate_w2 = S3[:, 512:1024]
        wpool = S3[:, 1024:1536].rearrange("p (g n) -> p g n", g=4)
        gateT_in = S3[:, 1536:2048]
        u_neg = S3[:, 2048:2560]
        vec = sb("vec", [P, 176])
        hot16 = sb("choices", [P, NT, EXPERTS], BF16)
        count16 = sb("count_tables", [P, 2 * P], BF16)

        bank_pair = [ctx.enter_context(nc.psum_tensor(f"bank_pair{i}", [P, 2, 512], F32)) for i in range(4)]
        bank67 = bank_pair[3]

        def bank(i):
            return bank_pair[i // 2][:, i % 2, :]

        def K(name, rows=P):
            return cst[0:rows, at[name][0]:at[name][1]]

        ident = K("ident")

        def slab(n, cols=SLAB):
            if n < 9:
                return S2[:, n * SLAB:n * SLAB + cols]
            if n < 16:
                return S1[:, (n - 10) * SLAB:(n - 10) * SLAB + cols]
            return S4[:, (n - 16) * SLAB:(n - 16) * SLAB + cols]

        def slot(s):
            return (first_slot, S5, S4)[s][:, :] if s < 3 else S1[:, (s - 3) * UNIT:(s - 2) * UNIT]

        hnT = S2[:, 0:UNIT].rearrange("p (c t) -> p c t", c=NC)
        hn = S2[:, UNIT:2 * UNIT].rearrange("p (i d) -> p i d", i=NT)

        cols = {}
        used = [0]

        def column(name, n):
            cols[name] = vec[:, used[0]:used[0] + n]
            used[0] += n

        for nm, n in (("g_mix0", 8), ("g_mix1", 8), ("g_ffn0", 8), ("g_ffn1", 8), ("mu", 14), ("w0", 4), ("a0", 4),
                      ("k_k", 4), ("k_a", 4), ("r_k", 4), ("ln_w", 4), ("ln_b", 4), ("pool_scale", 4), ("subln", 1),
                      ("lq", 4), ("one_minus_mu", 14), ("half_w0", 4), ("half_a0", 4), ("lam", 6), ("subln_s", 1),
                      ("ss", 4), ("ms", 4), ("rstd", 4), ("half_decay", 1), ("sub_eps", 1)):
            column(nm, n)
        vec_loads = [
            (cols["g_mix1"], a["norm_mix"][1].rearrange("(p c) -> p c", c=8)),
            (cols["mu"], a["a_mu"][0].rearrange("(c p) -> p c", p=P)),
            (cols["w0"], a["a_w0"][0].rearrange("(c p) -> p c", p=P)),
            (cols["a0"], a["a_a0"][0].rearrange("(c p) -> p c", p=P)),
            (cols["k_k"], a["a_k_k"][0].rearrange("(c p) -> p c", p=P)),
            (cols["k_a"], a["a_k_a"][0].rearrange("(c p) -> p c", p=P)),
            (cols["r_k"], a["a_r_k"][0].rearrange("(c h) n -> (h n) c", h=2)),
            (cols["ln_w"], a["a_ln_w"][0].rearrange("(c p) -> p c", p=P)),
            (cols["ln_b"], a["a_ln_b"][0].rearrange("(c p) -> p c", p=P)),
            (cols["pool_scale"], a["b_pool_scale"][0].rearrange("(c p) -> p c", p=P)),
            (cols["subln"], a["c_subln"].rearrange("o p -> p o")),
            (cols["lq"][0:64, 0:1], a["c_lambda_q1"].rearrange("o p -> p o")),
            (cols["lq"][0:64, 1:2], a["c_lambda_k1"].rearrange("o p -> p o")),
            (cols["lq"][0:64, 2:3], a["c_lambda_q2"].rearrange("o p -> p o")),
            (cols["lq"][0:64, 3:4], a["c_lambda_k2"].rearrange("o p -> p o")),
            (lora_w[0:64, :], a["a_w2"][0]),
            (lora_w[64:128, :], a["a_a2"][0]),
            (gate_w2[:, :], a["a_g2"][0]),
            (cols["g_ffn0"], a["norm_ffn"][0].rearrange("(p c) -> p c", c=8)),
            (cols["g_ffn1"], a["norm_ffn"][1].rearrange("(p c) -> p c", c=8)),
            (wpool[:, :, :], a["b_w_pool"][0].rearrange("g c d -> c g d")),
        ]

        s_x = sem("x_loaded")
        s_cst = sem("constants_loaded")
        s_vec = sem("vectors_loaded")
        s_zero = sem("zeros_made")
        s_zrows = sem("rows_zeroed")
        s_full = [sem(f"slot_full{i}") for i in range(6)]
        s_dve = sem("vector_order")
        s_act = sem("scalar_order")
        s_pool = sem("pool_order")
        s_ss = sem("square_sums")
        s_rstd = sem("rstd_made")
        s_hn = sem("rows_normed")
        s_tr = sem("norm_transposed")
        s_trv = sem("norm_evac_vector")
        s_tra = sem("norm_evac_scalar")
        s_proj = sem("proj_done")
        s_sh = sem("shift_part_made")
        s_z = sem("shifted_made")
        s_tanh = sem("lora_inner_made")
        s_lora = sem("lora_mm")
        s_wdec = sem("decay_made")
        s_am = sem("iclr_tanh_made")
        s_sq = sem("k_squares_made")
        s_hsum = sem("head_sums")
        s_hroot = sem("head_roots")
        s_hinv = sem("head_inverse")
        s_hb = sem("head_spread_mm")
        s_kk = sem("kk_made")
        s_rkp = sem("rk_products")
        s_rs = sem("bonus_sum_copied")
        s_bon = sem("bonus_made")
        s_prep = sem("prep_made")
        s_prepp = sem("prep_pool_made")
        s_u = sem("pool_input_copied")
        s_win = sem("window_sums")
        s_pd = sem("pool_diff")
        s_pmm = sem("pool_mm")
        s_yb = sem("pool_out")
        s_tt = sem("token_transposed")
        s_tev = sem("token_evac_vector")
        s_tea = sem("token_evac_scalar")
        s_gm = sem("gram_mm")
        s_gv = sem("gram_masked")
        s_jb = sem("join_blocks")
        s_jx = sem("join_x_mm")
        s_jxa = sem("join_x_copied")
        s_jt = sem("join_t_mm")
        s_jtv = sem("join_t_updated")
        s_lx = sem("ak_v_mm")
        s_lxa = sem("ak_v_copied")
        s_lw = sem("w_mm")
        s_lwa = sem("w_copied")
        s_lu = sem("uv_mm")
        s_luv = sem("uv_copied")
        s_um = sem("u_mm")
        s_ua = sem("u_made")
        s_y0m = sem("y_state_part_mm")
        s_sm = sem("state_mm")
        s_sv = sem("state_made")
        s_ym = sem("y_mm")
        s_ya = sem("y_copied")
        s_gn = sem("gn_mm")
        s_gnv = sem("gn_vector")
        s_gna = sem("gn_scalar")
        s_g = sem("gate_made")
        s_gmm = sem("gate_out_mm")
        s_yav = sem("ya_made")
        s_om = sem("out_mm")
        s_res = sem("residual_added")
        s_rw = sem("router_weights")
        s_lg = sem("logits_mm")
        s_lgc = sem("logits_copied")
        s_rt = sem("router_vector")
        s_re = sem("router_exp")
        s_oh = sem("choices_made")
        s_rk = sem("ranks_mm")
        s_slot = sem("slots_made")
        s_disp = sem("rows_dispatched")
        s_rows = [sem(f"rows_loaded{i}") for i in range(2)]
        s_xt = sem("block_transposed")
        s_xr = sem("block_rounded")
        s_xl = sem("block_rest")
        s_wr = sem("weights_rounded")
        s_wl = sem("weights_rest_vector")
        s_wlp = sem("weights_rest_pool")
        s_wu = sem("split_weights_used")
        s_gate = sem("gate_mm")
        s_th = sem("gate_tanh")
        s_h1 = sem("gate_used")
        s_up = sem("up_mm")
        s_h = sem("hidden_made")
        s_ht = sem("hidden_transposed")
        s_hr = sem("hidden_rounded")
        s_hl = sem("hidden_rest")
        s_down = sem("down_mm")
        s_y0 = sem("expert_out_scalar")
        s_y1 = sem("expert_out_vector")
        s_yw = [sem(f"expert_out_written{i}") for i in range(2)]
        s_ov = [{k: sem(f"extra{l}_{k}") for k in ("w", "rows", "pe", "dve", "act", "written")} for l in range(2)]
        EXTRA_MARKS = {"xt": ("pe", 4, 1), "up": ("pe", 4, 2), "ht": ("pe", 4, 3), "down": ("pe", 4, 4),
                       "xl": ("dve", 5, 1), "h1": ("dve", 5, 2), "h": ("dve", 5, 3), "hl": ("dve", 5, 4), "y1": ("dve", 5, 5),
                       "xr": ("act", 4, 1), "th": ("act", 4, 2), "hr": ("act", 4, 3), "y0": ("act", 4, 4)}

        def wait_extra(eng, l, what, b):
            name, per, at_ = EXTRA_MARKS[what]
            eng.wait_ge(s_ov[l][name], b * per + at_)

        s_got = [sem(f"expert_out_gathered{i}") for i in range(NT)]
        s_comb = sem("combined")
        s_rope = sem("rope_loaded")
        s_lam = sem("lambda_steps")
        s_lamm = sem("lambda_mm")
        s_qm = sem("qk_mm")
        s_qa = sem("qk_copied")
        s_rm = sem("rot_mm")
        s_qv = sem("qk_roped")
        s_vm = sem("v_mm")
        s_va = sem("v_copied")
        s_cr = sem("chunk_rounded")
        s_cl = sem("chunk_rest")
        s_clp = sem("chunk_rest_pool")
        s_yr = sem("y_rounded")
        s_yl = sem("y_rest")
        s_ybl = sem("pool_out_rest")
        s_gmv = sem("gate_copied")
        s_cu = sem("chunk_used")
        s_or = sem("o_rounded")
        s_ol = sem("o_rest")
        s_sc = sem("scores_mm")
        s_mx = sem("scores_max")
        s_ex = sem("scores_exp")
        s_pr = sem("probs_made")
        s_pt = sem("probs_transposed")
        s_pta = sem("probs_evac")
        s_ov_ = sem("values_mm")
        s_oc = sem("values_copied")
        s_osq = sem("o_squares")
        s_osm = sem("o_mean_mm")
        s_ort = sem("o_root")
        s_oi = sem("o_inverse")
        s_on = sem("o_normed")
        s_fnb = sem("final_weight_mm")
        s_fin = sem("final_rows")
        s_out = sem("stored")

        n_vec = 16 * len(vec_loads)
        n_zero = SLOTS // TB // 2 + EXTRA // 2

        A_SLOTS = [1] + [0] * 6
        C_SLOTS = [0, 1, 0, 1, 0, 1, 0, 1]
        before = {"A": [0] * 6}
        before["moe0"] = [A_SLOTS.count(s) for s in range(6)]
        before["C"] = [n + EXPERTS // 2 for n in before["moe0"]]
        before["moe1"] = [n + C_SLOTS.count(s) for s, n in enumerate(before["C"])]

        def use(phase, slots, u):
            return before[phase][slots[u]] + slots[:u + 1].count(slots[u])

        wA = a["a_w_in"][0].rearrange("(p c) n -> p c n", c=NC)
        A_COLS = [(1536, 1792), (512, 1024), (0, 512), (1792, 2304), (1024, 1536)]
        A_SRC = [wA[:, :, lo:hi] for lo, hi in A_COLS]
        woA = a["ab_w_out"][0].rearrange("(c p) n -> p c n", p=P)
        A_SRC += [woA[:, :, 0:512], woA[:, :, 512:1024]]
        wC = a["c_w_qkv"][0].rearrange("(p c) n -> p c n", c=NC)
        woC = a["c_w_out"][0].rearrange("(c p) n -> p c n", p=P)
        C_SRC = [wC[:, :, 512 * u:512 * u + 512] for u in range(6)] + [woC[:, :, 0:512], woC[:, :, 512:1024]]

        def a_chunk(g):
            return OUT_ORDER[g % NC] if g >= 5 * NC else g % NC

        def a_weights(g):
            return w_lora_in[:, g, :] if g < NC else slot_w(0)[:, a_chunk(g), :]

        def slot_w(s, c=NC):
            return slot(s).rearrange("p (c n) -> p c n", c=c)

        def pairs(n):
            return slab(n).rearrange("p (j t) -> p j t", j=NPAIR)

        kT, rT, vT, ybT = pairs(4), pairs(5), pairs(6), pairs(7)
        wT, pT, aT, kkT, alT = pairs(16), pairs(17), pairs(10), pairs(11), pairs(12)
        bonT, piT = pairs(13), pairs(16)
        rk_tmp = pairs(8)
        w_lora_in = slab(12).rearrange("p (c n) -> p c n", c=NC)
        zeros = S3[:, 0:256]
        gate = pairs(10)
        v_tok, al_tok, k_tok, b_tok = pairs(0), pairs(1), pairs(14), pairs(11)
        shift = [slab(2)[:, 520 * i:520 * i + T + 1] for i in range(2)]
        z_l0 = slab(2)[:, 1040:1040 + T]
        PAD = 16
        upad = [slab(3)[:, 528 * i:528 * i + PAD + T] for i in range(3)]
        sq_tmp = [slab(15)[:, T * i:T * i + T] for i in range(2)]
        scan_in = slab(15)[:, 1024:1024 + T]
        hs = slab(15)[0:H, 1536:1536 + T]
        wk = [{}, {}]
        for q in range(2):
            for n, name in enumerate(("Tm", "TT", "X", "LT", "Bm", "AK")):
                k = q * 6 + n
                wk[q][name] = slab((2, 3, 15)[k // 4])[:, (k % 4) * 512:(k % 4) * 512 + 512]
        keep = [{name: slab(n)[:, k * 512:k * 512 + 512] for k, name in enumerate(("RK", "RB", "UV", "WT"))}
                for n in (8, 16, 17, 8)]
        yT = vT
        hnR = S2r[:, 0:UNIT].rearrange("p (c t) -> p c t", c=NC)
        hnL_A = S1r[:, 3 * SLAB:5 * SLAB].rearrange("p (c t) -> p c t", c=NC)
        yR, yL = (S2r[:, k * UNIT:(k + 1) * UNIT].rearrange("p (c t) -> p c t", c=NC) for k in (0, 1))
        aR = [S5r[:, 1024 * i:1024 * i + 512] for i in range(4)]
        aL = [S5r[:, 1024 * i + 512:1024 * i + 1024] for i in range(4)]
        A_CHUNKS = 56
        OUT_ORDER = [4, 5, 6, 7, 0, 1, 2, 3]
        yc_sq = slab(16)
        ST = [sb(f"state{i}", [P, NPAIR, N]) for i in range(2)]
        STs = sb("state_sum", [P, NPAIR, N])
        pc = sb("chunk_decay", [P, NPAIR, NCH])

        def heads(ap):
            if len(ap.shape) == 3:
                return ap.rearrange("p a (j n) -> p a j n", j=NPAIR)
            return ap.rearrange("p (a j n) -> p a j n", a=2, j=NPAIR)

        def per_head(ap):
            return ap.unsqueeze(1).unsqueeze(1).to_broadcast([P, 2, NPAIR, C])

        def gram_place(q, k):
            n = 3 * (q % 2) + k // 2
            return bank_pair[3 - n % 4], 256 * (k % 2)

        def both(ap):
            return ap.rearrange("p (a m) -> p a m", a=2)

        o = 2 * UNIT
        rows = [S2[0:TB, o + D * i:o + D * i + D] for i in range(2)]
        o += 2 * D
        x_at = o
        o += 4 * NC * TB
        hid = [S2[0:TB, o + FF * i:o + FF * i + FF] for i in range(2)]
        tab_at = o
        o += 2 * FF
        yrow = [S2[0:TB, o + D * i:o + D * i + D] for i in range(2)]
        rt0 = o
        o += 2 * D
        rw_at = 9 * SLAB - 1280 - NC * 36
        w_router = S2[:, rw_at:rw_at + NC * 36].rearrange("p (c n) -> p c n", c=NC)
        assert o <= rw_at

        def split_views(buf, start, c):
            return [[buf[:, start + c * TB * (2 * i + k):start + c * TB * (2 * i + k + 1)].rearrange("p (c t) -> p c t", c=c) for i in range(2)]
                    for k in range(2)]

        xR, xL = split_views(S2r, x_at, NC)
        hR, hL = split_views(S3r, 0, 4)
        th = [S3[0:TB, 16 * TB + FF * i:16 * TB + FF * i + FF] for i in range(2)]
        g_row = S3[:, 16 * TB:16 * TB + D]
        b_row = S3[:, 16 * TB + D:16 * TB + D + 36]
        assert 16 * TB + D + 36 <= 5 * 512
        lgT = S2[0:36, x_at:x_at + T]
        GROUP = UNIT // 4
        wR = [S2r[:, 2 * GROUP * j:2 * GROUP * j + GROUP] for j in range(4)]
        wL = [S2r[:, 2 * GROUP * j + GROUP:2 * GROUP * j + 2 * GROUP] for j in range(4)]
        BATCHES = 3 * EXPERTS

        def q_gate(e):
            return 0 if isinstance(e, int) and e == 0 else 3 * e - 1

        def q_up(e):
            return 1 if isinstance(e, int) and e == 0 else 3 * e

        def q_down(e):
            return BATCHES - 1 if isinstance(e, int) and e == EXPERTS - 1 else 3 * e + 4

        got = [[S2[:, k * UNIT + D * i:k * UNIT + D * i + D] for i in range(NT)] for k in range(2)]
        e2_at = rt0 + ROUTER_E2
        slot_ix = sb("slot_ix", [P, 2, NT], I32)
        extra_tab = sb("extra_tab", [1, 1 + EXTRA], I32)
        wts = sb("wts", [P, 2, NT])

        rope_sb = S2[:, 9 * SLAB - 1280:9 * SLAB]
        cosT, sinT = rope_sb[:, 0:T], rope_sb[:, T:2 * T]
        swap, mask = rope_sb[:, 2 * T:2 * T + P], rope_sb[:, 2 * T + P:2 * T + 2 * P]
        v_att = hn
        kaT = S2[:, 3 * UNIT:4 * UNIT].rearrange("p (h t) -> p h t", h=H)
        q_half = [S2[:, 2 * UNIT:3 * UNIT].rearrange("p (h t) -> p h t", h=H), S1[:, UNIT:2 * UNIT].rearrange("p (h t) -> p h t", h=H)]
        oT = S1[:, 0:UNIT].rearrange("p (h t) -> p h t", h=H)
        o = 2 * UNIT
        raw = [S1[:, o + T * i:o + T * i + T] for i in range(4)]
        rot = [S1[:, o + 2048 + T * i:o + 2048 + T * i + T] for i in range(4)]
        pe_ = [S1[:, o + 1024 * i:o + 1024 * i + 1024].rearrange("p (c k) -> p c k", c=2) for i in range(2)]
        prob = [S1[:, o + 2048 + T * i:o + 2048 + T * i + T] for i in range(2)]
        probT = [S1[:, o + 3072 + T * i:o + 3072 + T * i + T] for i in range(2)]
        osq = S2[:, 0:UNIT].rearrange("p (h t) -> p h t", h=H)
        hnL = S1r[:, 0:UNIT].rearrange("p (c t) -> p c t", c=NC)
        oR, oL = (S2r[:, k * UNIT:(k + 1) * UNIT].rearrange("p (c t) -> p c t", c=NC) for k in (2, 3))
        cR = [S4r[:, 1024 * i:1024 * i + 512] for i in range(4)]
        cL = [S4r[:, 1024 * i + 512:1024 * i + 1024] for i in range(4)]
        o_inv = prob[0][0:H, :]
        mask16 = sb("mask16", [P, 2 * P], BF16)
        stat = sb("stat", [P, 2, 8])
        fn_row = S2[0:1, 2 * UNIT + D:2 * UNIT + 2 * D]
        fin = [S2[:, k * D:k * D + D] for k in range(NT)]

        block = ctx.enter_context(nc.Block())

        TILES = [(0, 0, 12), (0, 128, 13)] + [(1, 128 * j, 4 + j) for j in range(4)] \
            + [(2, 128 * j, j) for j in range(4)] + [(3, 128 * j, None) for j in range(4)] \
            + [(4, 128 * j, 8 + j) for j in range(4)]
        Z_OUT = [z_l0, gateT_in[:, :]] + [kT[:, j, :] for j in range(4)] + [rT[:, j, :] for j in range(4)] \
            + [None] * 4 + [vT[:, j, :] for j in range(4)]

        def z_index(m):
            return m if m < 10 else m - 4
        LEVELS = (2, 4, 8, 16, 32)
        n_setup = 15
        NL = len(LEVELS)

        def evac_before(n):
            return 4 * n + (4 if n > 0 else 0) + (4 if n > 2 else 0)

        def rstd_before(n):
            return n + (3 if n > 2 else 0)

        def moe_before(l, s):
            return before[f"moe{l}"][s]

        def experts_sp(sp, l):

            def load_one(e, half, n, k):
                srcs = [a["moe_w_gate"][l, bass.ds(e, 1)].rearrange("o (p c) n -> (o p) c n", c=NC),
                        a["moe_w_up"][l, bass.ds(e, 1)].rearrange("o (p c) n -> (o p) c n", c=NC),
                        a["moe_w_down"][l, bass.ds(e, 1)].rearrange("o (p c) n -> (o p) c n", c=4)]
                s = 3 * half + k
                if not (isinstance(n, int) and n == 0):
                    q = (q_gate, q_up, q_down)[k]
                    sp.wait_ge(s_wl, 3 * (BATCHES * l + q(e - 2) + 1))
                    sp.wait_ge(s_wlp, BATCHES * l + q(e - 2) + 1)
                sp.dma_start(slot_w(s, NC if k < 2 else 4), srcs[k]).then_inc(s_full[s], 16)

            def load_expert(e, half, n):
                for k in range(3):
                    load_one(e, half, n, k)

            if l == 0:
                sp.wait_ge(s_yav, 4)
                load_one(0, 0, 0, 2)
                for k in range(3):
                    load_one(1, 1, 0, k)
                sp.wait_ge(s_clp, A_CHUNKS)
                load_one(0, 0, 0, 0)
                sp.wait_ge(s_om, 8)
                load_one(0, 0, 0, 1)
            else:
                sp.wait_ge(s_ol, 8)
                for k in range(3):
                    load_one(1, 1, 0, k)
                sp.wait_ge(s_cl, 56)
                load_one(0, 0, 0, 0)
                sp.wait_ge(s_cl, 64)
                load_one(0, 0, 0, 1)
                sp.wait_ge(s_om, 16)
                load_one(0, 0, 0, 2)
            for e in (2, 3):
                load_expert(e, e % 2, 1)
            with sp.Fori(2, EXPERTS // 2) as i:
                load_expert(2 * i, 0, i)
                load_expert(2 * i + 1, 1, i)

        @block.sync
        def _(sp):
            for i in range(NT):
                sp.dma_start(x_sb[:, i, :], a["x"][0, P * i:P * i + P, :]).then_inc(s_x, 16)
            sp.dma_start(cst[:, :], consts).then_inc(s_cst, 16)
            sp.dma_start(cols["g_mix0"], a["norm_mix"][0].rearrange("(p c) -> p c", c=8)).then_inc(s_cst, 16)

            used_A = [(s_clp, 8 * (u + 1)) for u in range(7)]
            used_C = [(s_cl, 8 * (u + 1)) for u in range(8)] 

            def load_unit(used_up, slots, src, u):
                s = slots[u]
                for v in range(u - 1, -1, -1):
                    if slots[v] == s:
                        sp.wait_ge(*used_up[v])
                        break
                dst = w_lora_in if src is A_SRC and u == 0 else slot_w(s)
                sp.dma_start(dst, src[u]).then_inc(s_full[s], 16)

            for u in range(7):
                if u == 1:
                    for dst, src in vec_loads:
                        sp.dma_start(dst, src, allow_slow_non_contiguous=True).then_inc(s_vec, 16)
                load_unit(used_A, A_SLOTS, A_SRC, u)
            experts_sp(sp, 0)
            sp.dma_start(rope_sb, ropes).then_inc(s_rope, 16)
            sp.wait_ge(s_wl, 3 * (q_up(EXPERTS - 2) + 1))
            sp.wait_ge(s_wlp, q_up(EXPERTS - 2) + 1)
            for u in range(8):
                load_unit(used_C, C_SLOTS, C_SRC, u)
            experts_sp(sp, 1)
            sp.wait_ge(s_y1, 64)
            sp.dma_start(fn_row, a["final_norm"].rearrange("(o d) -> o d", o=1)).then_inc(s_rope, 16)
            for i in range(NT):
                sp.wait_ge(s_fin, i + 1)
                sp.dma_start(out[0, P * i:P * i + P, :], fin[i]).then_inc(s_out, 16)
            sp.wait_ge(s_out, 16 * NT)

        @block.tensor
        def _(pe):
            def norm_transposes(n):
                cut = (hn if n % 2 == 0 else x_sb).rearrange("p i (q c) -> p i c q", c=NC)
                for c in range(NC):
                    if c >= 4:
                        if n in (0, 2):
                            pe.wait_ge(s_trv, evac_before(n) + c - 3)
                        else:
                            pe.wait_ge(s_trv if c % 2 == 0 else s_tra, evac_before(n) + (c - 4) // 2 + 1)
                    for i in range(NT):
                        if c == 0 and n % 2 == 0:
                            pe.wait_ge(s_hn, 4 * n + i + 1)
                        elif c == 0:
                            pe.wait_ge(s_res, 4 * n + i + 1)
                        ins = pe.transpose(bank(c % 4)[:, P * i:P * i + P], cut[:, i, c, :], ident)
                    ins.then_inc(s_tr, 1)
                if n > 0:
                    pe.wait_ge(s_trv, evac_before(n + 1))
                    pe.wait_ge(s_tra, evac_before(n + 1))

            def quarter_mms(out_of, l_of, r_of):
                ins = None
                for h0 in range(0, H, 2):
                    for flip in range(2):
                        for s in range(2):
                            h = h0 + (s ^ flip)
                            ins = pe.matmul(out_of(h, s), l_of(h, s), r_of(h, s), start=True, stop=True)
                return ins

            pe.wait_ge(s_cst, 32)
            norm_transposes(0)

            def split_mms(o_, g, xr, xl, t, channels, buf):
                first, last = g % NC == 0, g % NC == NC - 1
                r, rest = (b[g % 4] for b in buf)
                tile_ = slice(P * t, P * t + P)
                if channels:
                    terms = ((r[:, tile_], xr), (r[:, tile_], xl), (rest[:, tile_], xr))
                else:
                    terms = ((xr[:, tile_], r), (xr[:, tile_], rest), (xl[:, tile_], r))
                for k, (l_, r_) in enumerate(terms):
                    ins = pe.matmul(o_, l_, r_, start=(first and k == 0), stop=(last and k == 2))
                return ins

            def project(u):
                tiles_ = [m for m in range(len(TILES)) if TILES[m][0] == u]
                for c in range(NC):
                    if u == 0:
                        pe.wait_ge(s_trv, c + 1)
                    pe.wait_ge(s_clp, 8 * u + c + 1)
                    for t, m in enumerate(tiles_):
                        if c == 0 and m >= 4:
                            if m < 14:
                                pe.wait_ge(s_z, m - 3)
                            else:
                                pe.wait_ge(s_u, m - 13)
                        ins = split_mms(bank(4 + m % 4), 8 * u + c, hnR[:, c, :], hnL_A[:, c, :], t, True, (aR, aL))
                        if c == NC - 1:
                            ins.then_inc(s_proj, 1)
                    if c == NC - 1:
                        pe.wait_ge(s_proj, tiles_[-1] + 1)
                        pe.nop().then_inc(s_cu, 1)
                    else:
                        ins.then_inc(s_cu, 1)

            project(0)
            project(1)
            pe.wait_ge(s_vec, n_vec)
            pe.wait_ge(s_tanh, 1)
            for j in range(NPAIR):
                if j >= 2:
                    pe.wait_ge(s_am, j - 1)
                b = 2 * (j % 2)
                pe.matmul(bank(b), lora_w[0:64, P * j:P * j + P], z_l0[0:64, :], start=True, stop=True)
                pe.matmul(bank(b + 1), lora_w[64:128, P * j:P * j + P], z_l0[64:128, :], start=True, stop=True).then_inc(s_lora, 1)
            project(2)
            pe.wait_ge(s_am, 4)
            for j in range(NPAIR):
                pe.wait_ge(s_sq, j + 1)
                pe.matmul(bank(0)[0:H, :], K("head_sel")[:, H * j:H * j + H], sq_tmp[j % 2], start=(j == 0), stop=(j == 3)).then_inc(s_hsum, 1)
            project(3)
            pe.wait_ge(s_hinv, 1)
            for j in range(NPAIR):
                pe.matmul(bank(j), K("head_spread", H)[:, P * j:P * j + P], hs, start=True, stop=True).then_inc(s_hb, 1)
            project(4)
            pe.wait_ge(s_rkp, 4)
            pe.wait_ge(s_kk, 4)
            for j in range(NPAIR):
                ins = pe.matmul(bank(0)[0:H, :], K("head_sel")[:, H * j:H * j + H], rk_tmp[:, j, :], start=(j == 0), stop=(j == 3))
            ins.then_inc(s_hsum, 1)
            def pooled(g):
                pe.wait_ge(s_pd, g + 1)
                pe.wait_ge(s_z, 11 + g)
                pe.matmul(bank(4 + (18 + g) % 4), wpool[:, g, :], ybT[:, g, :], start=True, stop=True).then_inc(s_pmm, 1)

            for g in range(3):
                pooled(g)
            pe.wait_ge(s_rs, 1)
            for j in range(NPAIR):
                pe.matmul(bank(j), K("head_spread", H)[:, P * j:P * j + P], hs, start=True, stop=True).then_inc(s_hb, 1)
            pooled(3)

            pe.wait_ge(s_prep, 4)
            pe.wait_ge(s_bon, 4)
            pe.wait_ge(s_yb, 4)
            for g in range(16):
                q, arr = g // 4, (vT, alT, kT, aT)[g % 4]
                if g >= 8:
                    pe.wait_ge(s_tev if g % 2 == 0 else s_tea, (g - 8) // 2 + 1)
                for j in range(NPAIR):
                    ins = pe.transpose(bank(g % 8)[:, P * j:P * j + P], arr[:, j, P * q:P * q + P], ident)
                ins.then_inc(s_tt, 1)
            pe.wait_ge(s_tev, 8)
            pe.wait_ge(s_tea, 8)

            def ch(arr, h, c):
                po = N * (h % 2)
                return arr[po:po + N, h // 2, C * c:C * c + C]

            def mat(ap, h, s):
                o_ = C * (NPAIR * (h % 2) + h // 2)
                return ap[C * s:C * s + C, o_:o_ + C]

            def half_mat(ap, h, s, r, c):
                o_ = C * (NPAIR * (h % 2) + h // 2) + C // 2 * c
                return ap[C * s + C // 2 * r:C * s + C // 2 * (r + 1), o_:o_ + C // 2]

            def tok(ap, h, s):
                return ap[C * s:C * s + C, N * h:N * h + N]

            def local(pr):
                for b in range(2):
                    q = 2 * pr + b
                    for k, (l, r) in enumerate(((aT, alT), (alT, aT), (kT, alT), (kT, rT), (aT, rT))):
                        if b == 1 and k // 2 >= 1:
                            pe.wait_ge(s_gv, 5 * (q - 1) + 2 if k // 2 == 1 else 5 * (q - 1) + 4)
                        bk, o_ = gram_place(q, k)
                        quarter_mms(lambda h, s: bk[C * s:C * s + C, h % 2, o_ + C * (h // 2):o_ + C * (h // 2) + C], lambda h, s: ch(l, h, 2 * q + s), lambda h, s: ch(r, h, 2 * q + s)).then_inc(s_gm, 1)
                pe.wait_ge(s_gv, 10 * pr + 10)
                for lv in range(NL):
                    for b in range(2):
                        q, w, n = 2 * pr + b, wk[b], 2 * NL * pr + 2 * lv + b
                        pe.wait_ge(s_jb, n + 1)
                        if lv > 0:
                            pe.wait_ge(s_jtv, n - 1)
                        if lv < NL - 1:
                            quarter_mms(lambda h, s: mat(bank(b), h, s), lambda h, s: mat(w["Bm"], h, s), lambda h, s: mat(w["Tm"], h, s)).then_inc(s_jx, 1)
                        else:
                            quarter_mms(lambda h, s: half_mat(bank(b), h, s, 1, 0), lambda h, s: half_mat(w["Bm"], h, s, 0, 1), lambda h, s: half_mat(w["Tm"], h, s, 0, 0)).then_inc(s_jx, 1)
                    for b in range(2):
                        q, w, n = 2 * pr + b, wk[b], 2 * NL * pr + 2 * lv + b
                        pe.wait_ge(s_jxa, n + 1)
                        if lv < NL - 2:
                            quarter_mms(lambda h, s: mat(bank(2 + b), h, s), lambda h, s: mat(w["TT"], h, s), lambda h, s: mat(w["X"], h, s))
                        elif lv == NL - 2:
                            quarter_mms(lambda h, s: half_mat(bank(2 + b), h, s, 0, 0), lambda h, s: half_mat(w["TT"], h, s, 0, 0), lambda h, s: half_mat(w["X"], h, s, 0, 0))
                        if lv < NL - 1:
                            quarter_mms(lambda h, s: mat(bank(4 + b), h, s), lambda h, s: mat(w["X"], h, s), lambda h, s: mat(w["TT"], h, s)).then_inc(s_jt, 1)
                        else:
                            quarter_mms(lambda h, s: half_mat(bank(4 + b), h, s, 0, 1), lambda h, s: half_mat(w["X"], h, s, 1, 0), lambda h, s: half_mat(w["TT"], h, s, 1, 1)).then_inc(s_jt, 1)
                for b in range(2):
                    q, w = 2 * pr + b, wk[b]
                    pe.wait_ge(s_jtv, 2 * NL * pr + 2 * NL - 1 + b)
                    quarter_mms(lambda h, s: mat(bank(b), h, s), lambda h, s: mat(w["AK"], h, s), lambda h, s: tok(v_tok[:, q, :], h, s)).then_inc(s_lx, 1)
                    ob = bank_pair[1 + 2 * b]
                    quarter_mms(lambda h, s: ob[N * (h % 2):N * (h % 2) + N, s, C * (h // 2):C * (h // 2) + C], lambda h, s: tok(al_tok[:, q, :], h, s), lambda h, s: mat(w["TT"], h, s)).then_inc(s_lw, 1)
                for b in range(2):
                    q, w = 2 * pr + b, wk[b]
                    pe.wait_ge(s_lxa, q + 1)
                    quarter_mms(lambda h, s: mat(bank(4 + b), h, s), lambda h, s: mat(w["TT"], h, s), lambda h, s: mat(w["X"], h, s)).then_inc(s_lu, 1)

            def sequence(c):
                q, s, kp = c // 2, c % 2, keep[c // 2]
                st = ST[c % 2]
                pe.wait_ge(s_sv, c + 1)
                wt = kp["WT"].rearrange("p (s j t) -> p s j t", s=2, j=NPAIR)
                for h in range(H):
                    po = N * (h % 2)
                    ins = pe.matmul(bank_pair[3][C * s:C * s + C, h % 2, C * (h // 2):C * (h // 2) + C], wt[po:po + N, s, h // 2, :],
                                    st[po:po + N, h // 2, :], start=True, stop=True)
                ins.then_inc(s_um, 1)
                if c >= 2:
                    pe.wait_ge(s_ya, c - 1)
                y_at = lambda h: bank(s)[N * (h % 2):N * (h % 2) + N, C * (h // 2):C * (h // 2) + C]
                for h in range(H):
                    ins = pe.matmul(y_at(h), st[N * (h % 2):N * (h % 2) + N, h // 2, :], ch(rT, h, c), start=(h < 2), stop=False, skip_group_check=True)
                ins.then_inc(s_y0m, 1)
                pe.wait_ge(s_ua, c + 1)
                for h in range(H):
                    po = N * (h % 2)
                    o_ = bank(5)[po:po + N, N * (h // 2):N * (h // 2) + N]
                    pe.matmul(o_, tok(k_tok[:, q, :], h, s), tok(v_tok[:, q, :], h, s), start=True, stop=False)
                    ins = pe.matmul(o_, tok(b_tok[:, q, :], h, s), mat(u_neg, h, s), start=False, stop=True)
                ins.then_inc(s_sm, 1)
                pe.wait_ge(s_y0m, c + 1)
                for h in range(H):
                    pe.matmul(y_at(h), tok(v_tok[:, q, :], h, s), mat(kp["RK"], h, s), start=False, stop=False, skip_group_check=True)
                    ins = pe.matmul(y_at(h), mat(u_neg, h, s), mat(kp["RB"], h, s), start=False, stop=(h >= 6), skip_group_check=True)
                ins.then_inc(s_ym, 1)

            pe.wait_ge(s_prepp, 4)
            local(0)
            pe.wait_ge(s_luv, 2)
            pe.wait_ge(s_lwa, 2)
            sequence(0)
            sequence(1)
            pe.wait_ge(s_ya, 2)
            pe.wait_ge(s_sv, 3)
            local(1)
            pe.wait_ge(s_luv, 4)
            pe.wait_ge(s_lwa, 4)
            pe.wait_ge(s_g, 1)
            for j in range(NPAIR):
                if j >= 2:
                    pe.wait_ge(s_gmv, j - 1)
                pe.matmul(bank(2 + j % 2), gate_w2[:, P * j:P * j + P], gateT_in[:, :], start=True, stop=True).then_inc(s_gmm, 1)
            for c in range(2, NCH):
                sequence(c)
            pe.wait_ge(s_ya, NCH)
            pe.wait_ge(s_gmv, 4)
            for j in range(NPAIR):
                pe.matmul(bank(j), K("head_mean"), yT[:, j, :], start=True, stop=True).then_inc(s_gn, 1)
            pe.wait_ge(s_sv, NCH + 1)

            def out_chunk(half, n):
                c, g = OUT_ORDER[n], 8 * (5 + half) + n
                pe.wait_ge(s_clp, g + 1)
                if c >= 4:
                    pe.wait_ge(s_ybl, c - 3)
                else:
                    pe.wait_ge(s_yl, c + 1)
                for i in range(NT):
                    ins = split_mms(bank(4 * (1 - half) + i), g, yR[:, c, :], yL[:, c, :], i, False, (aR, aL))
                    if n == NC - 1:
                        ins.then_inc(s_om, 1)
                if n < NC - 1:
                    ins.then_inc(s_cu, 1)
                else:
                    pe.wait_ge(s_om, 4 * half + 4)
                    pe.nop().then_inc(s_cu, 1)

            out_chunk(0, 0)
            pe.wait_ge(s_gnv, 4)
            for j in range(NPAIR):
                pe.wait_ge(s_gna, j + 1)
                ins = pe.matmul(bank(0)[0:H, :], K("head_sel")[:, H * j:H * j + H], yc_sq[:, T * j:T * j + T], start=(j == 0), stop=(j == 3))
            ins.then_inc(s_gn, 1)
            for n in range(1, 3):
                out_chunk(0, n)
            pe.wait_ge(s_gnv, 6)
            for j in range(NPAIR):
                pe.matmul(bank(j), K("head_spread", H)[:, P * j:P * j + P], hs, start=True, stop=True).then_inc(s_gn, 1)
            for n in range(3, NC):
                out_chunk(0, n)
            for n in range(NC):
                out_chunk(1, n)

            def router_mms(l):
                pe.wait_ge(s_rw, 80 * (l + 1))
                for c in range(NC):
                    ins = pe.matmul(bank(4)[0:36, :], w_router[:, c, :], hnT[:, c, :], start=(c == 0), stop=(c == NC - 1))
                ins.then_inc(s_lg, 1)
                pe.wait_ge(s_lgc, l + 1)
                for i in range(NT):
                    ins = pe.transpose(bank(5)[:, 256 + 36 * i:256 + 36 * i + 36], lgT[:, P * i:P * i + P], ident[0:36, 0:36])
                ins.then_inc(s_lg, 1)
                pe.wait_ge(s_oh, l + 1)
                ones_, earlier_ = count16[:, 0:P], count16[:, P:2 * P]
                for i in range(NT):
                    o_ = bank(4)[:, 32 * i:32 * i + 32]
                    for i2 in range(i):
                        pe.matmul(o_, ones_, hot16[:, i2, :], start=(i2 == 0), stop=False)
                    pe.matmul(o_, earlier_, hot16[:, i, :], start=(i == 0), stop=True)
                for i in range(NT):
                    ins = pe.matmul(bank(4)[:, 128:160], ones_, hot16[:, i, :], start=(i == 0), stop=(i == 3))
                ins.then_inc(s_rk, 1)

            XTB, GB, UB, HTB, YB = bank67, bank(0), bank(1), bank(2), (bank(3), bank(4))

            def block_transposes(par):
                cut = rows[par].rearrange("p (q c) -> p c q", c=NC)
                for c in range(NC):
                    ins = pe.transpose(XTB[:, c // 4, TB * (c % 4):TB * (c % 4) + TB], cut[:, c, :], ident[0:TB, 0:TB])
                return ins

            def mm_in(o_, par, q, used_up):
                for j in range(4):
                    wait_split(q, j)
                    for c in (2 * j, 2 * j + 1):
                        r, rest = (w[j][:, 512 * (c % 2):512 * (c % 2) + 512] for w in (wR, wL))
                        pe.matmul(o_[0:TB, :], xR[par][:, c, :], r, start=(c == 0), stop=False)
                        pe.matmul(o_[0:TB, :], xR[par][:, c, :], rest, start=False, stop=False)
                        ins = pe.matmul(o_[0:TB, :], xL[par][:, c, :], r, start=False, stop=(c == NC - 1))
                    ins.then_inc(s_wu, 1)
                pe.wait_ge(s_wu, 4 * q + 4)
                pe.nop().then_inc(used_up, 1)

            def wait_split(q, j):
                if j < 3:
                    pe.wait_ge(s_wl, 3 * q + j + 1)
                else:
                    pe.wait_ge(s_wlp, q + 1)

            def mm_in32(o_, w):
                for c in range(NC):
                    pe.matmul(o_[0:TB, :], xR[0][:, c, :].bitcast(F32), w[:, c, :], start=(c == 0), stop=False)
                    ins = pe.matmul(o_[0:TB, :], xL[0][:, c, :].bitcast(F32), w[:, c, :], start=False, stop=(c == NC - 1))
                return ins

            def hidden_transposes(par):
                cut = hid[par].rearrange("p (q c) -> p c q", c=4)
                for c in range(4):
                    ins = pe.transpose(HTB[:, TB * c:TB * c + TB], cut[:, c, :], ident[0:TB, 0:TB])
                return ins

            def mm_down(par, q, used_up):
                for c in range(4):
                    wait_split(q, c)
                    for half in range(2):
                        o_ = YB[half][0:TB, :]
                        r, rest = (w[c][:, 512 * half:512 * half + 512] for w in (wR, wL))
                        pe.matmul(o_, hR[par][:, c, :], r, start=(c == 0), stop=False)
                        pe.matmul(o_, hR[par][:, c, :], rest, start=False, stop=False)
                        ins = pe.matmul(o_, hL[par][:, c, :], r, start=False, stop=(c == 3))
                    ins.then_inc(s_wu, 1)
                pe.wait_ge(s_wu, 4 * q + 4)
                pe.nop().then_inc(used_up, 1)

            def mm_down32(w):
                for half in range(2):
                    for c in range(4):
                        w_ = w[:, c, 512 * half:512 * half + 512]
                        pe.matmul(YB[half][0:TB, :], hR[0][:, c, :].bitcast(F32), w_, start=(c == 0), stop=False)
                        ins = pe.matmul(YB[half][0:TB, :], hL[0][:, c, :].bitcast(F32), w_, start=False, stop=(c == 3))
                return ins

            def experts(l):
                B = EXPERTS * l

                Q = BATCHES * l

                def step(e, par, n, first=False, last=False):
                    pe.wait_ge(s_xl, B + e + 1)
                    if not (first and l == 0):
                        pe.wait_ge(s_h1, B + e)
                    mm_in(GB, par, Q + q_gate(e), s_gate)
                    if not first:
                        pe.wait_ge(s_h, B + e)
                        hidden_transposes(1 - par).then_inc(s_ht, 1)
                    mm_in(UB, par, Q + q_up(e), s_up)
                    if not last:
                        pe.wait_ge(s_rows[1 - par], 16 * (16 * l + (n + 1 if par == 1 else n) + 1))
                        block_transposes(1 - par).then_inc(s_xt, 1)
                    if not first:
                        down(e, 1 - par, Q + 3 * e + 1)

                def down(e, par, q):
                    pe.wait_ge(s_hl, B + e)
                    if not (l == 0 and isinstance(e, int) and e == 1):
                        pe.wait_ge(s_y0, B + e - 1)
                        pe.wait_ge(s_y1, B + e - 1)
                    mm_down(par, q, s_down)

                pe.wait_ge(s_slot, 4 * l + 4)
                pe.wait_ge(s_rows[0], 16 * (16 * l + 1))
                block_transposes(0).then_inc(s_xt, 1)
                step(0, 0, 0, first=True)
                with pe.Fori(0, EXPERTS // 2 - 1) as i:
                    step(2 * i + 1, 1, i)
                    step(2 * i + 2, 0, i + 1)
                step(EXPERTS - 1, 1, EXPERTS // 2 - 1, last=True)
                pe.wait_ge(s_h, B + EXPERTS)
                hidden_transposes(1).then_inc(s_ht, 1)
                down(EXPERTS, 1, Q + q_down(EXPERTS - 1))
                pe.wait_ge(s_y0, B + EXPERTS)
                pe.wait_ge(s_y1, B + EXPERTS)
                v = s_ov[l]
                n = pe.value_load(extra_tab[0:1, 0:1], min_val=0, max_val=EXTRA)
                with pe.If(n > 0):
                    with pe.Fori(0, n) as b:
                        pe.wait_ge(v["rows"], 16 * b + 16)
                        block_transposes(0).then_inc(v["pe"], 1)
                        wait_extra(pe, l, "xl", b)
                        pe.wait_ge(v["w"], 48 * b + 48)
                        mm_in32(GB, slot_w(3))
                        mm_in32(UB, slot_w(4)).then_inc(v["pe"], 1)
                        wait_extra(pe, l, "h", b)
                        hidden_transposes(0).then_inc(v["pe"], 1)
                        wait_extra(pe, l, "hl", b)
                        mm_down32(slot_w(5, 4)).then_inc(v["pe"], 1)
                        wait_extra(pe, l, "y1", b)
                        wait_extra(pe, l, "y0", b)

            def experts_phase(l):
                norm_transposes(1 + 2 * l)
                router_mms(l)
                experts(l)

            def mixer_c():
                norm_transposes(2)
                pe.wait_ge(s_dve, n_setup)
                pe.matmul(bank(7)[:, 0:2], K("ones", 64), cols["lam"][0:64, 0:2], start=True, stop=True).then_inc(s_lamm, 1)
                for u in range(6):
                    for c in range(NC):
                        pe.wait_ge(s_cl, 8 * u + c + 1)
                        for t in range(4):
                            if c == 0 and u == 1 and t == 3:
                                pe.wait_ge(s_lam, 1)
                            if c == 0 and u >= 2:
                                pe.wait_ge(s_qv, 4 * (u - 2) + t + 1)
                            ins = split_mms(bank(4 * (u % 2) + t), 8 * u + c, hnR[:, c, :], hnL[:, c, :], t, u < 4, (cR, cL))
                            if c == NC - 1:
                                ins.then_inc(s_qm if u < 4 else s_vm, 1)
                        if c == NC - 1:
                            pe.wait_ge(s_qm if u < 4 else s_vm, 4 * u + 4 if u < 4 else 4 * (u - 4) + 4)
                            pe.nop().then_inc(s_cu, 1)
                        else:
                            ins.then_inc(s_cu, 1)
                        if 1 <= u <= 4 and 3 <= c < 7:
                            rotate(4 * (u - 1) + c - 3)
                pe.wait_ge(s_va, 4)
                pe.wait_ge(s_qv, 16)
                for k in range(H * NT + 3):
                    if k < H * NT:
                        scores(k)
                    if k == H * NT:
                        pe.wait_ge(s_ex, 2 * k - 2)
                        for h in range(H - 1):
                            square_sum(h)
                    if 2 <= k < H * NT + 2:
                        if k == 2:
                            pe.wait_ge(s_va, 8)
                        transposes(k - 2)
                    if k >= 3:
                        values(k - 3)
                square_sum(H - 1).then_inc(s_osm, 1)
                pe.wait_ge(s_oi, 1)
                pe.wait_ge(s_oc, H)
                for h in range(H):
                    if h >= 4:
                        pe.wait_ge(s_on, h - 3)
                    pe.matmul(bank(4 + h % 4), ident[0:H, h:h + 1].to_broadcast([H, P]), o_inv, start=True, stop=True).then_inc(s_osm, 1)
                for half in range(2):
                    for c in range(NC):
                        g = 8 * (6 + half) + c
                        pe.wait_ge(s_cl, g + 1)
                        pe.wait_ge(s_ol, c + 1)
                        if half == 1:
                            pe.wait_ge(s_on, 8)
                        for i in range(NT):
                            ins = split_mms(bank(4 * half + i), g, oR[:, c, :], oL[:, c, :], i, False, (cR, cL))
                            if c == NC - 1:
                                ins.then_inc(s_om, 1)
                        if c < NC - 1:
                            ins.then_inc(s_cu, 1)
                        elif half == 0:
                            pe.wait_ge(s_om, 12)
                            pe.nop().then_inc(s_cu, 1)

            def rotate(m):
                pe.wait_ge(s_qa, m + 1)
                if m == 0:
                    pe.wait_ge(s_rope, 16)
                pe.matmul(bank(m % 8), swap, raw[m % 4], start=True, stop=True).then_inc(s_rm, 1)

            def square_sum(h):
                pe.wait_ge(s_osq, h + 1)
                return pe.matmul(bank(0)[0:H, :], K("one_col")[:, H - 1 - h:2 * H - 1 - h], osq[:, h, :], start=(h == 0), stop=(h == H - 1))

            SB = [[bank(0), bank(1)], [bank(2), bank(3)]]

            def scores(k):
                h, b = k // NT, k % NT
                w = P * (b + 1)
                if k >= 2:
                    pe.wait_ge(s_ex, 2 * (k - 1))
                for c in range(2):
                    pe.matmul(SB[k % 2][c][:, 0:w], q_half[c][:, h, P * b:P * b + P], kaT[:, h, 0:w], start=True, stop=False)
                for c in range(2):
                    ins = pe.matmul(SB[k % 2][c][:, w - P:w], mask16[:, 0:P], mask16[:, P:2 * P], start=False, stop=True)
                ins.then_inc(s_sc, 1)

            def transposes(k):
                b = k % NT
                pe.wait_ge(s_pr, k + 1)
                if k >= 2:
                    pe.wait_ge(s_pta, k - 1)
                for t in range(b + 1):
                    ins = pe.transpose(bank(4 + k % 2)[:, P * t:P * t + P], prob[k % 2][:, P * t:P * t + P], ident)
                ins.then_inc(s_pt, 1)

            def values(k):
                h, b = k // NT, k % NT
                pe.wait_ge(s_pta, k + 1)
                if b == 0 and h >= 2:
                    pe.wait_ge(s_osq, h - 1)
                for t in range(b + 1):
                    ins = pe.matmul(bank(6 + h % 2)[:, P * b:P * b + P], v_att[:, t, P * h:P * h + P], probT[k % 2][:, P * t:P * t + P], start=(t == 0), stop=(t == b))
                if b == NT - 1:
                    ins.then_inc(s_ov_, 1)

            experts_phase(0)
            mixer_c()
            experts_phase(1)
            pe.wait_ge(s_rope, 32)
            for half in range(2):
                ins = pe.matmul(bank67[:, half, :], K("ones", 1), fn_row[:, 512 * half:512 * half + 512], start=True, stop=True)
            ins.then_inc(s_fnb, 1)

        @block.vector
        def _(dve):
            own = Steps(dve, s_dve)

            def chunk_rest(g):
                dve.wait_ge(s_cr, A_CHUNKS + g + 1)
                s = C_SLOTS[g // NC]
                dve.tensor_tensor(cL[g % 4], slot_w(s)[:, g % NC, :], cR[g % 4], ALU.subtract).then_inc(s_cl, 1)

            def norm(n):
                g = cols[("g_mix0", "g_ffn0", "g_mix1", "g_ffn1")[n]]

                def rows_normed():
                    dve.wait_ge(s_rstd, rstd_before(n) + 1)
                    if n % 2 == 1:
                        dve.wait_ge(s_rw, 80 * (n // 2 + 1))
                    for i in range(NT):
                        if n % 2 == 0:
                            ins = dve.tensor_scalar(hn[:, i, :], x_sb[:, i, :], cols["rstd"][:, i:i + 1], None, ALU.mult)
                        else:
                            ins = dve.scalar_tensor_tensor(out=hn[:, i, :], in0=x_sb[:, i, :], scalar=cols["rstd"][:, i:i + 1], in1=g_row, op0=ALU.mult, op1=ALU.mult)
                        ins.then_inc(s_hn, 1)

                if n % 2 == 0:
                    if n == 0:
                        rows_normed()
                    rest = hnL_A if n == 0 else hnL
                    for c in range(NC):
                        dve.wait_ge(s_tra, evac_before(n) + c + 1)
                        dve.scalar_tensor_tensor(out=rest[:, c, :], in0=bank(c % 4), scalar=g[:, c:c + 1], in1=hnR[:, c, :],
                                                 op0=ALU.mult, op1=ALU.subtract).then_inc(s_trv, 1)
                else:
                    for c in range(0, NC, 2):
                        dve.wait_ge(s_tr, 8 * n + c + 1)
                        dve.tensor_scalar(hnT[:, c, :], bank(c % 4), g[:, c:c + 1], None, ALU.mult).then_inc(s_trv, 1)
                    rows_normed()

            dve.memset(ST[0][:, :, :], 0.0).then_inc(s_sv, 1)
            dve.wait_ge(s_cst, 32)
            own.mark(dve.tensor_copy(count16[:, 0:P], K("ones")))
            own.mark(dve.tensor_copy(count16[:, P:2 * P], K("earlier")))
            own.mark(dve.memset(cols["sub_eps"], SUBLN_EPS))
            own.mark(dve.memset(cols["half_decay"], -0.5 * math.exp(-0.5)))
            norm(0)
            dve.wait_ge(s_vec, n_vec)
            own.mark(dve.tensor_scalar(cols["one_minus_mu"], cols["mu"], -1.0, 1.0, ALU.mult, ALU.add))
            own.mark(dve.tensor_scalar(cols["half_w0"], cols["w0"], 0.5, None, ALU.mult))
            own.mark(dve.tensor_scalar(cols["half_a0"], cols["a0"], 0.5, None, ALU.mult))
            own.mark(dve.tensor_tensor(cols["lam"][0:64, 0:1], cols["lq"][0:64, 0:1], cols["lq"][0:64, 1:2], ALU.mult))
            own.mark(dve.tensor_tensor(cols["lam"][0:64, 1:2], cols["lq"][0:64, 2:3], cols["lq"][0:64, 3:4], ALU.mult))
            own.mark(dve.tensor_scalar(cols["subln_s"], cols["subln"], 1.0 - LAMBDA_INIT, None, ALU.mult))
            own.hold()
            dve.wait_ge(s_tr, 8)
            for i in range(3):
                own.mark(dve.memset(upad[i][:, 0:PAD], 0.0))
            for i in range(2):
                own.mark(dve.memset(shift[i][:, 0:1], 0.0))
            own.hold()

            def z(m):
                i = z_index(m)
                dve.wait_ge(s_sh, i + 1)
                col = TILES[m][2]
                dve.scalar_tensor_tensor(out=Z_OUT[m], in0=bank(4 + m % 4), scalar=cols["one_minus_mu"][:, col:col + 1], in1=shift[i % 2][:, 0:T],
                                         op0=ALU.mult, op1=ALU.add).then_inc(s_z, 1)

            for m in range(6):
                z(m)
            dve.wait_ge(s_tanh, 2)
            dve.tensor_scalar(gateT_in[:, :], gateT_in[:, :], 0.5, 0.5, ALU.mult, ALU.add).then_inc(s_g, 1)
            for j in range(NPAIR):
                z(6 + j)
            for j in range(NPAIR):
                dve.wait_ge(s_wdec, j + 1)
                dve.wait_ge(s_sq, j + 1)
                own.mark(dve.tensor_scalar(kkT[:, j, :], kT[:, j, :], cols["k_k"][:, j:j + 1], None, ALU.mult))
                own.next(dve.tensor_scalar(aT[:, j, :], aT[:, j, :], 0.5, 0.5, ALU.mult, ALU.add))
                own.next(dve.tensor_scalar(alT[:, j, :], aT[:, j, :], -1.0, cols["k_a"][:, j:j + 1], ALU.add, ALU.mult))
                own.next(dve.scalar_tensor_tensor(out=kT[:, j, :], in0=alT[:, j, :], scalar=1.0, in1=kT[:, j, :], op0=ALU.add, op1=ALU.mult))
                if j == 0:
                    own.mark(dve.memset(scan_in, 0.0))
                    own.hold()
                own.next(dve.tensor_copy(scan_in[:, 0:T:C], wT[:, j, 0:T:C]))
                own.next(dve.memset(wT[:, j, 0:T:C], 0.0))
                own.next(dve.tensor_tensor_scan(pT[:, j, :], wT[:, j, :], scan_in, 0.0, ALU.mult, ALU.add))
                own.mark(dve.tensor_copy(pc[:, j, :], pT[:, j, C - 1:T:C]))
                own.mark(dve.scalar_tensor_tensor(out=rk_tmp[:, j, :], in0=rT[:, j, :], scalar=cols["r_k"][:, j:j + 1], in1=kT[:, j, :], op0=ALU.mult, op1=ALU.mult))
            own.hold()
            dve.nop().then_inc(s_rkp, 4)
            dve.wait_ge(s_lora, 4)
            own.next(dve.memset(zeros, 0.0))
            dve.nop().then_inc(s_zero, 1)
            dve.wait_ge(s_hroot, 1)
            own.next(dve.tensor_scalar(hs, hs, 1e-12, None, ALU.max))
            own.next(dve.reciprocal(hs, hs))
            dve.nop().then_inc(s_hinv, 1)
            for j in range(NPAIR):
                own.mark(dve.reciprocal(piT[:, j, :], pT[:, j, :]))
            own.hold()

            def prepare(j):
                dve.wait_ge(s_hb, j + 1)
                own.next(dve.tensor_tensor(kkT[:, j, :], kkT[:, j, :], bank(j), ALU.mult))
                dve.nop().then_inc(s_kk, 1)
                c3 = lambda ap: ap.rearrange("p (c t) -> p c t", c=NCH)
                own.mark(dve.tensor_tensor(c3(alT[:, j, :])[:, :, 1:C], c3(kkT[:, j, :])[:, :, 1:C], c3(pT[:, j, :])[:, :, 0:C - 1], ALU.mult))
                own.mark(dve.tensor_copy(alT[:, j, 0:T:C], kkT[:, j, 0:T:C]))
                own.mark(dve.tensor_tensor(kT[:, j, :], kT[:, j, :], piT[:, j, :], ALU.mult))
                own.next(dve.tensor_tensor(aT[:, j, :], aT[:, j, :], kkT[:, j, :], ALU.mult))
                own.next(dve.tensor_tensor(aT[:, j, :], aT[:, j, :], piT[:, j, :], ALU.mult))
                dve.nop().then_inc(s_prep, 1)

            def pool_diff(g):
                dve.wait_ge(s_win, g + 1)
                dve.scalar_tensor_tensor(out=ybT[:, g, :], in0=upad[1 + g % 2][:, PAD:PAD + T], scalar=1.0 / WINDOWS[g], in1=upad[0][:, PAD:PAD + T],
                                         op0=ALU.mult, op1=ALU.subtract).then_inc(s_pd, 1)

            prepare(0)
            pool_diff(0)
            prepare(1)
            pool_diff(1)
            prepare(2)
            prepare(3)
            pool_diff(2)
            for m in range(14, 18):
                z(m)
            pool_diff(3)
            dve.wait_ge(s_z, 14)
            for j in range(NPAIR):
                dve.wait_ge(s_hb, 5 + j)
                dve.tensor_tensor(bonT[:, j, :], bank(j), vT[:, j, :], ALU.mult).then_inc(s_bon, 1)
            for g in range(0, 16, 2):
                dve.wait_ge(s_tt, g + 1)
                dve.tensor_copy((v_tok, al_tok, k_tok, b_tok)[g % 4][:, g // 4, :], bank(g % 8)).then_inc(s_tev, 1)

            def masked(o_, src, m):
                return dve.tensor_tensor(heads(o_), heads(src), per_head(K(m)), ALU.mult)

            def plus_eye(o_):
                return dve.tensor_tensor(heads(o_), heads(o_), per_head(K("eye64")), ALU.add)

            def grams(q):
                w, kp = wk[q % 2], keep[q]

                def finish(k):
                    dve.nop().then_inc(s_gv, 1)


                def b_(k):
                    bk, o_ = gram_place(q, k)
                    return bk[:, :, o_:o_ + 256]

                dve.wait_ge(s_gm, 5 * q + 2)
                own.next(masked(w["LT"], b_(0), "strict"))
                own.next(masked(w["TT"], w["LT"], "up1"))
                own.next(plus_eye(w["TT"]))
                finish(0)
                own.next(masked(w["Tm"], b_(1), "low1"))
                own.next(plus_eye(w["Tm"]))
                finish(1)
                for k, name, m in ((2, "AK", "strict"), (3, "RK", "upto"), (4, "RB", "upto")):
                    dve.wait_ge(s_gm, 5 * q + (4 if k < 4 else 5))
                    masked(w[name] if name == "AK" else kp[name], b_(k), m).then_inc(s_gv, 1)

            def local(pr):
                grams(2 * pr)
                grams(2 * pr + 1)
                dve.wait_ge(s_gv, 10 * pr + 10)
                for lv in range(NL):
                    for b in range(2):
                        w = wk[b]
                        dve.wait_ge(s_jt, 2 * NL * pr + 2 * lv + b + 1)
                        if lv < NL - 2:
                            own.mark(dve.tensor_tensor(w["Tm"], w["Tm"], bank(2 + b), ALU.subtract))
                        elif lv == NL - 2:
                            for s in range(2):
                                left = lambda ap: ap.rearrange("p (g n) -> p g n", n=C)[C * s:C * s + C // 2, :, 0:C // 2]
                                own.mark(dve.tensor_tensor(left(w["Tm"]), left(w["Tm"]), left(bank(2 + b)), ALU.subtract))
                        if lv < NL - 1:
                            own.mark(dve.tensor_tensor(w["TT"], w["TT"], bank(4 + b), ALU.subtract))
                        else:
                            for s in range(2):
                                upper = lambda ap: ap.rearrange("p (g n) -> p g n", n=C)[C * s:C * s + C // 2, :, C // 2:C]
                                own.mark(dve.tensor_tensor(upper(w["TT"]), upper(w["TT"]), upper(bank(4 + b)), ALU.subtract))
                        own.hold()
                        dve.nop().then_inc(s_jtv, 1)
                for b in range(2):
                    q = 2 * pr + b
                    dve.wait_ge(s_lu, q + 1)
                    dve.tensor_scalar(keep[q]["UV"], bank(4 + b), -1.0, None, ALU.mult).then_inc(s_luv, 1)
                dve.wait_ge(s_luv, 2 * pr + 2)

            def sequence(c):
                q, s = c // 2, c % 2
                r = slice(C * s, C * s + C)
                dve.wait_ge(s_um, c + 1)
                if c >= 2:
                    dve.wait_ge(s_ym, c - 1)
                dve.scalar_tensor_tensor(out=both(u_neg[r, :]), in0=bank_pair[3][r, :, 0:256], scalar=-1.0, in1=both(keep[q]["UV"][r, :]), op0=ALU.mult, op1=ALU.add).then_inc(s_ua, 1)
                dve.wait_ge(s_sm, c + 1)
                if c >= 1:
                    dve.wait_ge(s_ym, c)
                own.next(dve.tensor_tensor(STs[:, :, :], ST[c % 2][:, :, :], bank(5)[:, 0:256].rearrange("p (j i) -> p j i", j=NPAIR), ALU.add))
                dve.tensor_tensor(ST[(c + 1) % 2][:, :, :], STs[:, :, :], pc[:, :, c:c + 1].to_broadcast([P, NPAIR, N]), ALU.mult).then_inc(s_sv, 1)
                dve.wait_ge(s_sv, c + 2)

            local(0)
            sequence(0)
            sequence(1)
            local(1)
            for c in range(2, NCH):
                sequence(c)
            for j in range(NPAIR):
                dve.wait_ge(s_gn, j + 1)
                dve.tensor_tensor(yT[:, j, :], yT[:, j, :], bank(j), ALU.subtract).then_inc(s_gnv, 1)
            dve.wait_ge(s_gn, 5)
            own.next(dve.tensor_scalar(hs, bank(0)[0:H, :], 1.0 / N, GN_EPS, ALU.mult, ALU.add))
            dve.nop().then_inc(s_gnv, 1)
            dve.wait_ge(s_gna, 5)
            own.next(dve.reciprocal(hs, hs))
            dve.nop().then_inc(s_gnv, 1)

            def y_rest(j):
                dve.wait_ge(s_yr, 5 + j)
                dve.tensor_tensor(yL[:, j, :], yT[:, j, :], yR[:, j, :], ALU.subtract).then_inc(s_yl, 1)

            for j in range(NPAIR):
                dve.wait_ge(s_gn, 6 + j)
                y = yT[:, j, :]
                own.next(dve.scalar_tensor_tensor(out=y, in0=y, scalar=cols["ln_w"][:, j:j + 1], in1=bank(j), op0=ALU.mult, op1=ALU.mult))
                own.next(dve.scalar_tensor_tensor(out=y, in0=y, scalar=cols["ln_b"][:, j:j + 1], in1=bonT[:, j, :], op0=ALU.add, op1=ALU.add))
                if j == 0:
                    dve.wait_ge(s_gmv, 4)
                dve.tensor_tensor(y, y, gate[:, j, :], ALU.mult).then_inc(s_yav, 1)
                if j >= 1:
                    y_rest(j - 1)
            y_rest(NPAIR - 1)

            def residual(n):
                for o8 in range(8):
                    half, i = o8 // 4, o8 % 4
                    dve.wait_ge(s_om, 8 * n + o8 + 1)
                    xs = x_sb[:, i, 512 * half:512 * half + 512]
                    b = 4 * (half if n == 1 else 1 - half) + i
                    dve.tensor_tensor(xs, xs, bank(b), ALU.add).then_inc(s_res, 1)
                dve.wait_ge(s_res, 8 * n + 8)

            residual(0)

            def router(l):
                at_ = [rt0]

                def tmp(*shape):
                    n = int(np.prod(shape))
                    v = S2[:, at_[0]:at_[0] + n]
                    at_[0] += n
                    return v.rearrange("p (a b) -> p a b", a=shape[0]) if len(shape) == 2 else v

                n4 = lambda name, k: K(name).unsqueeze(1).to_broadcast([P, NT, k])
                over = lambda ap, k: ap.unsqueeze(2).to_broadcast([P, NT, k])
                lg, gm, gd = tmp(NT, 36), tmp(4), tmp(NT, 4)
                gl, el = lg[:, :, 0:4], lg[:, :, 4:36]
                cand, cmin, og = tmp(NT, 4), tmp(4), tmp(NT, 4)
                gsum, gw = tmp(4), tmp(4)
                em, cd = tmp(NT, 32), tmp(NT, 32)
                oh_at = at_[0]
                oh1, oh2 = tmp(NT, 32), tmp(NT, 32)
                m1, m2, cm, e2, den = tmp(4), tmp(4), tmp(4), tmp(4), tmp(4)
                rank, sl, ex, rv = tmp(NT, 32), tmp(NT, 32), tmp(NT, 32), tmp(2 * NT, 32)
                cnt, nov, incl, bo = tmp(32), tmp(32), tmp(32), tmp(32)
                sf = tmp(2 * NT)
                assert at_[0] <= rt0 + 2 * D
                both_oh = S2[:, oh_at:oh_at + 2 * NT * EXPERTS].rearrange("p (k n) -> p k n", k=2)
                edges = S2[:, tab_at:tab_at + EXPERTS * MORE].rearrange("p (e k) -> p e k", e=EXPERTS)
                tab = S2[:, tab_at:tab_at + EXTRA * 32].rearrange("p (b e) -> p b e", b=EXTRA)
                tabf = S2[:, tab_at + EXTRA * 32:tab_at + EXTRA * 32 + 1 + EXTRA]
                dve.wait_ge(s_lg, 2 * l + 2)
                for i in range(NT):
                    own.mark(dve.scalar_tensor_tensor(out=lg[:, i, :], in0=bank(5)[:, 256 + 36 * i:256 + 36 * i + 36], scalar=cols["rstd"][:, i:i + 1], in1=b_row,
                                                      op0=ALU.mult, op1=ALU.add))
                own.hold()
                own.next(dve.tensor_reduce(gm, gl, AX, ALU.max))
                own.next(dve.tensor_tensor(gd, gl, over(gm, 4), ALU.subtract))
                dve.nop().then_inc(s_rt, 1)
                own.next(dve.tensor_tensor(cand, gl, over(gm, 4), ALU.is_ge))
                own.next(dve.scalar_tensor_tensor(out=cand, in0=cand, scalar=-100.0, in1=n4("iota4", 4), op0=ALU.mult, op1=ALU.add))
                own.next(dve.tensor_reduce(cmin, cand, AX, ALU.min))
                own.next(dve.tensor_tensor(og, cand, over(cmin, 4), ALU.is_equal))
                own.next(dve.tensor_scalar(cand, og, BIG, -BIG, ALU.mult, ALU.add))
                g16 = lambda ap: ap.unsqueeze(3).to_broadcast([P, NT, GROUPS, PER_GROUP])
                e16 = lambda ap: ap.rearrange("p i (g e) -> p i g e", g=GROUPS)
                own.next(dve.tensor_tensor(e16(em), e16(el), g16(og), ALU.mult))
                own.next(dve.tensor_tensor(e16(em), e16(em), g16(cand), ALU.add))

                def first_largest(v, m, oh):
                    own.next(dve.tensor_reduce(m, v, AX, ALU.max))
                    own.next(dve.tensor_tensor(cd, v, over(m, 32), ALU.is_ge))
                    own.next(dve.scalar_tensor_tensor(out=cd, in0=cd, scalar=-100.0, in1=n4("iota32", 32), op0=ALU.mult, op1=ALU.add))
                    own.next(dve.tensor_reduce(cm, cd, AX, ALU.min))
                    own.next(dve.tensor_tensor(oh, cd, over(cm, 32), ALU.is_equal))

                first_largest(em, m1, oh1)
                own.next(dve.scalar_tensor_tensor(out=em, in0=oh1, scalar=-2 * BIG, in1=em, op0=ALU.mult, op1=ALU.add))
                first_largest(em, m2, oh2)
                own.next(dve.tensor_tensor(hot16[:, :, :], oh1, oh2, ALU.add))
                dve.nop().then_inc(s_oh, 1)
                own.next(dve.tensor_tensor(e2, m2, m1, ALU.subtract))
                dve.nop().then_inc(s_rt, 1)
                dve.wait_ge(s_rk, l + 1)
                own.mark(dve.tensor_copy(rank, bank(4)[:, 0:128].rearrange("p (i e) -> p i e", i=NT)))
                own.next(dve.tensor_copy(cnt, bank(4)[:, 128:160]))
                own.next(dve.tensor_tensor(edges, cnt.unsqueeze(2).to_broadcast([P, EXPERTS, MORE]), K("block_edges").unsqueeze(1).to_broadcast([P, EXPERTS, MORE]), ALU.is_gt))
                own.next(dve.tensor_reduce(nov, edges, AX, ALU.add))
                own.next(dve.tensor_tensor_scan(incl, K("ones")[:, 0:32], nov, 0.0, ALU.mult, ALU.add))
                own.next(dve.tensor_tensor(bo, incl, nov, ALU.subtract))
                own.next(dve.tensor_scalar(bo, bo, float(TB), float(MAIN_SLOTS - TB), ALU.mult, ALU.add))
                own.next(dve.tensor_tensor(bo, bo, K("first_slot"), ALU.subtract))
                own.next(dve.tensor_scalar(ex, rank, float(TB), None, ALU.is_ge))
                own.next(dve.tensor_tensor(ex, ex, bo.unsqueeze(1).to_broadcast([P, NT, 32]), ALU.mult))
                own.next(dve.tensor_tensor(sl, rank, n4("first_slot", 32), ALU.add))
                own.next(dve.tensor_tensor(sl, sl, ex, ALU.add))
                own.next(dve.tensor_tensor(rv.rearrange("p (k i) e -> p k (i e)", k=2), sl.rearrange("p i e -> p (i e)").unsqueeze(1).to_broadcast([P, 2, NT * EXPERTS]), both_oh, ALU.mult))
                own.next(dve.tensor_reduce(sf, rv, AX, ALU.add))
                if l > 0:
                    dve.wait_ge(s_comb, NT * l)
                own.next(dve.tensor_copy(slot_ix.rearrange("p k i -> p (k i)"), sf))
                dve.nop().then_inc(s_slot, 2)
                own.next(dve.tensor_tensor(tab, incl.unsqueeze(1).to_broadcast([P, EXTRA, 32]), K("iota_extra").unsqueeze(2).to_broadcast([P, EXTRA, 32]), ALU.is_le))
                own.next(dve.tensor_reduce(tabf[:, 1:1 + EXTRA], tab, AX, ALU.add))
                own.next(dve.tensor_scalar(tabf[:, 1:1 + EXTRA], tabf[:, 1:1 + EXTRA], float(EXPERTS - 1), None, ALU.min))
                own.next(dve.tensor_copy(tabf[:, 0:1], incl[:, 31:32]))
                own.next(dve.tensor_copy(extra_tab[0:1, :], tabf[0:1, :]))
                dve.nop().then_inc(s_slot, 2)
                dve.wait_ge(s_re, 2 * l + 1)
                own.next(dve.tensor_reduce(gsum, gd, AX, ALU.add))
                own.next(dve.reciprocal(gw, gsum))
                dve.wait_ge(s_re, 2 * l + 2)
                own.next(dve.tensor_scalar(den, e2, 1.0, None, ALU.add))
                own.next(dve.reciprocal(den, den))
                own.next(dve.tensor_tensor(wts[:, 0, :], gw, den, ALU.mult))
                own.next(dve.tensor_tensor(wts[:, 1, :], wts[:, 0, :], e2, ALU.mult))

            def block_rest(par):
                return dve.tensor_tensor(xL[par].rearrange("p (a c) t -> p a c t", a=2), bank67[:, :, 0:4 * TB].rearrange("p a (c t) -> p a c t", c=4),
                                         xR[par].rearrange("p (a c) t -> p a c t", a=2), ALU.subtract)

            def hidden_rest(par):
                return dve.tensor_tensor(hL[par], bank(2)[:, 0:4 * TB].rearrange("p (c t) -> p c t", c=4), hR[par], ALU.subtract)

            def hidden1(par):
                return dve.scalar_tensor_tensor(out=th[par], in0=th[par], scalar=1.0, in1=bank(0)[0:TB, :], op0=ALU.add, op1=ALU.mult)

            def hidden2(par):
                return dve.scalar_tensor_tensor(out=hid[par], in0=th[par], scalar=0.5, in1=bank(1)[0:TB, :], op0=ALU.mult, op1=ALU.mult)

            def out1(par):
                return dve.tensor_copy(yrow[par][:, 512:1024], bank(4)[0:TB, :])

            def experts(l):
                B = EXPERTS * l

                def y1(e, par, n):
                    dve.wait_ge(s_down, B + e)
                    if not (isinstance(n, int) and n == 0 and l == 0):
                        dve.wait_ge(s_yw[par], 16 * (16 * l + n))
                    out1(par).then_inc(s_y1, 1)

                Q = BATCHES * l

                def weights_rest(q, slot_):
                    for j in range(3):
                        dve.wait_ge(s_wr, 4 * (Q + q) + j + 1)
                        dve.tensor_tensor(wL[j], slot(slot_)[:, GROUP * j:GROUP * j + GROUP], wR[j], ALU.subtract).then_inc(s_wl, 1)

                def xrest(e, par):
                    dve.wait_ge(s_xr, B + e + 1)
                    block_rest(par).then_inc(s_xl, 1)

                def hrest(e, par):
                    dve.wait_ge(s_hr, B + e + 1)
                    hidden_rest(par).then_inc(s_hl, 1)

                def step(e, par, n, first=False, last=False):
                    if not (first or (isinstance(e, int) and e == 1)):
                        y1(e - 1, par, n - 1)
                    weights_rest(q_up(e), 3 * par + 1)
                    if not first:
                        hrest(e - 1, 1 - par)
                    dve.wait_ge(s_th, B + e + 1)
                    hidden1(par).then_inc(s_h1, 1)
                    if not first:
                        weights_rest(q_down(e - 1), 3 * (1 - par) + 2)
                    if not last:
                        xrest(e + 1, 1 - par)
                    dve.wait_ge(s_up, B + e + 1)
                    dve.wait_ge(s_h1, B + e + 1)
                    if not (first or (isinstance(e, int) and e == 1)):
                        dve.wait_ge(s_ht, B + e - 1)
                    hidden2(par).then_inc(s_h, 1)
                    if not last:
                        weights_rest(q_gate(e + 1), 3 * (1 - par))

                weights_rest(0, 0)
                xrest(0, 0)
                step(0, 0, 0, first=True)
                step(1, 1, 0)
                step(2, 0, 1)
                with dve.Fori(1, EXPERTS // 2 - 1) as i:
                    step(2 * i + 1, 1, i)
                    step(2 * i + 2, 0, i + 1)
                step(EXPERTS - 1, 1, EXPERTS // 2 - 1, last=True)
                y1(EXPERTS - 1, 0, EXPERTS // 2 - 1)
                hrest(EXPERTS - 1, 1)
                weights_rest(q_down(EXPERTS - 1), 5)
                y1(EXPERTS, 1, EXPERTS // 2 - 1)
                v = s_ov[l]
                dve.wait_ge(s_y1, B + EXPERTS)
                dve.wait_ge(s_yw[0], 16 * 16 * (l + 1))
                n = dve.value_load(extra_tab[0:1, 0:1], min_val=0, max_val=EXTRA)
                with dve.If(n > 0):
                    with dve.Fori(0, n) as b:
                        wait_extra(dve, l, "xr", b)
                        block_rest(0).then_inc(v["dve"], 1)
                        wait_extra(dve, l, "th", b)
                        hidden1(0).then_inc(v["dve"], 1)
                        wait_extra(dve, l, "h1", b)
                        hidden2(0).then_inc(v["dve"], 1)
                        wait_extra(dve, l, "hr", b)
                        hidden_rest(0).then_inc(v["dve"], 1)
                        wait_extra(dve, l, "down", b)
                        out1(0).then_inc(v["dve"], 1)
                        dve.wait_ge(v["written"], 16 * b + 16)

            def combine(l, rows_done):
                for i in range(NT):
                    dve.wait_ge(s_got[i], 32 * (l + 1))
                    for k in range(2):
                        ins = dve.scalar_tensor_tensor(out=x_sb[:, i, :], in0=got[k][i], scalar=wts[:, k, i:i + 1], in1=x_sb[:, i, :], op0=ALU.mult, op1=ALU.add)
                        if k == 0:
                            own.next(ins)
                    ins.then_inc(s_comb, 1)
                    if i >= 1:
                        rows_done(i - 1)
                rows_done(NT - 1)

            def normed_row_c(i):
                dve.wait_ge(s_rstd, rstd_before(2) + i + 1)
                dve.tensor_scalar(hn[:, i, :], x_sb[:, i, :], cols["rstd"][:, i:i + 1], None, ALU.mult).then_inc(s_hn, 1)

            def final_row(i):
                dve.wait_ge(s_rstd, rstd_before(4) + i + 1)
                if i == 0:
                    dve.wait_ge(s_fnb, 1)
                dve.scalar_tensor_tensor(out=fin[i], in0=x_sb[:, i, :], scalar=cols["rstd"][:, i:i + 1], in1=bank67.rearrange("p a b -> p (a b)"),
                                         op0=ALU.mult, op1=ALU.mult).then_inc(s_fin, 1)

            def mixer_c():
                dve.wait_ge(s_rope, 16)
                own.mark(dve.tensor_copy(mask16[:, 0:P], ident))
                own.next(dve.tensor_copy(mask16[:, P:2 * P], mask))

                def rope(m):
                    w, r = raw[m % 4], rot[m % 4]
                    dve.wait_ge(s_qa, m + 1)
                    dve.wait_ge(s_rm, m + 1)
                    own.mark(dve.tensor_tensor(w, w, cosT, ALU.mult))
                    own.next(dve.tensor_tensor(r, bank(m % 8), sinT, ALU.mult))
                    if m < 8:
                        own.mark(dve.tensor_tensor(q_half[0][0:64, m, :], w[0:64], r[0:64], ALU.add))
                        dve.tensor_tensor(q_half[1][64:128, m, :], w[64:128], r[64:128], ALU.add).then_inc(s_qv, 1)
                    else:
                        dve.tensor_tensor(kaT[:, m - 8, :], w, r, ALU.add).then_inc(s_qv, 1)

                for g in range(4, 48):
                    chunk_rest(g)
                    u, c = g // NC, g % NC
                    if g == 7:
                        own.mark(dve.memset(q_half[0][64:128], 0.0))
                    if g == 9:
                        own.mark(dve.memset(q_half[1][0:64], 0.0))
                    if 1 <= u <= 4 and c >= 4:
                        rope(4 * (u - 1) + c - 4)
                for g in range(48, 52):
                    chunk_rest(g)
                dve.wait_ge(s_qv, 16)
                dve.wait_ge(s_lam, 1)
                own.next(dve.tensor_tensor(cols["lam"][:, 4:5], cols["lam"][:, 3:4], cols["lam"][:, 2:3], ALU.subtract))
                own.next(dve.tensor_scalar(cols["lam"][:, 4:5], cols["lam"][:, 4:5], -LAMBDA_INIT, None, ALU.add))

                def maxima(k):
                    w = P * (k % NT + 1)
                    st = stat[:, k % 2, :]
                    dve.wait_ge(s_sc, k + 1)
                    if k >= 2:
                        dve.wait_ge(s_pr, k - 1)
                    dve.tensor_reduce(st[:, 2:4], bank_pair[k % 2][:, :, 0:w], AX, ALU.max, negate=True).then_inc(s_mx, 1)

                def probabilities(k):
                    w = P * (k % NT + 1)
                    st, p = stat[:, k % 2, :], pe_[k % 2]
                    dve.wait_ge(s_ex, 2 * k + 2)
                    own.next(dve.reciprocal(st[:, 6:8], st[:, 4:6]))
                    own.next(dve.tensor_tensor(st[:, 7:8], st[:, 7:8], cols["lam"][:, 4:5], ALU.mult))
                    if k >= 2:
                        dve.wait_ge(s_pt, k - 1)
                    own.next(dve.tensor_scalar(prob[k % 2][:, 0:w], p[:, 0, 0:w], st[:, 6:7], None, ALU.mult))
                    dve.scalar_tensor_tensor(out=prob[k % 2][:, 0:w], in0=p[:, 1, 0:w], scalar=st[:, 7:8], in1=prob[k % 2][:, 0:w], op0=ALU.mult, op1=ALU.add).then_inc(s_pr, 1)

                for k in range(H * NT):
                    maxima(k)
                    if k >= 1:
                        probabilities(k - 1)
                probabilities(H * NT - 1)

                def o_rest(h):
                    dve.wait_ge(s_or, h + 1)
                    dve.tensor_tensor(oL[:, h, :], oT[:, h, :], oR[:, h, :], ALU.subtract).then_inc(s_ol, 1)

                dve.wait_ge(s_ort, 1)
                dve.reciprocal(o_inv, o_inv).then_inc(s_oi, 1)
                for h in range(H):
                    dve.wait_ge(s_osm, h + 2)
                    dve.scalar_tensor_tensor(out=oT[:, h, :], in0=oT[:, h, :], scalar=cols["subln_s"], in1=bank(4 + h % 4), op0=ALU.mult, op1=ALU.mult).then_inc(s_on, 1)
                    if h >= 1:
                        o_rest(h - 1)
                o_rest(H - 1)
                for g in range(52, 64):
                    chunk_rest(g)
                residual(1)

            norm(1)
            router(0)
            experts(0)
            for g in range(4):
                chunk_rest(g)
            combine(0, normed_row_c)
            norm(2)
            mixer_c()
            norm(3)
            router(1)
            experts(1)
            combine(1, final_row)

        @block.scalar
        def _(act):
            def router_weights(l):
                act.dma_start(b_row[:, 0:4], a["moe_b_group"][l:l + 1, :].to_broadcast([P, 4]), allow_slow_non_contiguous=True).then_inc(s_rw, 16)
                act.dma_start(b_row[:, 4:36], a["moe_b_expert"][l:l + 1, :].to_broadcast([P, 32]), allow_slow_non_contiguous=True).then_inc(s_rw, 16)
                act.dma_start(g_row, a["norm_ffn"][l:l + 1, :].to_broadcast([P, D])).then_inc(s_rw, 16)
                act.dma_start(w_router[:, :, 0:4], a["moe_w_group"][l].rearrange("(p c) n -> p c n", c=NC), allow_slow_non_contiguous=True).then_inc(s_rw, 16)
                act.dma_start(w_router[:, :, 4:36], a["moe_w_expert"][l].rearrange("(p c) n -> p c n", c=NC), allow_slow_non_contiguous=True).then_inc(s_rw, 16)

            own = Steps(act, s_act)

            def chunk_rounded(g):
                s = C_SLOTS[g // NC]
                if g % NC == 0:
                    act.wait_ge(s_full[s], 16 * use("C", C_SLOTS, g // NC))
                if g >= 4:
                    act.wait_ge(s_cu, A_CHUNKS + g - 3)
                act.activation(cR[g % 4], slot_w(s)[:, g % NC, :], ACT.Copy).then_inc(s_cr, 1)

            def rounded(lo, hi):
                for g in range(lo, hi):
                    u, c = g // NC, g % NC
                    if c == 0:
                        act.wait_ge(s_full[A_SLOTS[u]], 16 * use("A", A_SLOTS, u))
                    if g >= 4:
                        act.wait_ge(s_cu, g - 3)
                    w = A_SRC[u].shape[2]
                    act.activation(aR[g % 4][:, 0:w], a_weights(g), ACT.Copy).then_inc(s_cr, 1)

            def norm(n):
                def squares():
                    src = {0: (s_x, 16 * NT, 0), 1: (s_res, 4, 1), 2: (s_comb, 0, 1), 3: (s_res, 12, 1), 4: (s_comb, 4, 1)}[n]
                    for i in range(NT):
                        act.wait_ge(src[0], src[1] + src[2] * (i + 1))
                        unused = hn[:, i, :] if n != 1 else slab(4 + i, D)
                        act.activation(unused, x_sb[:, i, :], ACT.Square, accum_out=cols["ss"][:, i:i + 1]).then_inc(s_ss, 1)

                if n == 4:
                    squares()
                    return
                g = cols[("g_mix0", "g_ffn0", "g_mix1", "g_ffn1")[n]]
                if n % 2 == 0:
                    if n == 2:
                        for chunk in range(4):
                            chunk_rounded(chunk)
                    squares()
                    if n == 0:
                        rounded(0, 4)
                        act.wait_ge(s_cst, 32)
                    for c in range(NC):
                        act.wait_ge(s_tr, 8 * n + c + 1)
                        act.activation(hnR[:, c, :], bank(c % 4), ACT.Copy, scale=g[:, c:c + 1]).then_inc(s_tra, 1)
                else:
                    for c in range(1, NC, 2):
                        act.wait_ge(s_tr, 8 * n + c + 1)
                        act.activation(hnT[:, c, :], bank(c % 4), ACT.Copy, scale=g[:, c:c + 1]).then_inc(s_tra, 1)
                    squares()
                    act.wait_ge(s_lg, 2 * (n // 2) + 1)
                    act.wait_ge(s_ss, 4 * n + 4)
                    act.activation(lgT, bank(4)[0:36, :], ACT.Copy).then_inc(s_lgc, 1)

            norm(0)

            def shifted(m):
                i = z_index(m)
                act.wait_ge(s_proj, m + 1)
                if i >= 2:
                    act.wait_ge(s_z, i - 1)
                if m == 0:
                    act.wait_ge(s_trv, 8)
                    act.wait_ge(s_dve, n_setup)
                col = TILES[m][2]
                act.activation(shift[i % 2][:, 1:T + 1], bank(4 + m % 4), ACT.Copy, scale=cols["mu"][:, col:col + 1]).then_inc(s_sh, 1)

            rounded(4, 12)
            shifted(0)
            shifted(1)
            act.wait_ge(s_z, 1)
            act.activation(z_l0[0:64, :], z_l0[0:64, :], ACT.Tanh).then_inc(s_tanh, 1)
            act.wait_ge(s_z, 2)
            act.activation(gateT_in[:, :], gateT_in[:, :], ACT.Tanh, scale=0.5).then_inc(s_tanh, 1)
            rounded(12, 20)
            for m in range(2, 6):
                shifted(m)
            for j in range(NPAIR):
                act.wait_ge(s_lora, j + 1)
                b = 2 * (j % 2)
                act.activation(wT[:, j, :], bank(b), ACT.Tanh, scale=0.5, bias=cols["half_w0"][:, j:j + 1]).then_inc(s_act, 1)
                act.activation(aT[:, j, :], bank(b + 1), ACT.Tanh, scale=0.5, bias=cols["half_a0"][:, j:j + 1]).then_inc(s_am, 1)
                act.wait_ge(s_am, j + 1)
                act.activation(wT[:, j, :], wT[:, j, :], ACT.Exp, scale=-0.5 * math.exp(-0.5), bias=cols["half_decay"]).then_inc(s_wdec, 1)
            rounded(20, 28)
            for j in range(NPAIR):
                shifted(6 + j)
                if j >= 2:
                    act.wait_ge(s_hsum, j - 1)
                act.activation(sq_tmp[j % 2], kT[:, j, :], ACT.Square, scale=cols["k_k"][:, j:j + 1]).then_inc(s_sq, 1)
            act.wait_ge(s_hsum, 4)
            act.activation(hs, bank(0)[0:H, :], ACT.Sqrt).then_inc(s_hroot, 1)
            rounded(28, 36)
            for g in range(4):
                act.wait_ge(s_proj, 11 + g)
                act.activation(ybT[:, g, :], bank(4 + (10 + g) % 4), ACT.Copy).then_inc(s_u, 1)

            def padded(g):
                act.wait_ge(s_u, g + 4 if g else 4)
                if g >= 1:
                    act.wait_ge(s_pd, g)
                act.activation(upad[0][:, PAD:PAD + T], ybT[:, g, :], ACT.Copy).then_inc(s_u, 1)

            padded(0)
            rounded(36, 38)
            padded(1)
            rounded(38, 40)
            padded(2)
            shifted(14)
            shifted(15)
            padded(3)
            shifted(16)
            shifted(17)
            act.wait_ge(s_hsum, 5)
            act.activation(hs, bank(0)[0:H, :], ACT.Copy).then_inc(s_rs, 1)
            rounded(40, 44)
            for g in range(4):
                act.wait_ge(s_pmm, g + 1)
                act.activation(ybT[:, g, :], bank(4 + (18 + g) % 4), ACT.Copy, scale=cols["pool_scale"][:, g:g + 1]).then_inc(s_yb, 1)
            for g in range(1, 16, 2):
                act.wait_ge(s_tt, g + 1)
                act.activation((v_tok, al_tok, k_tok, b_tok)[g % 4][:, g // 4, :], bank(g % 8), ACT.Copy).then_inc(s_tea, 1)

            def local(pr):
                for lv in range(NL):
                    for b in range(2):
                        n = 2 * NL * pr + 2 * lv + b
                        act.wait_ge(s_jx, n + 1)
                        if lv >= 1:
                            act.wait_ge(s_jt, n - 1)
                        act.activation(wk[b]["X"], bank(b), ACT.Copy).then_inc(s_jxa, 1)
                for b in range(2):
                    q = 2 * pr + b
                    act.wait_ge(s_lx, q + 1)
                    act.wait_ge(s_jxa, 2 * NL * pr + 2 * NL)
                    act.activation(wk[b]["X"], bank(b), ACT.Copy).then_inc(s_lxa, 1)
                    act.wait_ge(s_lw, q + 1)
                    act.activation(both(keep[q]["WT"]), bank_pair[1 + 2 * b][:, :, 0:256], ACT.Copy).then_inc(s_lwa, 1)

            def sequence(c):
                q, s = c // 2, c % 2
                act.wait_ge(s_ym, c + 1)
                act.activation(yT[:, :, C * c:C * c + C], bank(s)[:, 0:256].rearrange("p (j t) -> p j t", j=NPAIR), ACT.Copy).then_inc(s_ya, 1)

            local(0)
            sequence(0)
            sequence(1)
            local(1)
            for j in range(NPAIR):
                act.wait_ge(s_gmm, j + 1)
                if j == 0:
                    act.wait_ge(s_lu, 4)
                act.activation(gate[:, j, :], bank(2 + j % 2), ACT.Copy).then_inc(s_gmv, 1)
            for g in range(4):
                act.activation(yR[:, 4 + g, :], ybT[:, g, :], ACT.Copy).then_inc(s_yr, 1)
            for c in range(2, NCH):
                sequence(c)
            for j in range(NPAIR):
                act.wait_ge(s_gnv, j + 1)
                act.activation(yc_sq[:, T * j:T * j + T], yT[:, j, :], ACT.Square).then_inc(s_gna, 1)
            act.wait_ge(s_gnv, 5)
            act.activation(hs, hs, ACT.Sqrt).then_inc(s_gna, 1)
            for j in range(NPAIR):
                act.wait_ge(s_yav, j + 1)
                act.activation(yR[:, j, :], yT[:, j, :], ACT.Copy).then_inc(s_yr, 1)
                rounded(*((44, 46), (46, 47), (47, 48), (48, A_CHUNKS))[j])
            router_weights(0)

            def tanh_half(par):
                return act.activation(th[par], bank(0)[0:TB, :], ACT.Tanh, scale=0.5)

            def block_copy(par):
                return act.activation(xR[par].rearrange("p (a c) t -> p a c t", a=2), bank67[:, :, 0:4 * TB].rearrange("p a (c t) -> p a c t", c=4), ACT.Copy)

            def hidden_copy(par):
                return act.activation(hR[par], bank(2)[:, 0:4 * TB].rearrange("p (c t) -> p c t", c=4), ACT.Copy)

            def out0(par):
                return act.activation(yrow[par][:, 0:512], bank(3)[0:TB, :], ACT.Copy)

            def experts(l):
                B = EXPERTS * l
                act.wait_ge(s_rt, 2 * l + 1)
                gd = S2[:, rt0 + 16 + 128 + 4:rt0 + 16 + 128 + 4 + 16]
                act.activation(gd, gd, ACT.Exp).then_inc(s_re, 1)
                act.wait_ge(s_rt, 2 * l + 2)
                e2 = S2[:, e2_at:e2_at + 4]
                act.activation(e2, e2, ACT.Exp).then_inc(s_re, 1)

                Q = BATCHES * l

                def y0(e, par, n):
                    act.wait_ge(s_down, B + e)
                    if not (isinstance(n, int) and n == 0 and l == 0):
                        act.wait_ge(s_yw[par], 16 * (16 * l + n))
                    out0(par).then_inc(s_y0, 1)

                def xround(e, par):
                    act.wait_ge(s_xt, B + e + 1)
                    block_copy(par).then_inc(s_xr, 1)

                def hround(e, par):
                    act.wait_ge(s_ht, B + e + 1)
                    if not (isinstance(e, int) and e <= 1):
                        act.wait_ge(s_down, B + e - 1)
                    hidden_copy(par).then_inc(s_hr, 1)

                def weights_rounded(q, slot_, n, quarters=range(4)):
                    act.wait_ge(s_full[slot_], 16 * (moe_before(l, slot_) + n + 1))
                    for j in quarters:
                        if not (isinstance(q, int) and q == 0):
                            act.wait_ge(s_wu, 4 * (Q + q - 1) + j + 1)
                        act.activation(wR[j], slot(slot_)[:, GROUP * j:GROUP * j + GROUP], ACT.Copy).then_inc(s_wr, 1)

                def load_rows(e, par):
                    act.dma_start(rows[par], xp[bass.ds(TB * e, TB), :]).then_inc(s_rows[par], 16)

                def store(e, par):
                    act.wait_ge(s_y0, B + e)
                    act.wait_ge(s_y1, B + e)
                    act.dma_start(yp[bass.ds(TB * (e - 1), TB), :], yrow[par]).then_inc(s_yw[par], 16)

                act.wait_ge(s_rk, l + 1)
                weights_rounded(0, 0, 0, (0, 1))
                act.wait_ge(s_disp, 16 * 2 * NT * (l + 1))
                load_rows(0, 0)
                load_rows(1, 1)
                weights_rounded(0, 0, 0, (2, 3))

                def step(e, par, n, first=False, last=False):
                    if not (first or (isinstance(e, int) and e == 1)):
                        y0(e - 1, par, n - 1)
                    weights_rounded(q_up(e), 3 * par + 1, n)
                    if not (first or (isinstance(e, int) and e == 1)):
                        store(e - 1, par)
                    if not first:
                        hround(e - 1, 1 - par)
                    act.wait_ge(s_gate, B + e + 1)
                    if not (isinstance(e, int) and e <= 1):
                        act.wait_ge(s_h, B + e - 1)
                    tanh_half(par).then_inc(s_th, 1)
                    if not last and not (isinstance(e, int) and e == EXPERTS - 2):
                        load_rows(e + 2, par)
                    if not first:
                        weights_rounded(q_down(e - 1), 3 * (1 - par) + 2, n if par == 1 else n - 1)
                    if not last:
                        xround(e + 1, 1 - par)
                        weights_rounded(q_gate(e + 1), 3 * (1 - par), n + 1 if par == 1 else n)

                xround(0, 0)
                step(0, 0, 0, first=True)
                step(1, 1, 0)
                step(2, 0, 1)
                with act.Fori(1, EXPERTS // 2 - 2) as i:
                    step(2 * i + 1, 1, i)
                    step(2 * i + 2, 0, i + 1)
                step(EXPERTS - 3, 1, EXPERTS // 2 - 2)
                step(EXPERTS - 2, 0, EXPERTS // 2 - 1)
                step(EXPERTS - 1, 1, EXPERTS // 2 - 1, last=True)
                y0(EXPERTS - 1, 0, EXPERTS // 2 - 1)
                store(EXPERTS - 1, 0)
                hround(EXPERTS - 1, 1)
                weights_rounded(q_down(EXPERTS - 1), 5, EXPERTS // 2 - 1)
                y0(EXPERTS, 1, EXPERTS // 2 - 1)
                store(EXPERTS, 1)
                v = s_ov[l]
                act.wait_ge(s_down, B + EXPERTS)
                act.wait_ge(s_y0, B + EXPERTS)
                act.wait_ge(s_yw[0], 16 * 16 * (l + 1))
                n = act.value_load(extra_tab[0:1, 0:1], min_val=0, max_val=EXTRA)
                with act.If(n > 0):
                    with act.Fori(0, n) as b:
                        e = act.value_load(extra_tab[0:1, bass.ds(b + 1, 1)], min_val=0, max_val=EXPERTS - 1)
                        act.dma_start(slot_w(3), a["moe_w_gate"][l, bass.ds(e, 1)].rearrange("o (p c) n -> (o p) c n", c=NC)).then_inc(v["w"], 16)
                        act.dma_start(slot_w(4), a["moe_w_up"][l, bass.ds(e, 1)].rearrange("o (p c) n -> (o p) c n", c=NC)).then_inc(v["w"], 16)
                        act.dma_start(slot_w(5, 4), a["moe_w_down"][l, bass.ds(e, 1)].rearrange("o (p c) n -> (o p) c n", c=4)).then_inc(v["w"], 16)
                        act.dma_start(rows[0], xp[bass.ds(TB * b + MAIN_SLOTS, TB), :]).then_inc(v["rows"], 16)
                        wait_extra(act, l, "xt", b)
                        block_copy(0).then_inc(v["act"], 1)
                        wait_extra(act, l, "up", b)
                        tanh_half(0).then_inc(v["act"], 1)
                        wait_extra(act, l, "ht", b)
                        hidden_copy(0).then_inc(v["act"], 1)
                        wait_extra(act, l, "down", b)
                        out0(0).then_inc(v["act"], 1)
                        wait_extra(act, l, "y0", b)
                        wait_extra(act, l, "y1", b)
                        act.dma_start(yp[bass.ds(TB * b + MAIN_SLOTS, TB), :], yrow[0]).then_inc(v["written"], 16)
                        act.wait_ge(v["written"], 16 * b + 16)
                if l == 0:
                    router_weights(1)

            def mixer_c():
                act.wait_ge(s_lamm, 1)
                act.activation(cols["lam"][:, 2:4], bank(7)[:, 0:2], ACT.Exp).then_inc(s_lam, 1)

                def raw_copy(m):
                    act.wait_ge(s_qm, m + 1)
                    if m >= 4:
                        act.wait_ge(s_qv, m - 3)
                    act.activation(raw[m % 4], bank(m % 8), ACT.Copy, scale=(SCALE if m < H else 1.0)).then_inc(s_qa, 1)

                def v_copy(n):
                    half, i = n // NT, n % NT
                    act.wait_ge(s_vm, n + 1)
                    act.activation(v_att[:, i, 512 * half:512 * half + 512], bank(n), ACT.Copy).then_inc(s_va, 1)

                for g in range(4, 48):
                    chunk_rounded(g)
                    u, c = g // NC, g % NC
                    if u >= 1 and 2 <= c < 6:
                        if u < 5:
                            raw_copy(4 * (u - 1) + c - 2)
                        else:
                            v_copy(c - 2)
                for i in range(NT):
                    chunk_rounded(48 + i)
                for i in range(NT):
                    v_copy(NT + i)

                def exps(k):
                    w = P * (k % NT + 1)
                    st = stat[:, k % 2, :]
                    act.wait_ge(s_mx, k + 1)
                    for c in range(2):
                        act.activation(pe_[k % 2][:, c, 0:w], bank(2 * (k % 2) + c)[:, 0:w], ACT.Exp, bias=st[:, 2 + c:3 + c],
                                       accum_out=st[:, 4 + c:5 + c]).then_inc(s_ex, 1)

                def evac(k):
                    w = P * (k % NT + 1)
                    act.wait_ge(s_pt, k + 1)
                    if k >= 2:
                        act.wait_ge(s_pta, k - 1)
                    act.activation(probT[k % 2][:, 0:w], bank(4 + k % 2)[:, 0:w], ACT.Copy).then_inc(s_pta, 1)

                def head_out(h):
                    act.wait_ge(s_ov_, h + 1)
                    act.activation(oT[:, h, :], bank(6 + h % 2), ACT.Copy).then_inc(s_oc, 1)
                    act.activation(osq[:, h, :], bank(6 + h % 2), ACT.Square, scale=128 ** -0.5).then_inc(s_osq, 1)

                for k in range(H * NT + 3):
                    if k < H * NT:
                        exps(k)
                    if 2 <= k < H * NT + 2:
                        evac(k - 2)
                    if k >= 3 and (k - 3) % NT == NT - 1:
                        head_out((k - 3) // NT)
                act.wait_ge(s_osm, 1)
                act.activation(o_inv, bank(0)[0:H, :], ACT.Sqrt, bias=cols["sub_eps"][0:H]).then_inc(s_ort, 1)
                for h in range(H):
                    act.wait_ge(s_on, h + 1)
                    act.activation(oR[:, h, :], oT[:, h, :], ACT.Copy).then_inc(s_or, 1)
                for g in range(52, 64):
                    chunk_rounded(g)

            norm(1)
            experts(0)
            norm(2)
            mixer_c()
            norm(3)
            experts(1)
            norm(4)

        @block.gpsimd
        def _(pool):
            own = Steps(pool, s_pool)

            def rstd(n):
                if n == 0:
                    pool.wait_ge(s_cst, 32)
                if n >= 1 and n < 4:
                    pool.wait_ge(s_hn, 4 * n)
                for part in [slice(i, i + 1) for i in range(NT)] if n in (2, 4) else [slice(0, NT)]:
                    pool.wait_ge(s_ss, 4 * n + part.stop)
                    own.next(pool.tensor_scalar(cols["ms"][:, part], cols["ss"][:, part], 1.0 / D, RMS_EPS, ALU.mult, ALU.add))
                    own.next(pool.tensor_tensor(cols["rstd"][:, part], cols["ms"][:, part], K("minus_half")[:, part], ALU.pow))
                    pool.nop().then_inc(s_rstd, 1)

            rstd(0)
            zr = xp.rearrange("(p r) d -> p (r d)", p=TB)
            ze = yp[MAIN_SLOTS:SLOTS, :].rearrange("(p r) d -> p (r d)", p=TB)
            zero_parts = [zr[:, 2 * D * k:2 * D * k + 2 * D] for k in range(SLOTS // TB // 2)] \
                + [ze[:, 2 * D * k:2 * D * k + 2 * D] for k in range(EXTRA // 2)]

            def weights_rest(lo, hi):
                for g in range(lo, hi):
                    pool.wait_ge(s_cr, g + 1)
                    w = A_SRC[g // NC].shape[2]
                    pool.tensor_tensor(aL[g % 4][:, 0:w], a_weights(g), aR[g % 4][:, 0:w], ALU.subtract).then_inc(s_clp, 1)

            weights_rest(0, 36)
            for g in range(4):
                if g in (1, 2):
                    weights_rest(34 + 2 * g, 36 + 2 * g)
                pool.wait_ge(s_u, 4 + g + 1)
                src = upad[0]
                for k in range(g + 1):
                    dst = upad[1 + k % 2]
                    own.next(pool.tensor_tensor(dst[:, PAD:PAD + T], src[:, PAD:PAD + T], src[:, PAD - 2 ** k:PAD + T - 2 ** k], ALU.add))
                    src = dst
                own.next(pool.tensor_tensor(src[:, PAD:2 * PAD], src[:, PAD:2 * PAD], K("short_window")[:, 16 * g:16 * g + 16], ALU.mult))
                pool.nop().then_inc(s_win, 1)
            pool.wait_ge(s_rkp, 4)
            for j in range(NPAIR):
                own.mark(pool.tensor_tensor(rT[:, j, :], rT[:, j, :], pT[:, j, :], ALU.mult))
            own.hold()
            pool.nop().then_inc(s_prepp, 4)
            weights_rest(40, 44)
            def local(pr):
                for lv, m in enumerate(LEVELS):
                    for b in range(2):
                        q, w, n = 2 * pr + b, wk[b], 2 * NL * pr + 2 * lv + b
                        pool.wait_ge(s_gv, 5 * q + 1)
                        if lv >= 1:
                            pool.wait_ge(s_jx, n - 1)
                        pool.tensor_tensor(heads(w["Bm"]), heads(w["LT"]), per_head(K(f"join{m}")), ALU.mult).then_inc(s_jb, 1)

            local(0)
            pool.wait_ge(s_zero, 1)
            for part in zero_parts:
                pool.dma_start(part.rearrange("p (r n) -> p r n", n=256), zeros[0:TB, :].unsqueeze(1).to_broadcast([TB, 8, 256])).then_inc(s_zrows, 16)
            local(1)
            for g in range(4):
                pool.wait_ge(s_yr, g + 1)
                pool.tensor_tensor(yL[:, 4 + g, :], ybT[:, g, :], yR[:, 4 + g, :], ALU.subtract).then_inc(s_ybl, 1)
            weights_rest(44, A_CHUNKS)

            def experts(l):
                B = 16 * l
                if l == 0:
                    pool.wait_ge(s_zrows, 16 * n_zero)
                pool.wait_ge(s_slot, 4 * l + 2)
                pool.wait_ge(s_hn, 4 * (1 + 2 * l) + 4)
                for k in range(2):
                    for i in range(NT):
                        pool.indirect_dma_start(out=xp, out_offset=bass.IndirectOffsetOnAxis(ap=slot_ix[:, k, i:i + 1], axis=0),
                                                in_=hn[:, i, :], in_offset=None).then_inc(s_disp, 16)
                Q = BATCHES * l

                def weights_rest(q, slot_):
                    pool.wait_ge(s_wr, 4 * (Q + q) + 4)
                    pool.tensor_tensor(wL[3], slot(slot_)[:, 3 * GROUP:UNIT], wR[3], ALU.subtract).then_inc(s_wlp, 1)

                def step(e, par):
                    weights_rest(q_up(e), 3 * par + 1)
                    weights_rest(q_down(e - 1), 3 * (1 - par) + 2)
                    weights_rest(q_gate(e + 1), 3 * (1 - par))

                weights_rest(0, 0)
                weights_rest(1, 1)
                weights_rest(2, 3)
                with pool.Fori(0, EXPERTS // 2 - 1) as i:
                    step(2 * i + 1, 1)
                    step(2 * i + 2, 0)
                weights_rest(q_up(EXPERTS - 1), 4)
                weights_rest(q_down(EXPERTS - 2), 2)
                weights_rest(q_down(EXPERTS - 1), 5)
                for par in range(2):
                    pool.wait_ge(s_yw[par], 16 * 16 * (l + 1))
                pool.wait_ge(s_xt, EXPERTS * (l + 1))
                v = s_ov[l]
                n = pool.value_load(extra_tab[0:1, 0:1], min_val=0, max_val=EXTRA)
                with pool.If(n > 0):
                    with pool.Fori(0, n) as b:
                        pool.wait_ge(v["written"], 16 * b + 16)
                for i in range(NT):
                    for k in range(2):
                        pool.indirect_dma_start(out=got[k][i], out_offset=None, in_=yp,
                                                in_offset=bass.IndirectOffsetOnAxis(ap=slot_ix[:, k, i:i + 1], axis=0)).then_inc(s_got[i], 16)

            rstd(1)
            experts(0)
            rstd(2)
            rstd(3)
            experts(1)
            rstd(4)


_INS = ["x", "norm_mix", "norm_ffn", "final_norm", "a_w_in", "a_mu", "a_w0", "a_w2", "a_a0", "a_a2", "a_g2",
        "a_k_k", "a_k_a", "a_r_k", "a_ln_w", "a_ln_b", "b_w_pool", "b_pool_scale", "ab_w_out",
        "c_w_qkv", "c_lambda_q1", "c_lambda_k1", "c_lambda_q2", "c_lambda_k2", "c_subln", "c_w_out",
        "moe_w_group", "moe_b_group", "moe_w_expert", "moe_b_expert", "moe_w_gate", "moe_w_up", "moe_w_down"]


def kernel(**inputs):
    import numpy as _np
    import concourse.bacc as _bacc
    from concourse import mybir as _mybir
    from concourse.bass_utils import run_bass_kernel_spmd as _run

    nc = _bacc.Bacc("TRN2", target_bir_lowering=False, num_devices=1)
    arrays, args = {}, {}
    for name in _INS:
        arr = _np.ascontiguousarray(inputs[name])
        arrays[f"in_{name}"] = arr
        args[name] = nc.dram_tensor(f"in_{name}", arr.shape, _mybir.dt.from_np(arr.dtype), kind="ExternalInput").ap()
    tables = {"constants": constant_table()[1], "rope": rope_table()}
    aps = {}
    for name, arr in tables.items():
        arrays[name] = arr
        aps[name] = nc.dram_tensor(name, arr.shape, _mybir.dt.from_np(arr.dtype), kind="ExternalInput").ap()
    out = nc.dram_tensor("out", (1, T, D), _mybir.dt.float32, kind="ExternalOutput").ap()
    build(nc, args, aps["constants"], aps["rope"], out)
    r = _run(nc, [arrays], core_ids=[0])
    return r.results[0]["out"]
```
